# Optimizing a Trainium2 kernel written in Bass

```python
import jax, jax.numpy as jnp
from jax import lax
import numpy as np

D_MODEL = 1024
BATCH = 1
SEQ = 512
DEPTH = 2

MLSTM_HEADS = 4
MLSTM_QK_DIM = 64
MLSTM_V_DIM = 128
MLSTM_QK_W = MLSTM_HEADS * MLSTM_QK_DIM
MLSTM_W = MLSTM_HEADS * MLSTM_V_DIM
MLSTM_CHUNK = 128
QK_CONV = 4
FORGET_BIAS = 3.0
ATTN_HEADS = 8
ATTN_KV_HEADS = 2
ATTN_HEAD_DIM = 64
ATTN_W = ATTN_HEADS * ATTN_HEAD_DIM
ATTN_KV_W = ATTN_KV_HEADS * ATTN_HEAD_DIM
WINDOW = 128
ROPE_THETA = 10000.0
MIX_W = MLSTM_W + ATTN_W
SPLITS = (MLSTM_QK_W, MLSTM_QK_W, MLSTM_W, MLSTM_W, 2 * MLSTM_HEADS, ATTN_W, ATTN_KV_W, ATTN_KV_W)
IN_W = sum(SPLITS)
D_FF = 2816
FFN_CONV = 3
EPS = 1e-6


def rmsnorm(x, g):
    xf = x.astype(jnp.float32)
    y = xf * lax.rsqrt(jnp.mean(xf * xf, axis=-1, keepdims=True) + EPS)
    return (y * g.astype(jnp.float32)).astype(x.dtype)

def causal_dwconv(x, w):
    K, C = w.shape
    return lax.conv_general_dilated(
        x, w[:, None, :].astype(x.dtype), window_strides=(1,), padding=[(K - 1, 0)],
        dimension_numbers=('NWC', 'WIO', 'NWC'), feature_group_count=C)

def rope(x):
    S, D = x.shape[1], x.shape[-1]
    inv = 1.0 / (ROPE_THETA ** (jnp.arange(0, D, 2, dtype=jnp.float32) / D))
    ang = jnp.arange(S, dtype=jnp.float32)[:, None] * inv[None, :]
    cos = jnp.cos(ang)[None, :, None, :]
    sin = jnp.sin(ang)[None, :, None, :]
    xf = x.astype(jnp.float32)
    x1, x2 = xf[..., :D // 2], xf[..., D // 2:]
    return jnp.concatenate([x1 * cos - x2 * sin, x2 * cos + x1 * sin], axis=-1)

def mlstm_chunkwise(q, k, v, log_i, log_f):
    B, S, H, DK = q.shape
    DV = v.shape[-1]
    L = MLSTM_CHUNK
    NC = S // L

    def chunks(a):
        a = a.reshape((B, NC, L) + a.shape[2:])
        return jnp.moveaxis(a, (1, 3), (0, 2))

    qc = chunks(q)
    kc = chunks(k * (DK ** -0.5))
    vc = chunks(v)
    lic = chunks(log_i)
    bc = jnp.cumsum(chunks(log_f), axis=-1)
    causal = jnp.tril(jnp.ones((L, L), dtype=bool))

    def step(carry, inp):
        C, n, m = carry
        q_, k_, v_, b_, li_ = inp
        dlog = b_[..., :, None] - b_[..., None, :] + li_[..., None, :]
        dlog = jnp.where(causal, dlog, -jnp.inf)
        inter = b_ + m[..., None]
        m_row = jnp.maximum(inter, jnp.max(dlog, axis=-1))
        w_intra = jnp.exp(dlog - m_row[..., None])
        w_inter = jnp.exp(inter - m_row)
        s = jnp.einsum('bhtd,bhsd->bhts', q_, k_) * w_intra
        num = (w_inter[..., None] * jnp.einsum('bhtd,bhde->bhte', q_, C)
               + jnp.einsum('bhts,bhse->bhte', s, v_))
        den = w_inter * jnp.einsum('bhtd,bhd->bht', q_, n) + jnp.sum(s, axis=-1)
        h = num / jnp.maximum(jnp.abs(den), jnp.exp(-m_row))[..., None]
        b_last = b_[..., -1]
        ls = b_last[..., None] - b_ + li_
        m_new = jnp.maximum(b_last + m, jnp.max(ls, axis=-1))
        decay = jnp.exp(b_last + m - m_new)
        ws = jnp.exp(ls - m_new[..., None])
        C = decay[..., None, None] * C + jnp.einsum('bhs,bhsd,bhse->bhde', ws, k_, v_)
        n = decay[..., None] * n + jnp.einsum('bhs,bhsd->bhd', ws, k_)
        return (C, n, m_new), h

    init = (jnp.zeros((B, H, DK, DV), jnp.float32), jnp.zeros((B, H, DK), jnp.float32),
            jnp.zeros((B, H), jnp.float32))
    _, hs = lax.scan(step, init, (qc, kc, vc, bc, lic))
    return jnp.moveaxis(hs, (0, 2), (1, 3)).reshape(B, S, H, DV)

def sliding_window_attention(q, k, v, sinks):
    B, S, H, D = q.shape
    KV = k.shape[2]
    G = H // KV
    W = WINDOW
    NB = S // W
    qb = q.reshape(B, NB, W, KV, G, D)
    kb = k.reshape(B, NB, W, KV, D)
    vb = v.reshape(B, NB, W, KV, D)
    kk = jnp.concatenate([jnp.concatenate([jnp.zeros_like(kb[:, :1]), kb[:, :-1]], axis=1), kb], axis=2)
    vv = jnp.concatenate([jnp.concatenate([jnp.zeros_like(vb[:, :1]), vb[:, :-1]], axis=1), vb], axis=2)
    s = jnp.einsum('bnqkgd,bnskd->bnkgqs', qb, kk) * (D ** -0.5)
    qpos = jnp.arange(W)[:, None] + W
    kpos = jnp.arange(2 * W)[None, :]
    diff = qpos - kpos
    band = (diff >= 0) & (diff < W)
    first = (jnp.arange(NB) == 0)[:, None, None]
    valid = band[None] & ~(first & (kpos[None] < W))
    s = jnp.where(valid[None, :, None, None], s, -jnp.inf)
    sink = sinks.astype(jnp.float32).reshape(1, 1, KV, G, 1, 1)
    mx = jnp.maximum(jnp.max(s, axis=-1, keepdims=True), sink)
    p = jnp.exp(s - mx)
    denom = jnp.sum(p, axis=-1, keepdims=True) + jnp.exp(sink - mx)
    o = jnp.einsum('bnkgqs,bnskd->bnqkgd', p / denom, vv)
    return o.reshape(B, S, H * D)

def token_mixer(h, w_in, qk_conv_w, qk_conv_b, gate_bias, mh_norm_g, attn_sinks, w_out):
    B, S, _ = h.shape
    z = h @ w_in
    parts = []
    off = 0
    for w in SPLITS:
        parts.append(z[..., off:off + w])
        off += w
    mq, mk, mv, mo, mif, aq, ak, av = parts
    qk = jax.nn.silu(causal_dwconv(jnp.concatenate([mq, mk], axis=-1), qk_conv_w) + qk_conv_b)
    qk = qk.astype(jnp.float32)
    mq_h = qk[..., :MLSTM_QK_W].reshape(B, S, MLSTM_HEADS, MLSTM_QK_DIM)
    mk_h = qk[..., MLSTM_QK_W:].reshape(B, S, MLSTM_HEADS, MLSTM_QK_DIM)
    mv_h = mv.astype(jnp.float32).reshape(B, S, MLSTM_HEADS, MLSTM_V_DIM)
    gates = mif.astype(jnp.float32) + gate_bias.astype(jnp.float32)
    log_i = gates[..., :MLSTM_HEADS]
    log_f = jax.nn.log_sigmoid(gates[..., MLSTM_HEADS:])
    ht = mlstm_chunkwise(mq_h, mk_h, mv_h, log_i, log_f)
    ht = ht * lax.rsqrt(jnp.mean(ht * ht, axis=-1, keepdims=True) + EPS)
    m_out = ht.reshape(B, S, MLSTM_W) * mh_norm_g.astype(jnp.float32) * jax.nn.sigmoid(mo.astype(jnp.float32))
    q = rope(aq.reshape(B, S, ATTN_HEADS, ATTN_HEAD_DIM))
    k = rope(ak.reshape(B, S, ATTN_KV_HEADS, ATTN_HEAD_DIM))
    v = av.astype(jnp.float32).reshape(B, S, ATTN_KV_HEADS, ATTN_HEAD_DIM)
    a_out = sliding_window_attention(q, k, v, attn_sinks)
    y = jnp.concatenate([m_out, a_out], axis=-1).astype(h.dtype)
    return y @ w_out

def conv_ffn(h, w_up, ffn_conv_w, w_down):
    u = causal_dwconv(h @ w_up, ffn_conv_w)
    gate, val = u[..., :D_FF], u[..., D_FF:]
    return (jax.nn.silu(gate) * val) @ w_down

def first_inputs(seed: int = 0) -> dict:
    key = jax.random.key(seed)
    ks = jax.random.split(key, 20)
    f32 = jnp.float32
    nrm = lambda k, shape: jax.random.normal(k, shape, f32)
    return {
        "x": nrm(ks[0], (BATCH, SEQ, D_MODEL)),
        "g_pre_mix": 1.0 + 0.05 * nrm(ks[1], (DEPTH, D_MODEL)),
        "w_in": nrm(ks[2], (DEPTH, D_MODEL, IN_W)) * D_MODEL ** -0.5,
        "qk_conv_w": nrm(ks[3], (DEPTH, QK_CONV, 2 * MLSTM_QK_W)) * QK_CONV ** -0.5,
        "qk_conv_b": 0.02 * nrm(ks[4], (DEPTH, 2 * MLSTM_QK_W)),
        "gate_bias": jnp.concatenate([0.1 * nrm(ks[5], (DEPTH, MLSTM_HEADS)),
                                      FORGET_BIAS + 0.5 * nrm(ks[6], (DEPTH, MLSTM_HEADS))], axis=-1),
        "mh_norm_g": 1.0 + 0.05 * nrm(ks[7], (DEPTH, MLSTM_W)),
        "attn_sinks": 0.5 * nrm(ks[8], (DEPTH, ATTN_HEADS)),
        "w_out": nrm(ks[9], (DEPTH, MIX_W, D_MODEL)) * MIX_W ** -0.5,
        "g_post_mix": 1.0 + 0.05 * nrm(ks[10], (DEPTH, D_MODEL)),
        "g_pre_ffn": 1.0 + 0.05 * nrm(ks[11], (DEPTH, D_MODEL)),
        "w_up": nrm(ks[12], (DEPTH, D_MODEL, 2 * D_FF)) * D_MODEL ** -0.5,
        "ffn_conv_w": nrm(ks[13], (DEPTH, FFN_CONV, 2 * D_FF)) * FFN_CONV ** -0.5,
        "w_down": nrm(ks[14], (DEPTH, D_FF, D_MODEL)) * D_FF ** -0.5,
        "g_post_ffn": 1.0 + 0.05 * nrm(ks[15], (DEPTH, D_MODEL)),
    }

def first_block(x, g_pre_mix, w_in, qk_conv_w, qk_conv_b, gate_bias, mh_norm_g, attn_sinks, w_out,
              g_post_mix, g_pre_ffn, w_up, ffn_conv_w, w_down, g_post_ffn):
    for l in range(DEPTH):
        h = rmsnorm(x, g_pre_mix[l])
        y = token_mixer(h, w_in[l], qk_conv_w[l], qk_conv_b[l], gate_bias[l], mh_norm_g[l],
                        attn_sinks[l], w_out[l])
        x = x + rmsnorm(y, g_post_mix[l])
        h = rmsnorm(x, g_pre_ffn[l])
        y = conv_ffn(h, w_up[l], ffn_conv_w[l], w_down[l])
        x = x + rmsnorm(y, g_post_ffn[l])
    return x


GRID_W = 64
CTX_LEN = 256
D_MIX = D_MODEL
HEAD_DIM = 64
POOL_GROUPS = 4
POOL_WINDOWS = (2, 4, 8, 16)
POOL_DIM = D_MIX // 4
POOL_GROUP_DIM = POOL_DIM // POOL_GROUPS
NA_HEADS = (D_MIX - POOL_DIM) // 2 // HEAD_DIM
NA_DIM = NA_HEADS * HEAD_DIM
NA_KH = 8
NA_KW = 16
RET_HEADS = (D_MIX - POOL_DIM - NA_DIM) // HEAD_DIM
RET_DIM = RET_HEADS * HEAD_DIM
RET_CHUNK = 128
CONV_W = 3
ROPE_BASE = 10000.0
ROT_QUARTER = HEAD_DIM // 4
NEG_INF = -1e30
IN_SIZES = (POOL_DIM, NA_DIM, NA_DIM, NA_DIM, RET_DIM, RET_DIM, RET_DIM, RET_DIM)
IN_DIM = sum(IN_SIZES)
SPLIT_POINTS = tuple(int(s) for s in np.cumsum(IN_SIZES)[:-1])


def rmsnorm_2(t, g):
    tf = t.astype(jnp.float32)
    y = tf * lax.rsqrt(jnp.mean(tf * tf, axis=-1, keepdims=True) + EPS) * g.astype(jnp.float32)
    return y.astype(t.dtype)

def modulate(t, shift, scale):
    return t * (1 + scale) + shift

def heads(t, n):
    return t.reshape(t.shape[0], t.shape[1], n, HEAD_DIM)

def pool_mixer(p, w_grp, scale):
    B, L, _ = p.shape
    pf = p.astype(jnp.float32).reshape(B, L, POOL_GROUPS, POOL_GROUP_DIM)
    csum = jnp.concatenate([jnp.zeros_like(pf[:, :1]), jnp.cumsum(pf, axis=1)], axis=1)
    t = jnp.arange(L)[:, None]
    win = jnp.asarray(POOL_WINDOWS, dtype=jnp.int32)[None, :]
    lo = jnp.clip(t - win // 2, 0, L)
    hi = jnp.clip(t - win // 2 + win, 0, L)
    g = jnp.arange(POOL_GROUPS)[None, :]
    total = csum[:, hi, g] - csum[:, lo, g]
    mean = total / (hi - lo).astype(jnp.float32)[None, :, :, None]
    y = jnp.einsum('blgc,gcd->blgd', mean - pf, w_grp.astype(jnp.float32))
    return (y.reshape(B, L, POOL_DIM) * scale.astype(jnp.float32)).astype(p.dtype)

def neighborhood_attention(q, k, v, kc, vc, rpb, rows):
    B, L, H, dh = q.shape
    kh = min(NA_KH, rows)
    span = 2 * NA_KW
    n_cb = GRID_W // NA_KW
    qg = (q * dh ** -0.5).reshape(B, rows, GRID_W, H, dh)
    kg = k.reshape(B, rows, GRID_W, H, dh)
    vg = v.reshape(B, rows, GRID_W, H, dh)
    qcol = np.arange(GRID_W).reshape(n_cb, NA_KW)
    win_start = np.clip(qcol - NA_KW // 2, 0, GRID_W - NA_KW)
    col_start = np.clip(np.arange(n_cb) * NA_KW - NA_KW // 2, 0, GRID_W - span)
    kcol = col_start[:, None] + np.arange(span)
    col_valid = (kcol[:, None, :] >= win_start[:, :, None]) & (kcol[:, None, :] < win_start[:, :, None] + NA_KW)
    dc_idx = np.clip(kcol[:, None, :] - qcol[:, :, None] + NA_KW - 1, 0, 2 * NA_KW - 2)
    rpb_c = rpb.astype(jnp.float32)[:, :, dc_idx]
    valid = jnp.asarray(col_valid)[:, :, None, :]

    def one_row(r):
        rs = jnp.clip(r - kh // 2, 0, rows - kh)
        qr = lax.dynamic_index_in_dim(qg, r, axis=1, keepdims=False)
        kr = lax.dynamic_slice_in_dim(kg, rs, kh, axis=1)
        vr = lax.dynamic_slice_in_dim(vg, rs, kh, axis=1)
        kb = kr[:, :, kcol]
        vb = vr[:, :, kcol]
        qb = qr.reshape(B, n_cb, NA_KW, H, dh)
        dr_idx = rs + jnp.arange(kh) - r + NA_KH - 1
        bias = rpb_c[:, dr_idx].transpose(0, 2, 3, 1, 4)
        s_loc = jnp.einsum('bnqhd,binshd->bhnqis', qb, kb).astype(jnp.float32)
        s_loc = jnp.where(valid, s_loc + bias, NEG_INF)
        s_ctx = jnp.einsum('bnqhd,bkhd->bhnqk', qb, kc).astype(jnp.float32)
        s = jnp.concatenate([s_loc.reshape(B, H, n_cb, NA_KW, kh * span), s_ctx], axis=-1)
        p = jax.nn.softmax(s, axis=-1).astype(v.dtype)
        p_loc = p[..., :kh * span].reshape(B, H, n_cb, NA_KW, kh, span)
        p_ctx = p[..., kh * span:]
        o = jnp.einsum('bhnqis,binshd->bnqhd', p_loc, vb) + jnp.einsum('bhnqk,bkhd->bnqhd', p_ctx, vc)
        return o.reshape(B, GRID_W, H, dh)

    out = lax.map(one_row, jnp.arange(rows))
    return out.transpose(1, 0, 2, 3, 4).reshape(B, L, H, dh)

def context_attention(q, k, v):
    s = jnp.einsum('bqhd,bkhd->bhqk', q * HEAD_DIM ** -0.5, k).astype(jnp.float32)
    p = jax.nn.softmax(s, axis=-1).astype(v.dtype)
    return jnp.einsum('bhqk,bkhd->bqhd', p, v)

def axial_rotary(t, cos_r, sin_r, cos_c, sin_c):
    def rot(u, cos, sin):
        u1, u2 = jnp.split(u, 2, axis=-1)
        cos = cos[None, :, None, :]
        sin = sin[None, :, None, :]
        return jnp.concatenate([u1 * cos - u2 * sin, u1 * sin + u2 * cos], axis=-1)
    tr, tc = jnp.split(t, 2, axis=-1)
    return jnp.concatenate([rot(tr, cos_r, sin_r), rot(tc, cos_c, sin_c)], axis=-1)

def retention_chunks(q, k, v, log_gamma, state, with_outputs):
    B, L, H, _ = q.shape
    n = L // RET_CHUNK
    lg = log_gamma.astype(jnp.float32)
    idx = jnp.arange(RET_CHUNK, dtype=jnp.float32)
    diff = idx[:, None] - idx[None, :]
    intra = jnp.exp(jnp.where(diff[None] >= 0, diff[None] * lg[:, None, None], -jnp.inf))
    q_dec = jnp.exp((idx + 1)[None, :] * lg[:, None])
    k_dec = jnp.exp((RET_CHUNK - 1 - idx)[None, :] * lg[:, None])
    c_dec = jnp.exp(RET_CHUNK * lg)

    def to_chunks(t):
        return t.reshape(B, n, RET_CHUNK, H, t.shape[-1]).transpose(1, 0, 3, 2, 4)

    def step(s, blk):
        qb, kb, vb = blk
        s_new = s * c_dec[None, :, None, None] + jnp.einsum('bhcd,bhce->bhde', kb * k_dec[None, :, :, None], vb)
        if not with_outputs:
            return s_new, None
        a = jnp.einsum('bhid,bhjd->bhij', qb, kb) * intra[None]
        y = jnp.einsum('bhij,bhje->bhie', a, vb) + jnp.einsum('bhid,bhde->bhie', qb, s) * q_dec[None, :, :, None]
        return s_new, y

    s_fin, ys = lax.scan(step, state, (to_chunks(q), to_chunks(k), to_chunks(v)))
    if not with_outputs:
        return None, s_fin
    return ys.transpose(1, 0, 3, 2, 4).reshape(B, L, H, v.shape[-1]), s_fin

def bidirectional_retention(q, k, v, qc, kc, vc, dec_f, dec_b, need_ctx):
    B = q.shape[0]
    s0 = jnp.zeros((B, RET_HEADS, HEAD_DIM, HEAD_DIM), jnp.float32)
    rev = lambda t: jnp.flip(t, axis=1)
    yc_f, s_f = retention_chunks(qc, kc, vc, dec_f, s0, need_ctx)
    yx_f, _ = retention_chunks(q, k, v, dec_f, s_f, True)
    yc_b, s_b = retention_chunks(rev(qc), rev(kc), rev(vc), dec_b, s0, need_ctx)
    yx_b, _ = retention_chunks(rev(q), rev(k), rev(v), dec_b, s_b, True)
    yc = yc_f + rev(yc_b) if need_ctx else None
    return yx_f + rev(yx_b), yc

def retention_output(y, gate, gn_g):
    B, L = y.shape[:2]
    mu = jnp.mean(y, axis=-1, keepdims=True)
    var = jnp.mean((y - mu) ** 2, axis=-1, keepdims=True)
    yn = ((y - mu) * lax.rsqrt(var + EPS)).reshape(B, L, RET_DIM) * gn_g.astype(jnp.float32)
    return (jax.nn.silu(gate.astype(jnp.float32)) * yn).astype(gate.dtype)

def mixing_layer(px, pc, pool_w, pool_scale, na_rpb, dec_f, dec_b, gn_g, rope, rows, need_ctx):
    B, L, _ = px.shape
    xs = jnp.split(px, SPLIT_POINTS, axis=-1)
    cs = jnp.split(pc, SPLIT_POINTS, axis=-1)
    f32 = jnp.float32
    pool_x = pool_mixer(xs[0], pool_w, pool_scale)
    na_q, na_k, na_v = [heads(t, NA_HEADS) for t in xs[1:4]]
    nc_q, nc_k, nc_v = [heads(t, NA_HEADS) for t in cs[1:4]]
    na_x = neighborhood_attention(na_q, na_k, na_v, nc_k, nc_v, na_rpb, rows).reshape(B, L, NA_DIM)
    rq = axial_rotary(heads(xs[4], RET_HEADS).astype(f32), *rope)
    rk = axial_rotary(heads(xs[5], RET_HEADS).astype(f32), *rope) * HEAD_DIM ** -0.5
    rv = heads(xs[6], RET_HEADS).astype(f32)
    cq = heads(cs[4], RET_HEADS).astype(f32)
    ck = heads(cs[5], RET_HEADS).astype(f32) * HEAD_DIM ** -0.5
    cv = heads(cs[6], RET_HEADS).astype(f32)
    ret_x, ret_c = bidirectional_retention(rq, rk, rv, cq, ck, cv, dec_f, dec_b, need_ctx)
    ret_x = retention_output(ret_x, xs[7], gn_g)
    yx = jnp.concatenate([pool_x, na_x.astype(px.dtype), ret_x.astype(px.dtype)], axis=-1)
    if not need_ctx:
        return yx, None
    pool_c = pool_mixer(cs[0], pool_w, pool_scale)
    na_c = context_attention(nc_q, nc_k, nc_v).reshape(B, pc.shape[1], NA_DIM)
    ret_c = retention_output(ret_c, cs[7], gn_g)
    yc = jnp.concatenate([pool_c, na_c.astype(pc.dtype), ret_c.astype(pc.dtype)], axis=-1)
    return yx, yc

def conv_ffn_2(h, w_up, conv_w, conv_b, w_down):
    u = h @ w_up
    up = jnp.pad(u, ((0, 0), (1, 1), (0, 0)))
    u = up[:, :-2] * conv_w[0] + up[:, 1:-1] * conv_w[1] + up[:, 2:] * conv_w[2] + conv_b
    a, b = jnp.split(u, 2, axis=-1)
    return (jax.nn.silu(a) * b) @ w_down

def second_inputs(seed: int = 0) -> dict:
    key = jax.random.key(seed)
    ks = jax.random.split(key, 24)
    f32 = jnp.float32
    nrm = lambda k, shape, s: jax.random.normal(k, shape, f32) * s
    exps_f = 5.0 + jnp.arange(RET_HEADS, dtype=f32)[None, :] + 0.25 * jax.random.uniform(ks[11], (DEPTH, RET_HEADS), f32)
    exps_b = 5.0 + jnp.arange(RET_HEADS, dtype=f32)[None, :] + 0.25 * jax.random.uniform(ks[12], (DEPTH, RET_HEADS), f32)
    return {
        "x": nrm(ks[0], (BATCH, SEQ, D_MODEL), 1.0),
        "c": nrm(ks[1], (BATCH, D_MODEL), 1.0),
        "ctx": nrm(ks[2], (BATCH, CTX_LEN, D_MODEL), 1.0),
        "c_ctx": nrm(ks[3], (D_MODEL,), 1.0),
        "w_mod": nrm(ks[4], (DEPTH, D_MODEL, 6 * D_MODEL), 0.5 * D_MODEL ** -0.5),
        "b_mod": nrm(ks[5], (DEPTH, 6 * D_MODEL), 0.02),
        "norm1_g": 1.0 + nrm(ks[6], (DEPTH, D_MODEL), 0.02),
        "w_in": nrm(ks[7], (DEPTH, D_MODEL, IN_DIM), D_MODEL ** -0.5),
        "pool_w": nrm(ks[8], (DEPTH, POOL_GROUPS, POOL_GROUP_DIM, POOL_GROUP_DIM), POOL_GROUP_DIM ** -0.5),
        "pool_scale": 1.0 + nrm(ks[9], (DEPTH, POOL_DIM), 0.1),
        "na_rpb": nrm(ks[10], (DEPTH, NA_HEADS, 2 * NA_KH - 1, 2 * NA_KW - 1), 0.1),
        "ret_decay_fwd": jnp.log1p(-jnp.exp2(-exps_f)),
        "ret_decay_bwd": jnp.log1p(-jnp.exp2(-exps_b)),
        "ret_gn_g": 1.0 + nrm(ks[13], (DEPTH, RET_DIM), 0.02),
        "w_out": nrm(ks[14], (DEPTH, D_MIX, D_MODEL), D_MIX ** -0.5),
        "norm2_g": 1.0 + nrm(ks[15], (DEPTH, D_MODEL), 0.02),
        "w_up": nrm(ks[16], (DEPTH, D_MODEL, 2 * D_FF), D_MODEL ** -0.5),
        "conv_w": nrm(ks[17], (DEPTH, CONV_W, 2 * D_FF), CONV_W ** -0.5),
        "conv_b": nrm(ks[18], (DEPTH, 2 * D_FF), 0.02),
        "w_down": nrm(ks[19], (DEPTH, D_FF, D_MODEL), D_FF ** -0.5),
        "final_g": 1.0 + nrm(ks[20], (D_MODEL,), 0.02),
    }

def second_block(x, c, ctx, c_ctx, w_mod, b_mod, norm1_g, w_in, pool_w, pool_scale, na_rpb, ret_decay_fwd, ret_decay_bwd, ret_gn_g, w_out, norm2_g, w_up, conv_w, conv_b, w_down, final_g):
    B, L, _ = x.shape
    rows = L // GRID_W
    pos = jnp.arange(L)
    inv = ROPE_BASE ** (-jnp.arange(ROT_QUARTER, dtype=jnp.float32) / ROT_QUARTER)
    ang_r = (pos // GRID_W).astype(jnp.float32)[:, None] * inv[None, :]
    ang_c = (pos % GRID_W).astype(jnp.float32)[:, None] * inv[None, :]
    rope = (jnp.cos(ang_r), jnp.sin(ang_r), jnp.cos(ang_c), jnp.sin(ang_c))
    silu_c = jax.nn.silu(c)[:, None, :]
    silu_cc = jax.nn.silu(c_ctx)
    h = x
    hc = ctx
    for l in range(DEPTH):
        need_ctx = l < DEPTH - 1
        mx = jnp.split(silu_c @ w_mod[l] + b_mod[l], 6, axis=-1)
        mc = jnp.split(silu_cc @ w_mod[l] + b_mod[l], 6, axis=-1)
        ax = modulate(rmsnorm_2(h, norm1_g[l]), mx[0], mx[1])
        ac = modulate(rmsnorm_2(hc, norm1_g[l]), mc[0], mc[1])
        yx, yc = mixing_layer(ax @ w_in[l], ac @ w_in[l], pool_w[l], pool_scale[l], na_rpb[l],
                              ret_decay_fwd[l], ret_decay_bwd[l], ret_gn_g[l], rope, rows, need_ctx)
        h = h + mx[2] * (yx @ w_out[l])
        h = h + mx[5] * conv_ffn_2(modulate(rmsnorm_2(h, norm2_g[l]), mx[3], mx[4]), w_up[l], conv_w[l], conv_b[l], w_down[l])
        if need_ctx:
            hc = hc + mc[2] * (yc @ w_out[l])
            hc = hc + mc[5] * conv_ffn_2(modulate(rmsnorm_2(hc, norm2_g[l]), mc[3], mc[4]), w_up[l], conv_w[l], conv_b[l], w_down[l])
    return rmsnorm_2(h, final_g)


def setup_inputs(seed=0):
    out = dict(first_inputs(seed))
    for name, value in second_inputs(seed + 1).items():
        if name != "x":
            out[name + "_2"] = value
    return out


def reference(
    x, g_pre_mix, w_in, qk_conv_w, qk_conv_b, gate_bias, mh_norm_g, attn_sinks, w_out,
    g_post_mix, g_pre_ffn, w_up, ffn_conv_w, w_down, g_post_ffn, c_2, ctx_2, c_ctx_2, w_mod_2,
    b_mod_2, norm1_g_2, w_in_2, pool_w_2, pool_scale_2, na_rpb_2, ret_decay_fwd_2,
    ret_decay_bwd_2, ret_gn_g_2, w_out_2, norm2_g_2, w_up_2, conv_w_2, conv_b_2, w_down_2,
    final_g_2,
):
    x = first_block(
        x, g_pre_mix, w_in, qk_conv_w, qk_conv_b, gate_bias, mh_norm_g, attn_sinks, w_out,
        g_post_mix, g_pre_ffn, w_up, ffn_conv_w, w_down, g_post_ffn,
    )
    return second_block(
        x, c_2, ctx_2, c_ctx_2, w_mod_2, b_mod_2, norm1_g_2, w_in_2, pool_w_2, pool_scale_2,
        na_rpb_2, ret_decay_fwd_2, ret_decay_bwd_2, ret_gn_g_2, w_out_2, norm2_g_2, w_up_2,
        conv_w_2, conv_b_2, w_down_2, final_g_2,
    )


_drawn_inputs = setup_inputs


def setup_inputs(seed=0):
    import zlib

    import numpy as np

    out = dict(_drawn_inputs(seed))
    spreads = {}
    factors = {'attn_sinks': 2.714,
     'b_mod_2': 3.808,
     'norm1_g_2': 8.0,
     'pool_scale_2': 8.0,
     'na_rpb_2': 31.717,
     'ret_decay_fwd_2': 3.651,
     'ret_decay_bwd_2': 3.618,
     'ret_gn_g_2': 8.0,
     'norm2_g_2': 8.0,
     'conv_b_2': 8.0,
     'final_g_2': 8.083}
    for name, (base, spread) in spreads.items():
        noise = np.random.default_rng([zlib.crc32(name.encode()), seed]).standard_normal(out[name].shape)
        drawn = base * np.exp(spread * noise) if base else spread * noise
        out[name] = __import__('jax').numpy.asarray(drawn.astype(out[name].dtype))
    for name, factor in factors.items():
        out[name] = (out[name] * factor).astype(out[name].dtype)
    return out
```

```python
from contextlib import ExitStack

import numpy as np

import concourse.bass as bass
from concourse import mybir

F32 = mybir.dt.float32
F32R = mybir.dt.float32r
ALU = mybir.AluOpType
ACT = mybir.ActivationFunctionType
AX = mybir.AxisListType

P = 128
D = 1024
DC = D // P
SEQ = 512
CTX = 256
TOK = SEQ + CTX
DEPTH = 2
EPS = 1e-6
FF = 2816
HALF = FF // P // 2
PAIR = 2 * P

Q1, K1, V1, O1, AQ1, AK1, AV1, GT1 = 0, 2, 4, 8, 12, 16, 17, 18
N1 = 19
NK, NV, RK, RV, PO, NQ, RQ, RG = 0, 3, 6, 9, 12, 14, 17, 20
N2 = 23
N2_KV = 12
NA_H = 6
RET_H = 6
GRID = 64
SPAN = 32
COL0 = (0, 8, 24, 32)

V1_PRE, V1_CW, V1_CB, V1_GI, V1_GF, V1_MH, V1_SINK, V1_POST, V1_PREF, V1_FCW, V1_POSTF = (
    0, 8, 24, 28, 29, 30, 34, 42, 50, 58, 58 + 132)
V1_N = V1_POSTF + 8
V2_BM, V2_N1, V2_PS, V2_LF, V2_LB, V2_GN, V2_N2, V2_CW, V2_CB = (
    0, 48, 56, 58, 64, 70, 73, 81, 81 + 132)
V2_N = V2_CB + 44

C_ID, C_BLK, C_RR = 0, 128, 256
C_SMALL = 384
C1_MASK, C1_COS, C1_SIN, C1_RP, C1_SELF, C1_SELH = 0, 256, 768, 1280, 1408, 1412
C1_N = C1_SELH + 512
CN_MASK = 1024
CR_COS, CR_SIN, CR_DP, CR_DN, CR_QF, CR_QB, CR_MF, CR_MB, CR_KE = (
    0, 512, 1024, 1536, 2048, 2560, 3072, 3200, 3328)
CR_N = CR_KE + 4


def ranges(tokens):
    return [(0, SEQ)] + ([(SEQ, CTX)] if tokens == TOK else [])


class Signal:

    def __init__(self, nc, ctx, name):
        self.sem = ctx.enter_context(nc.semaphore(name))
        self.base = 0
        self.n = 0

    def at(self, n):
        return n + self.base

    def next(self):
        self.n += 1
        return self.base + self.n


def later(n):
    return not isinstance(n, int) or n > 0


def tile_loop(eng, n, body, tail=1):
    pairs = (n - tail) // 2
    body(0, 0)
    body(1, 1)
    if pairs > 1:
        with eng.Fori(1, pairs) as i:
            body(i * 2, 0)
            body(i * 2 + 1, 1)
    for t in range(max(2, 2 * pairs), n):
        body(t, t % 2)


def at(i, n=1):
    return slice(i, i + n) if isinstance(i, int) else bass.ds(i, n)


def build(nc, a, out):
    ctx = ExitStack()
    with ctx:
        base = (nc.sbuf_base + 31) // 32 * 32
        used = [base]

        def sb(name, shape, dt=F32, offset=None):
            size = 4 * int(np.prod(shape[1:]))
            if offset is None:
                offset = used[0]
                used[0] += (size + 31) // 32 * 32
            return nc.alloc_sbuf_tensor_at(name, shape, dt, offset=offset)

        def room(size):
            offset = used[0]
            used[0] += (size + 31) // 32 * 32
            return offset

        X = sb("X", [P, DC, TOK])
        o_h = used[0]
        HH = sb("HH", [P, DC, TOK], F32R)
        HL = sb("HL", [P, DC, TOK], F32R)
        o_big = room(N2 * TOK * 4)
        o_stage = used[0]
        STAGE = [sb(f"STAGE{s}", [P, HALF * P]) for s in range(2)]
        WH = [sb(f"WH{s}", [P, HALF * P], F32R) for s in range(2)]
        WL = [sb(f"WL{s}", [P, HALF * P], F32R) for s in range(2)]
        o_tmp = room(5 * TOK * 4)
        SQ = [sb(f"SQ{s}", [P, TOK], offset=o_tmp + s * TOK * 4) for s in range(2)]
        SUM = sb("SUM", [P, TOK], offset=o_tmp + 2 * TOK * 4)
        RSTD = sb("RSTD", [P, TOK], offset=o_tmp + 3 * TOK * 4)
        CG = sb("CG", [P, TOK], offset=o_tmp)
        CV = sb("CV", [P, TOK], offset=o_tmp + TOK * 4)
        T1 = [sb(f"T1{s}", [P, TOK], offset=o_tmp + s * TOK * 4) for s in range(2)]
        VEC = sb("VEC", [P, max(V1_N, V2_N)])
        CS = sb("CS", [P, C_SMALL])
        IDENT, BLK, RROT = CS[:, 0:128], CS[:, 128:256], CS[:, 256:384]
        ONES = sb("ONES", [P, P])
        EPSC = sb("EPSC", [P, 1])
        ZERO = sb("ZERO", [P, 1])
        MEAN = sb("MEAN", [P, P])
        MOD = sb("MOD", [P, 48, 2])
        A1 = sb("A1", [P, DC, 2])
        A2 = sb("A2", [P, DC, 2])
        CC = sb("CC", [P, DC, 2])
        SC = sb("SC", [P, DC, 2])
        SM = sb("SM", [P, 256])
        assert used[0] <= nc.sbuf_usable_end, used[0]

        Z = sb("Z", [P, N2, TOK], offset=o_big)
        Z1 = sb("Z1", [P, N1, SEQ], offset=o_big)
        GH = sb("GH", [P, HALF, TOK], F32R, offset=o_big)
        GL = sb("GL", [P, HALF, TOK], F32R, offset=o_big + HALF * TOK * 4)
        GH1 = sb("GH1", [P, HALF, SEQ], F32R, offset=o_big)
        GL1 = sb("GL1", [P, HALF, SEQ], F32R, offset=o_big + HALF * SEQ * 4)
        Y = sb("Y", [P, DC, SEQ], offset=o_big + 2 * HALF * SEQ * 4)

        PS = [ctx.enter_context(nc.psum_tensor(f"PS{i}", [P, 1024], F32)) for i in range(4)]

        sig = {}

        def S(name):
            if name not in sig:
                sig[name] = Signal(nc, ctx, name)
            return sig[name]

        def block():
            return nc.Block(no_gpsimd_drain=True)

        def done(**counts):
            for name, n in counts.items():
                S(name).base += n
                S(name).n = 0

        def load(pairs):
            loaded = S("small_loaded")
            with block() as b:
                @b.sync
                def _(sp):
                    for dst, src in pairs:
                        sp.dma_start(dst, src).then_inc(loaded.sem, 16)
                    sp.wait_ge(loaded.sem, loaded.at(16 * len(pairs)))
            done(small_loaded=16 * len(pairs))

        def gemm(weights, first, n, kc, rhs_hi, rhs_lo, tokens, out_act=None, out_dve=None):
            loaded = [S("w_loaded0"), S("w_loaded1")]
            w_hi, w_lo, acc_done, acc_free = S("w_hi"), S("w_lo"), S("acc_done"), S("acc_free")
            size = kc * P

            with block() as b:
                @b.sync
                def _(sp):
                    def body(t, s):
                        if later(t - 1):
                            sp.wait_ge(w_lo.sem, w_lo.at(t - 1))
                        src = weights[at(t + first)].rearrange("a p n -> p (a n)")
                        sp.dma_start(STAGE[s][:, 0:size], src).then_inc(loaded[s].sem, 16)
                    tile_loop(sp, n, body)

                @b.scalar
                def _(act):
                    def split(t, s, half):
                        if later(half):
                            act.wait_ge(loaded[s].sem, loaded[s].at(half))
                        act.activation(WH[s][:, 0:size], STAGE[s][:, 0:size],
                                       ACT.Copy).then_inc(w_hi.sem, 1)

                    def body(t, s):
                        act.wait_ge(acc_done.sem, acc_done.at(t + 1))
                        if out_act:
                            out_act(act, t, PS[s]).then_inc(acc_free.sem, 1)
                        if not isinstance(t, int) or t + 2 < n:
                            split(t + 2, s, (t + 2 - s) * 8 + 16)
                    split(0, 0, 16)
                    split(1, 1, 16)
                    tile_loop(act, n, body, tail=2)

                @b.vector
                def _(dve):
                    def split(t, s):
                        dve.wait_ge(w_hi.sem, w_hi.at(t + 1))
                        dve.tensor_tensor(WL[s][:, 0:size], STAGE[s][:, 0:size],
                                          WH[s][:, 0:size].bitcast(F32),
                                          ALU.subtract).then_inc(w_lo.sem, 1)

                    def body(t, s):
                        if out_dve:
                            dve.wait_ge(acc_done.sem, acc_done.at(t + 1))
                            out_dve(dve, t, PS[s]).then_inc(acc_free.sem, 1)
                        if not isinstance(t, int) or t + 2 < n:
                            split(t + 2, s)
                    split(0, 0)
                    split(1, 1)
                    tile_loop(dve, n, body, tail=2)

                @b.tensor
                def _(pe):
                    def body(t, s):
                        pe.wait_ge(w_lo.sem, w_lo.at(t + 1))
                        if later(t - 1):
                            pe.wait_ge(acc_free.sem, acc_free.at(t - 1))
                        product(pe, PS[s], s, kc, rhs_hi, rhs_lo, tokens).then_inc(acc_done.sem, 1)
                    tile_loop(pe, n, body)
            even, odd = (n + 1) // 2, n // 2
            done(w_loaded0=16 * even, w_loaded1=16 * odd, w_hi=n, w_lo=n, acc_done=n, acc_free=n)

        def product(pe, acc, s, kc, rhs_hi, rhs_lo, tokens):
            for k in range(kc):
                parts = ((WH[s], rhs_hi), (WH[s], rhs_lo), (WL[s], rhs_hi))
                for j, (w, r) in enumerate(parts):
                    for t0, tn in ranges(tokens):
                        ins = pe.matmul(acc[:, t0:t0 + tn], w[:, k * P:k * P + P], r[:, k, t0:t0 + tn],
                                        start=(k == 0 and j == 0), stop=(k == kc - 1 and j == 2))
            return ins

        def statistics(act, dve, pe, src, tokens, part):
            sq_done, sum_done, ms_done, lg, rstd = (S("sq_done"), S("sum_done"), S("ms_done"),
                                                    S("log_done"), S("rstd_done"))
            if part == "act":
                for c in range(1, DC):
                    if c > 2:
                        if later(c - 1):
                            act.wait_ge(sum_done.sem, sum_done.at(c - 1))
                    act.activation(SQ[c % 2][:, 0:tokens], src[:, c, 0:tokens],
                                   ACT.Square).then_inc(sq_done.sem, 1)
                act.wait_ge(ms_done.sem, ms_done.at(1))
                act.activation(RSTD[:, 0:tokens], PS[2][:, 0:tokens], ACT.Ln,
                               bias=EPSC[:, 0:1]).then_inc(lg.sem, 1)
                act.wait_ge(lg.sem, lg.at(1))
                act.activation(RSTD[:, 0:tokens], RSTD[:, 0:tokens], ACT.Exp,
                               scale=-0.5).then_inc(rstd.sem, 1)
            if part == "dve":
                dve.tensor_tensor(SUM[:, 0:tokens], src[:, 0, 0:tokens], src[:, 0, 0:tokens],
                                  ALU.mult).then_inc(sum_done.sem, 1)
                for c in range(1, DC):
                    dve.wait_ge(sq_done.sem, sq_done.at(c))
                    dve.wait_ge(sum_done.sem, sum_done.at(c))
                    dve.tensor_tensor(SUM[:, 0:tokens], SUM[:, 0:tokens], SQ[c % 2][:, 0:tokens],
                                      ALU.add).then_inc(sum_done.sem, 1)
            if part == "pe":
                pe.wait_ge(sum_done.sem, sum_done.at(DC))
                for t0, tn in ranges(tokens):
                    ins = pe.matmul(PS[2][:, t0:t0 + tn], MEAN[:], SUM[:, t0:t0 + tn],
                                    start=True, stop=True)
                ins.then_inc(ms_done.sem, 1)

        STATS = dict(sq_done=DC - 1, sum_done=DC, ms_done=1, log_done=1, rstd_done=1)

        def pre_norm(scale, shift, tokens):
            rstd, t_done, hi_done, lo_done = S("rstd_done"), S("t_done"), S("h_hi"), S("h_lo")
            rs = ranges(tokens)
            with block() as b:
                @b.tensor
                def _(pe):
                    statistics(None, None, pe, X, tokens, "pe")

                @b.scalar
                def _(act):
                    statistics(act, None, None, X, tokens, "act")
                    for c in range(DC):
                        act.wait_ge(t_done.sem, t_done.at(c + 1))
                        for st, (t0, tn) in enumerate(rs):
                            ins = act.activation(HH[:, c, t0:t0 + tn], T1[c % 2][:, t0:t0 + tn],
                                                 ACT.Identity, bias=shift(c, st))
                        ins.then_inc(hi_done.sem, 1)

                @b.vector
                def _(dve):
                    statistics(None, dve, None, X, tokens, "dve")
                    dve.wait_ge(rstd.sem, rstd.at(1))

                    def normed(c):
                        if later(c - 1):
                            dve.wait_ge(lo_done.sem, lo_done.at(c - 1))
                        for st, (t0, tn) in enumerate(rs):
                            ins = dve.scalar_tensor_tensor(
                                out=T1[c % 2][:, t0:t0 + tn], in0=X[:, c, t0:t0 + tn], scalar=scale(c, st),
                                in1=RSTD[:, t0:t0 + tn], op0=ALU.mult, op1=ALU.mult)
                        ins.then_inc(t_done.sem, 1)

                    normed(0)
                    for c in range(DC):
                        if c + 1 < DC:
                            normed(c + 1)
                        dve.wait_ge(hi_done.sem, hi_done.at(c + 1))
                        for st, (t0, tn) in enumerate(rs):
                            ins = dve.scalar_tensor_tensor(
                                out=HL[:, c, t0:t0 + tn], in0=T1[c % 2][:, t0:t0 + tn], scalar=shift(c, st),
                                in1=HH[:, c, t0:t0 + tn].bitcast(F32), op0=ALU.add, op1=ALU.subtract)
                        ins.then_inc(lo_done.sem, 1)
            done(**STATS, t_done=DC, h_hi=DC, h_lo=DC)

        def add_normed(src, gain):
            rstd, t_done, added = S("rstd_done"), S("t_done"), S("added")
            with block() as b:
                @b.tensor
                def _(pe):
                    statistics(None, None, pe, src, SEQ, "pe")

                @b.scalar
                def _(act):
                    statistics(act, None, None, src, SEQ, "act")

                @b.vector
                def _(dve):
                    statistics(None, dve, None, src, SEQ, "dve")
                    dve.wait_ge(rstd.sem, rstd.at(1))
                    for c in range(DC):
                        dve.scalar_tensor_tensor(out=src[:, c, :], in0=src[:, c, :], scalar=gain(c),
                                                 in1=RSTD[:, 0:SEQ], op0=ALU.mult,
                                                 op1=ALU.mult).then_inc(t_done.sem, 1)
                    for c in range(DC):
                        dve.wait_ge(t_done.sem, t_done.at(c + 1))
                        dve.tensor_tensor(X[:, c, 0:SEQ], X[:, c, 0:SEQ], src[:, c, :],
                                          ALU.add).then_inc(added.sem, 1)
            done(**STATS, t_done=DC, added=DC)

        def split_rows(src, chunks, tokens):
            hi_done, lo_done = S("h_hi"), S("h_lo")
            with block() as b:
                @b.scalar
                def _(act):
                    for c, z in enumerate(chunks):
                        act.activation(HH[:, c, 0:tokens], src[:, z, 0:tokens],
                                       ACT.Copy).then_inc(hi_done.sem, 1)

                @b.vector
                def _(dve):
                    for c, z in enumerate(chunks):
                        dve.wait_ge(hi_done.sem, hi_done.at(c + 1))
                        dve.tensor_tensor(HL[:, c, 0:tokens], src[:, z, 0:tokens],
                                          HH[:, c, 0:tokens].bitcast(F32),
                                          ALU.subtract).then_inc(lo_done.sem, 1)
            done(h_hi=DC, h_lo=DC)

        def ffn_up(weights, first, gh, gl, tokens, taps, tap_col, bias_col, half):
            n = 2 * HALF
            loaded = [S("w_loaded0"), S("w_loaded1")]
            w_hi, w_lo, acc_done, acc_free = S("w_hi"), S("w_lo"), S("acc_done"), S("acc_free")
            own_done, tap_done = S("own_done"), S("tap_done")
            silu_done, gated, g_hi, g_lo = S("silu_done"), S("gated"), S("g_hi"), S("g_lo")
            size = DC * P
            own, others = taps
            rs = ranges(tokens)

            def tap(t, k):
                return VEC[:, at(t * 3 + (tap_col + half * n * 3 + k))]

            with block() as b:
                @b.sync
                def _(sp):
                    def body(t, s):
                        if later(t - 1):
                            sp.wait_ge(w_lo.sem, w_lo.at(t - 1))
                        src = weights[at(t + first)].rearrange("a p n -> p (a n)")
                        sp.dma_start(STAGE[s][:, 0:size], src).then_inc(loaded[s].sem, 16)
                    tile_loop(sp, n, body)

                @b.scalar
                def _(act):
                    def split(t, s, arrived):
                        act.wait_ge(loaded[s].sem, loaded[s].at(arrived))
                        act.activation(WH[s][:, 0:size], STAGE[s][:, 0:size],
                                       ACT.Copy).then_inc(w_hi.sem, 1)

                    def body(t, s, j):
                        buf = (CG, CV)[s]
                        act.wait_ge(acc_done.sem, acc_done.at(t + 1))
                        if later(j):
                            act.wait_ge(g_lo.sem, g_lo.at(j))
                        bias = VEC[:, at(t + (bias_col + half * n))] if bias_col is not None else ZERO[:, 0:1]
                        act.activation(buf[:, 0:tokens], PS[s][:, 0:tokens], ACT.Identity,
                                       scale=tap(t, own), bias=bias).then_inc(own_done.sem, 1)
                        if not isinstance(t, int) or t + 2 < n:
                            split(t + 2, s, (t + 2 - s) * 8 + 16)
                        if s == 1:
                            if later(t):
                                act.wait_ge(acc_free.sem, acc_free.at(t))
                            act.activation(CG[:, 0:tokens], CG[:, 0:tokens],
                                           ACT.Silu).then_inc(silu_done.sem, 1)
                            act.wait_ge(gated.sem, gated.at(j + 1))
                            act.activation(gh[:, at(j), 0:tokens].rearrange("p a t -> p (a t)"),
                                           CV[:, 0:tokens], ACT.Copy).then_inc(g_hi.sem, 1)

                    split(0, 0, 16)
                    split(1, 1, 16)
                    body(0, 0, 0)
                    body(1, 1, 0)
                    with act.Fori(1, HALF - 1) as j:
                        body(j * 2, 0, j)
                        body(j * 2 + 1, 1, j)
                    body(n - 2, 0, HALF - 1)
                    body(n - 1, 1, HALF - 1)

                @b.vector
                def _(dve):
                    def split(t, s):
                        dve.wait_ge(w_hi.sem, w_hi.at(t + 1))
                        dve.tensor_tensor(WL[s][:, 0:size], STAGE[s][:, 0:size],
                                          WH[s][:, 0:size].bitcast(F32),
                                          ALU.subtract).then_inc(w_lo.sem, 1)

                    def body(t, s, j):
                        buf = (CG, CV)[s]
                        dve.wait_ge(own_done.sem, own_done.at(t + 1))
                        for m, (k, shift) in enumerate(others):
                            if m:
                                dve.wait_ge(tap_done.sem, tap_done.at(t + 1))
                            for r, (t0, tn) in enumerate(rs):
                                lo, hi = max(0, shift), min(0, shift)
                                ins = dve.scalar_tensor_tensor(
                                    out=buf[:, t0 + lo:t0 + tn + hi],
                                    in0=PS[s][:, t0 + lo - shift:t0 + tn + hi - shift], scalar=tap(t, k),
                                    in1=buf[:, t0 + lo:t0 + tn + hi], op0=ALU.mult, op1=ALU.add)
                                if r == len(rs) - 1:
                                    ins.then_inc((tap_done if m == 0 else acc_free).sem, 1)
                        if not isinstance(t, int) or t + 2 < n:
                            split(t + 2, s)
                        if s == 1:
                            dve.wait_ge(silu_done.sem, silu_done.at(j + 1))
                            dve.wait_ge(acc_free.sem, acc_free.at(t + 1))
                            dve.tensor_tensor(CV[:, 0:tokens], CV[:, 0:tokens], CG[:, 0:tokens],
                                              ALU.mult).then_inc(gated.sem, 1)
                            dve.wait_ge(g_hi.sem, g_hi.at(j + 1))
                            dve.tensor_tensor(gl[:, at(j), 0:tokens].rearrange("p a t -> p (a t)"),
                                              CV[:, 0:tokens],
                                              gh[:, at(j), 0:tokens].rearrange("p a t -> p (a t)").bitcast(F32),
                                              ALU.subtract).then_inc(g_lo.sem, 1)
                    split(0, 0)
                    split(1, 1)
                    body(0, 0, 0)
                    body(1, 1, 0)
                    with dve.Fori(1, HALF - 1) as j:
                        body(j * 2, 0, j)
                        body(j * 2 + 1, 1, j)
                    body(n - 2, 0, HALF - 1)
                    body(n - 1, 1, HALF - 1)

                @b.tensor
                def _(pe):
                    def body(t, s):
                        pe.wait_ge(w_lo.sem, w_lo.at(t + 1))
                        if later(t - 1):
                            pe.wait_ge(acc_free.sem, acc_free.at(t - 1))
                        product(pe, PS[s], s, DC, HH, HL, tokens).then_inc(acc_done.sem, 1)
                    tile_loop(pe, n, body)
            done(w_loaded0=16 * HALF, w_loaded1=16 * HALF, w_hi=n, w_lo=n, acc_done=n, acc_free=n,
                 own_done=n, tap_done=n, silu_done=HALF, gated=HALF, g_hi=HALF, g_lo=HALF)

        def region(offset, size):
            at_, end = [offset], offset + size

            def take(name, shape):
                o = at_[0]
                at_[0] += (4 * int(np.prod(shape[1:])) + 31) // 32 * 32
                assert at_[0] <= end, (name, at_[0], end)
                return sb(name, shape, offset=o)
            return take

        h1 = region(o_h, 2 * DC * TOK * 4)
        QK = h1("QK", [P, 4, SEQ])
        VT = h1("VT", [P, 4, SEQ])
        AVT = h1("AVT", [P, 4, P])
        EM = h1("EM", [P, SEQ])
        LI, XF, AB, CUM, GG, MX, NM = (h1(n, [P, SEQ]) for n in ("LI", "XF", "AB", "CUM", "GG", "MX", "NM"))
        WT = [h1(f"WT{i}", [P, SEQ]) for i in range(2)]
        PT = [h1(f"PT{i}", [P, SEQ]) for i in range(2)]
        HT = h1("HT", [P, SEQ])
        ONE4 = h1("ONE4", [P, SEQ])
        b1 = region(o_big + N1 * SEQ * 4, (N2 * TOK - N1 * SEQ) * 4)
        CST1 = b1("CST1", [P, C1_N])
        PW = [b1(f"PW{i}", [P, 4, PAIR]) for i in range(2)]
        PTT = [b1(f"PTT{i}", [P, 2 * SEQ]) for i in range(2)]
        GT = SM[:, 0:16]

        def mix1_prepare():
            vt_ps, vt_free, rot_ps, rot_free = S("vt_ps"), S("vt_free"), S("rot_ps"), S("rot_free")
            own_done, conv_done = S("own_done"), S("conv_done")
            rope = [AQ1, AQ1 + 1, AQ1 + 2, AQ1 + 3, AK1]
            with block() as b:
                @b.tensor
                def _(pe):
                    pe.matmul(PS[3][0:4, 0:SEQ], CST1[:, C1_SELF:C1_SELF + 4], Z1[:, GT1, :],
                              start=True, stop=True)
                    for i in range(4):
                        if later(i - 1):
                            pe.wait_ge(vt_free.sem, vt_free.at(i - 1))
                        for c in range(4):
                            ins = pe.transpose(PS[i % 2][:, c * P:c * P + P],
                                               Z1[:, V1 + c, i * P:i * P + P], IDENT)
                        ins.then_inc(vt_ps.sem, 1)
                    for i in range(4):
                        ins = pe.transpose(PS[2][:, i * P:i * P + P], Z1[:, AV1, i * P:i * P + P], IDENT)
                    ins.then_inc(vt_ps.sem, 1)
                    for n, c in enumerate(rope):
                        if later(n - 1):
                            pe.wait_ge(rot_free.sem, rot_free.at(n - 1))
                        pe.matmul(PS[n % 2 + 2][:, SEQ:2 * SEQ], CST1[:, C1_RP:C1_RP + P], Z1[:, c, :],
                                  start=True, stop=True).then_inc(rot_ps.sem, 1)

                @b.scalar
                def _(act):
                    for i in range(4):
                        act.wait_ge(vt_ps.sem, vt_ps.at(i + 1))
                        act.activation(VT[:, i, :], PS[i % 2][:, 0:SEQ], ACT.Copy).then_inc(vt_free.sem, 1)
                    for c in range(4):
                        act.activation(QK[:, c, :], Z1[:, c, :], ACT.Identity,
                                       scale=VEC[:, V1_CW + c * 4 + 3:V1_CW + c * 4 + 4],
                                       bias=VEC[:, V1_CB + c:V1_CB + c + 1]).then_inc(own_done.sem, 1)
                    act.wait_ge(vt_ps.sem, vt_ps.at(5))
                    act.activation(AVT[:].rearrange("p a b -> p (a b)"), PS[2][:, 0:SEQ],
                                   ACT.Copy).then_inc(vt_free.sem, 1)
                    act.activation(Z1[:, O1:O1 + 4, :], Z1[:, O1:O1 + 4, :], ACT.Sigmoid)
                    for c in range(4):
                        act.wait_ge(conv_done.sem, conv_done.at(3 * c + 3))
                        act.activation(QK[:, c, :], QK[:, c, :], ACT.Silu)

                @b.vector
                def _(dve):
                    conv_done, rot_step = S("conv_done"), S("rot_step")
                    for c in range(4):
                        dve.wait_ge(own_done.sem, own_done.at(c + 1))
                        for k in range(3):
                            d = 3 - k
                            dve.scalar_tensor_tensor(
                                out=QK[:, c, d:SEQ], in0=Z1[:, c, 0:SEQ - d],
                                scalar=VEC[:, V1_CW + c * 4 + k:V1_CW + c * 4 + k + 1],
                                in1=QK[:, c, d:SEQ], op0=ALU.mult, op1=ALU.add).then_inc(conv_done.sem, 1)
                            dve.wait_ge(conv_done.sem, conv_done.next())
                    for n, c in enumerate(rope):
                        dve.wait_ge(rot_ps.sem, rot_ps.at(n + 1))
                        dve.tensor_tensor(HT[:], PS[n % 2 + 2][:, SEQ:2 * SEQ],
                                          CST1[:, C1_SIN:C1_SIN + SEQ], ALU.mult).then_inc(rot_free.sem, 1)
                        dve.tensor_tensor(Z1[:, c, :], Z1[:, c, :], CST1[:, C1_COS:C1_COS + SEQ],
                                          ALU.mult).then_inc(rot_step.sem, 1)
                        dve.wait_ge(rot_step.sem, rot_step.next())
                        dve.wait_ge(rot_free.sem, rot_free.at(n + 1))
                        dve.tensor_tensor(Z1[:, c, :], Z1[:, c, :], HT[:], ALU.add).then_inc(rot_step.sem, 1)
                        dve.wait_ge(rot_step.sem, rot_step.next())
            done(vt_ps=5, vt_free=5, rot_ps=5, rot_free=5, own_done=4, conv_done=12, rot_step=10)

        def mix1_gates():
            abs_done, exp_done, ln_done, scans, gt_ps = (S("abs_done"), S("exp_done"), S("ln_done"),
                                                         S("scan_step"), S("gt_ps"))
            with block() as b:
                @b.vector
                def _(dve):
                    scan_step = S("scan_step")
                    dve.tensor_scalar(LI[0:4, :], Z1[0:4, GT1, :], VEC[0:4, V1_GI:V1_GI + 1], None, ALU.add)
                    dve.tensor_scalar(XF[0:4, :], PS[3][0:4, 0:SEQ], VEC[0:4, V1_GF:V1_GF + 1],
                                      None, ALU.add).then_inc(scan_step.sem, 1)
                    dve.wait_ge(scan_step.sem, scan_step.next())
                    dve.memset(ONE4[0:4, :], 1.0).then_inc(scan_step.sem, 1)
                    dve.wait_ge(scan_step.sem, scan_step.next())
                    dve.wait_ge(ln_done.sem, ln_done.at(1))
                    dve.scalar_tensor_tensor(out=XF[0:4, :], in0=XF[0:4, :], scalar=0.0,
                                             in1=AB[0:4, :], op0=ALU.min, op1=ALU.subtract).then_inc(scan_step.sem, 1)
                    dve.wait_ge(scan_step.sem, scan_step.next())
                    dve.tensor_tensor_scan(CUM[0:4, :], ONE4[0:4, :], XF[0:4, :], 0.0,
                                           ALU.mult, ALU.add).then_inc(scan_step.sem, 1)
                    dve.wait_ge(scan_step.sem, scan_step.next())
                    dve.tensor_tensor(GG[0:4, :], LI[0:4, :], CUM[0:4, :], ALU.subtract).then_inc(scan_step.sem, 1)
                    dve.wait_ge(scan_step.sem, scan_step.next())
                    dve.tensor_tensor_scan(MX[0:4, :], GG[0:4, :], GG[0:4, :], 0.0, ALU.max, ALU.max).then_inc(scan_step.sem, 1)
                    dve.wait_ge(scan_step.sem, scan_step.next())
                    dve.scalar_tensor_tensor(out=NM[0:4, :], in0=CUM[0:4, :], scalar=-1.0,
                                             in1=MX[0:4, :], op0=ALU.mult, op1=ALU.subtract).then_inc(scan_step.sem, 1)
                    dve.wait_ge(scan_step.sem, scan_step.next())
                    dve.wait_ge(gt_ps.sem, gt_ps.at(1))
                    dve.tensor_copy(GT, PS[3][:, SEQ:SEQ + 16])

                @b.scalar
                def _(act):
                    act.wait_ge(scans.sem, scans.at(1))
                    act.activation(AB[0:4, :], XF[0:4, :], ACT.Abs).then_inc(abs_done.sem, 1)
                    act.wait_ge(abs_done.sem, abs_done.at(1))
                    act.activation(AB[0:4, :], AB[0:4, :], ACT.Exp, scale=-1.0).then_inc(exp_done.sem, 1)
                    act.wait_ge(exp_done.sem, exp_done.at(1))
                    act.activation(AB[0:4, :], AB[0:4, :], ACT.Ln, bias=ONES[0:4, 0:1]).then_inc(ln_done.sem, 1)

                @b.tensor
                def _(pe):
                    pe.wait_ge(scans.sem, scans.at(5))
                    for i in range(4):
                        ins = pe.transpose(PS[3][:, SEQ + 4 * i:SEQ + 4 * i + 4],
                                           GG[0:4, i * P:i * P + P], IDENT[0:4, 0:4])
                    ins.then_inc(gt_ps.sem, 1)
            done(scan_step=7, abs_done=1, exp_done=1, ln_done=1, gt_ps=1)

        def mlstm():
            names = ("bc_ps", "em_done", "w_exp", "w_done", "s_ps", "p_done", "pv_done", "den_step",
                     "hsq_done", "hms_ps", "hln_done", "hrstd", "head_out")
            bc_ps, em_done, w_exp, w_done, s_ps, p_done, pv_done, den_step, hsq, hms, hln, hrstd, head_out = (
                S(n) for n in names)
            NB = SEQ // P
            with block() as b:
                @b.tensor
                def _(pe):
                    for h in range(4):
                        r = 64 * (h % 2)
                        sel = CST1[0:4, C1_SELH + h * P:C1_SELH + (h + 1) * P]
                        if later(NB * h):
                            pe.wait_ge(w_exp.sem, w_exp.at(NB * h))
                        if later(h):
                            pe.wait_ge(em_done.sem, em_done.at(h))
                        pe.matmul(PS[0][:, 0:SEQ], sel, MX[0:4, :], start=True, stop=True)
                        pe.matmul(PS[0][:, SEQ:], sel, NM[0:4, :], start=True,
                                  stop=True).then_inc(bc_ps.sem, 1)

                        def scores(i):
                            n = NB * h + i
                            if later(n - 1):
                                pe.wait_ge(p_done.sem, p_done.at(n - 1))
                            q = (i % 2) * SEQ
                            pe.matmul(PS[1][:, q:q + SEQ - i * P],
                                      QK[r:r + 64, 2 + h // 2, i * P:i * P + P],
                                      QK[r:r + 64, h // 2, i * P:SEQ], start=True, stop=True
                                      ).then_inc(s_ps.sem, 1)
                        scores(0)
                        for i in range(NB):
                            if i + 1 < NB:
                                scores(i + 1)
                            n = NB * h + i
                            pe.wait_ge(p_done.sem, p_done.at(n + 1))
                            if i == 0:
                                if later(4 * h):
                                    pe.wait_ge(den_step.sem, den_step.at(4 * h))
                            w = PT[i % 2][:, 0:SEQ - i * P]
                            pe.matmul(PS[2][:, i * P:SEQ], VT[:, i, h * P:h * P + P], w,
                                      start=(i == 0), stop=(i == NB - 1))
                            pe.matmul(PS[2][:, SEQ + i * P:], ONES[:], w,
                                      start=(i == 0), stop=(i == NB - 1)).then_inc(pv_done.sem, 1)
                        pe.wait_ge(hsq.sem, hsq.at(h + 1))
                        pe.matmul(PS[3][:, 0:SEQ], MEAN[:],
                                  HSQ, start=True, stop=True).then_inc(hms.sem, 1)

                @b.scalar
                def _(act):
                    for h in range(4):
                        act.wait_ge(bc_ps.sem, bc_ps.at(h + 1))
                        if later(4 * h):
                            act.wait_ge(den_step.sem, den_step.at(4 * h))
                        act.activation(EM[:], PS[0][:, SEQ:], ACT.Exp).then_inc(em_done.sem, 1)
                        for i in range(NB):
                            n = NB * h + i
                            if later(n - 1):
                                act.wait_ge(p_done.sem, p_done.at(n - 1))
                            act.activation(WT[i % 2][:, 0:SEQ - i * P], PS[0][:, i * P:SEQ], ACT.Exp,
                                           scale=-1.0, bias=GT[:, 4 * i + h:4 * i + h + 1]
                                           ).then_inc(w_exp.sem, 1)
                        act.wait_ge(den_step.sem, den_step.at(4 * h + 4))
                        act.activation(HSQ, HT[:], ACT.Square).then_inc(hsq.sem, 1)
                        act.wait_ge(hms.sem, hms.at(h + 1))
                        act.activation(RSTD[:, 0:SEQ], PS[3][:, 0:SEQ], ACT.Ln, scale=float(D // P),
                                       bias=EPSC[:, 0:1]).then_inc(hln.sem, 1)
                        act.wait_ge(hln.sem, hln.at(h + 1))
                        act.activation(RSTD[:, 0:SEQ], RSTD[:, 0:SEQ], ACT.Exp,
                                       scale=-0.5).then_inc(hrstd.sem, 1)

                @b.gpsimd
                def _(pool):
                    for n in range(4 * NB):
                        pool.wait_ge(w_exp.sem, w_exp.at(n + 1))
                        pool.affine_select(out=WT[n % 2][:, 0:P], in_=WT[n % 2][:, 0:P],
                                           compare_op=ALU.is_ge, fill=0.0, base=0, pattern=[[1, P]],
                                           channel_multiplier=-1).then_inc(w_done.sem, 1)

                @b.vector
                def _(dve):
                    den_step = S("den_step")
                    for h in range(4):
                        for i in range(NB):
                            n = NB * h + i
                            dve.wait_ge(s_ps.sem, s_ps.at(n + 1))
                            dve.wait_ge(w_done.sem, w_done.at(n + 1))
                            if later(n - 1):
                                dve.wait_ge(pv_done.sem, pv_done.at(n - 1))
                            q = (i % 2) * SEQ
                            dve.scalar_tensor_tensor(
                                out=PT[i % 2][:, 0:SEQ - i * P], in0=PS[1][:, q:q + SEQ - i * P],
                                scalar=0.125, in1=WT[i % 2][:, 0:SEQ - i * P],
                                op0=ALU.mult, op1=ALU.mult).then_inc(p_done.sem, 1)
                        dve.wait_ge(pv_done.sem, pv_done.at(NB * (h + 1)))
                        dve.wait_ge(em_done.sem, em_done.at(h + 1))
                        if later(h):
                            dve.wait_ge(hsq.sem, hsq.at(h))
                        if later(2 * h):
                            dve.wait_ge(head_out.sem, head_out.at(2 * h))
                        dve.scalar_tensor_tensor(out=DEN, in0=PS[2][:, SEQ:], scalar=-1.0, in1=EM[:],
                                                 op0=ALU.mult, op1=ALU.max).then_inc(den_step.sem, 1)
                        dve.wait_ge(den_step.sem, den_step.next())
                        dve.tensor_tensor(DEN, DEN, PS[2][:, SEQ:], ALU.max).then_inc(den_step.sem, 1)
                        dve.wait_ge(den_step.sem, den_step.next())
                        dve.reciprocal(DEN, DEN).then_inc(den_step.sem, 1)
                        dve.wait_ge(den_step.sem, den_step.next())
                        dve.tensor_tensor(HT[:], PS[2][:, 0:SEQ], DEN, ALU.mult).then_inc(den_step.sem, 1)
                        dve.wait_ge(den_step.sem, den_step.next())
                        dve.wait_ge(hrstd.sem, hrstd.at(h + 1))
                        dve.scalar_tensor_tensor(out=DEN, in0=Z1[:, O1 + h, :],
                                                 scalar=VEC[:, V1_MH + h:V1_MH + h + 1], in1=RSTD[:, 0:SEQ],
                                                 op0=ALU.mult, op1=ALU.mult).then_inc(head_out.sem, 1)
                        dve.wait_ge(head_out.sem, head_out.at(2 * h + 1))
                        dve.tensor_tensor(Z1[:, V1 + h, :], HT[:], DEN,
                                          ALU.mult).then_inc(head_out.sem, 1)
            done(bc_ps=4, em_done=4, w_exp=16, w_done=16, s_ps=16, p_done=16, pv_done=16, den_step=16,
                 hsq_done=4, hms_ps=4, hln_done=4, hrstd=4, head_out=8)

        HSQ, DEN = SQ[0][:, 0:SEQ], SQ[1][:, 0:SEQ]

        def window_attention():
            names = ("s_ps", "masked", "max_step", "exp_done", "sink_exp", "norm_step", "pt_ps",
                     "pt_done", "pv_done", "o_done")
            s_ps, masked, max_step, exp_done, sink_exp, norm_step, pt_ps, pt_done, pv_done, o_done = (
                S(n) for n in names)
            units = [(n, kv) for n in range(4) for kv in range(2)]
            U = len(units)
            MXV = [SM[:, 32 + 16 * i:36 + 16 * i] for i in range(2)]
            SE = [SM[:, 36 + 16 * i:40 + 16 * i] for i in range(2)]
            SUMS = [SM[:, 40 + 16 * i:44 + 16 * i] for i in range(2)]
            with block() as b:
                @b.tensor
                def _(pe):
                    def scores(u):
                        n, kv = units[u]
                        r = 64 * kv
                        if later(u - 1):
                            pe.wait_ge(masked.sem, masked.at(u - 1))
                        for j in range(4):
                            k0 = max(0, n - 1) * P
                            lo = 0 if n else P
                            ins = pe.matmul(PS[u % 2][:, j * PAIR + lo:(j + 1) * PAIR],
                                            Z1[r:r + 64, AQ1 + j, n * P:n * P + P],
                                            Z1[r:r + 64, AK1, k0:(n + 1) * P], start=True, stop=True)
                        ins.then_inc(s_ps.sem, 1)
                    scores(0)
                    for u, (n, kv) in enumerate(units):
                        if u + 1 < U:
                            scores(u + 1)
                        r = 64 * kv
                        pe.wait_ge(norm_step.sem, norm_step.at(3 * u + 3))
                        if later(u):
                            pe.wait_ge(pt_done.sem, pt_done.at(u))
                        blocks = (0, 1) if n else (1,)
                        for m in blocks:
                            for j in range(4):
                                ins = pe.transpose(PS[2][:, m * SEQ + j * P:m * SEQ + j * P + P],
                                                   PW[u % 2][:, j, m * P:m * P + P], IDENT)
                        ins.then_inc(pt_ps.sem, 1)
                        pe.wait_ge(pt_done.sem, pt_done.at(u + 1))
                        if later(u):
                            pe.wait_ge(o_done.sem, o_done.at(u))
                        for m in blocks:
                            ins = pe.matmul(PS[3][r:r + 64, 0:SEQ], AVT[:, n - 1 + m, r:r + 64],
                                            PTT[u % 2][:, m * SEQ:m * SEQ + SEQ],
                                            start=(m == blocks[0]), stop=(m == 1))
                        ins.then_inc(pv_done.sem, 1)

                @b.scalar
                def _(act):
                    for u, (n, kv) in enumerate(units):
                        lo = 0 if n else P
                        act.wait_ge(max_step.sem, max_step.at(4 * u + 4))
                        for j in range(4):
                            ins = act.activation(PW[u % 2][:, j, lo:], PW[u % 2][:, j, lo:], ACT.Exp,
                                                 bias=MXV[u % 2][:, j:j + 1],
                                                 accum_out=SUMS[u % 2][:, j:j + 1])
                        ins.then_inc(exp_done.sem, 1)
                        act.activation(SE[u % 2], SE[u % 2], ACT.Exp).then_inc(sink_exp.sem, 1)
                        act.wait_ge(pt_ps.sem, pt_ps.at(u + 1))
                        if later(u - 1):
                            act.wait_ge(pv_done.sem, pv_done.at(u - 1))
                        b0 = 0 if n else SEQ
                        act.activation(PTT[u % 2][:, b0:], PS[2][:, b0:], ACT.Copy).then_inc(pt_done.sem, 1)

                @b.vector
                def _(dve):
                    max_step, norm_step = S("max_step"), S("norm_step")

                    def masked_max(u):
                        n, kv = units[u]
                        lo = 0 if n else P
                        sink = VEC[:, V1_SINK + 4 * kv:V1_SINK + 4 * kv + 4]
                        dve.wait_ge(s_ps.sem, s_ps.at(u + 1))
                        if later(u - 1):
                            dve.wait_ge(pt_ps.sem, pt_ps.at(u - 1))
                        mask = CST1[:, None, C1_MASK + lo:C1_MASK + PAIR].broadcast_to([P, 4, PAIR - lo])
                        dve.scalar_tensor_tensor(
                            out=PW[u % 2][:, :, lo:],
                            in0=PS[u % 2][:].rearrange("p (j s) -> p j s", j=4)[:, :, lo:],
                            scalar=0.125, in1=mask, op0=ALU.mult, op1=ALU.add).then_inc(masked.sem, 1)
                        dve.wait_ge(masked.sem, masked.at(u + 1))
                        dve.tensor_reduce(MXV[u % 2], PW[u % 2][:, :, lo:], AX.X, ALU.max).then_inc(max_step.sem, 1)
                        dve.wait_ge(max_step.sem, max_step.next())
                        dve.tensor_tensor(MXV[u % 2], MXV[u % 2], sink, ALU.max).then_inc(max_step.sem, 1)
                        dve.wait_ge(max_step.sem, max_step.next())
                        dve.tensor_scalar(MXV[u % 2], MXV[u % 2], -1.0, None, ALU.mult).then_inc(max_step.sem, 1)
                        dve.wait_ge(max_step.sem, max_step.next())
                        dve.tensor_tensor(SE[u % 2], MXV[u % 2], sink, ALU.add).then_inc(max_step.sem, 1)
                        dve.wait_ge(max_step.sem, max_step.next())

                    masked_max(0)
                    for u, (n, kv) in enumerate(units):
                        lo = 0 if n else P
                        if u + 1 < U:
                            masked_max(u + 1)
                        dve.wait_ge(exp_done.sem, exp_done.at(u + 1))
                        dve.wait_ge(sink_exp.sem, sink_exp.at(u + 1))
                        dve.tensor_tensor(SUMS[u % 2], SUMS[u % 2], SE[u % 2], ALU.add).then_inc(norm_step.sem, 1)
                        dve.wait_ge(norm_step.sem, norm_step.next())
                        dve.reciprocal(SUMS[u % 2], SUMS[u % 2]).then_inc(norm_step.sem, 1)
                        dve.wait_ge(norm_step.sem, norm_step.next())
                        dve.tensor_tensor(PW[u % 2][:, :, lo:], PW[u % 2][:, :, lo:],
                                          SUMS[u % 2].unsqueeze(2).broadcast_to([P, 4, PAIR - lo]),
                                          ALU.mult).then_inc(norm_step.sem, 1)
                        dve.wait_ge(norm_step.sem, norm_step.next())
                        dve.wait_ge(pv_done.sem, pv_done.at(u + 1))
                        r = 64 * kv
                        dve.tensor_copy(Z1[r:r + 64, AQ1:AQ1 + 4, n * P:n * P + P],
                                        PS[3][r:r + 64, 0:SEQ].rearrange("p (j q) -> p j q", j=4)
                                        ).then_inc(o_done.sem, 1)
            done(s_ps=U, masked=U, max_step=4 * U, exp_done=U, sink_exp=U, norm_step=3 * U, pt_ps=U,
                 pt_done=U, pv_done=U, o_done=U)

        def silu_conditions():
            with block() as b:
                @b.scalar
                def _(act):
                    act.activation(SC[:], CC[:], ACT.Silu)

        def modulation(weights, first):
            n = 48
            loaded = [S("w_loaded0"), S("w_loaded1")]
            acc_done, acc_free = S("acc_done"), S("acc_free")
            with block() as b:
                @b.sync
                def _(sp):
                    def body(t, s):
                        if later(t - 1):
                            sp.wait_ge(acc_done.sem, acc_done.at(t - 1))
                        src = weights[at(t + first)].rearrange("a p n -> p (a n)")
                        sp.dma_start(STAGE[s][:, 0:DC * P], src).then_inc(loaded[s].sem, 16)
                    tile_loop(sp, n, body, tail=0)

                @b.tensor
                def _(pe):
                    def body(t, s):
                        pe.wait_ge(loaded[s].sem, loaded[s].at((t - s) * 8 + 16))
                        if later(t - 1):
                            pe.wait_ge(acc_free.sem, acc_free.at(t - 1))
                        for k in range(DC):
                            ins = pe.matmul(PS[s][:, 0:2], STAGE[s][:, k * P:k * P + P], SC[:, k, :],
                                            start=(k == 0), stop=(k == DC - 1))
                        ins.then_inc(acc_done.sem, 1)
                    tile_loop(pe, n, body, tail=0)

                @b.vector
                def _(dve):
                    def body(t, s):
                        dve.wait_ge(acc_done.sem, acc_done.at(t + 1))
                        dve.tensor_scalar(MOD[:, at(t), :].rearrange("p a c -> p (a c)"), PS[s][:, 0:2],
                                          VEC[:, at(t + V2_BM)], None, ALU.add).then_inc(acc_free.sem, 1)
                    tile_loop(dve, n, body, tail=0)
            done(w_loaded0=16 * n // 2, w_loaded1=16 * n // 2, acc_done=n, acc_free=n)
            with block() as b:
                @b.vector
                def _(dve):
                    for dst, scale, gain in ((A1, 1, V2_N1), (A2, 4, V2_N2)):
                        dve.scalar_tensor_tensor(
                            out=dst[:], in0=MOD[:, scale * DC:(scale + 1) * DC, :], scalar=1.0,
                            in1=VEC[:, gain:gain + DC].unsqueeze(2).broadcast_to([P, DC, 2]),
                            op0=ALU.add, op1=ALU.mult)

        PADX, PADC, PADN = 8, SEQ + 24, TOK + 32
        h2 = region(o_h, 2 * DC * TOK * 4)
        PP = [h2(f"PP{i}", [P, 2, PADN]) for i in range(5)]
        INV = h2("INV", [P, 2, TOK])
        PU = h2("PU", [P, 2, TOK])
        PWM = h2("PWM", [P, 2, P])

        def pooling(tokens):
            pads, copied, psum, y_ps, o_done = (S("pads"), S("copied"), S("pool_step"), S("y_ps"), S("o_done"))
            rs = ranges(tokens)
            with block() as b:
                @b.gpsimd
                def _(pool):
                    pool.memset(PP[0][:], 0.0).then_inc(pads.sem, 1)

                @b.scalar
                def _(act):
                    act.wait_ge(pads.sem, pads.at(1))
                    act.activation(PP[0][:, :, PADX:PADX + SEQ], Z[:, PO:PO + 2, 0:SEQ], ACT.Copy)
                    if tokens == TOK:
                        act.activation(PP[0][:, :, PADC:PADC + CTX], Z[:, PO:PO + 2, SEQ:TOK], ACT.Copy)
                    act.activation(ZERO[:], ZERO[:], ACT.Copy).then_inc(copied.sem, 1)
                    act.wait_ge(y_ps.sem, y_ps.at(2))
                    for c in range(2):
                        for t0, tn in rs:
                            act.activation(Z[:, PO + c, t0:t0 + tn], PS[c][:, t0:t0 + tn], ACT.Copy,
                                           scale=VEC[:, V2_PS + c:V2_PS + c + 1])

                @b.vector
                def _(dve):
                    pool_step = S("pool_step")
                    dve.wait_ge(copied.sem, copied.at(1))
                    N = PADN
                    dve.tensor_tensor(PP[1][:, :, 1:N], PP[0][:, :, 0:N - 1], PP[0][:, :, 1:N], ALU.add).then_inc(pool_step.sem, 1)
                    dve.wait_ge(pool_step.sem, pool_step.next())
                    for i, d in ((2, 1), (3, 2), (4, 4)):
                        dve.tensor_tensor(PP[i][:, :, 2 * d:N - 2 * d + 1], PP[i - 1][:, :, d:N - 3 * d + 1],
                                          PP[i - 1][:, :, 3 * d:N - d + 1], ALU.add).then_inc(pool_step.sem, 1)
                        dve.wait_ge(pool_step.sem, pool_step.next())
                    for c in range(2):
                        for half in range(2):
                            r = 64 * half
                            for t0, tn in rs:
                                p0 = PADX if t0 == 0 else PADC
                                dve.tensor_tensor(PU[r:r + 64, c, t0:t0 + tn],
                                                  PP[1 + 2 * c + half][r:r + 64, c, p0:p0 + tn],
                                                  INV[r:r + 64, c, t0:t0 + tn], ALU.mult).then_inc(pool_step.sem, 1)
                                dve.wait_ge(pool_step.sem, pool_step.next())
                    for c in range(2):
                        dve.tensor_tensor(PU[:, c, 0:tokens], PU[:, c, 0:tokens],
                                          Z[:, PO + c, 0:tokens], ALU.subtract).then_inc(pool_step.sem, 1)
                        dve.wait_ge(pool_step.sem, pool_step.next())

                @b.tensor
                def _(pe):
                    pe.wait_ge(psum.sem, psum.at(4 + 4 * len(rs) + 2))
                    for c in range(2):
                        for t0, tn in rs:
                            ins = pe.matmul(PS[c][:, t0:t0 + tn], PWM[:, c, :], PU[:, c, t0:t0 + tn],
                                            start=True, stop=True)
                        ins.then_inc(y_ps.sem, 1)
            done(pads=1, copied=1, pool_step=4 + 4 * len(rs) + 2, y_ps=2)

        h3 = region(o_h, 2 * DC * TOK * 4)
        VTN = h3("VTN", [P, 10, 3 * P])
        BM = [h3(f"BM{i}", [P, 4 * PAIR]) for i in range(2)]
        CNM = h3("CNM", [P, 4 * PAIR])
        PN = [h3(f"PN{i}", [P, SEQ]) for i in range(2)]
        QP = h3("QP", [P, 3, TOK])
        PTN = [h3(f"PTN{i}", [P, SEQ]) for i in range(2)]

        def grid(z, rows, c0, cn):
            return z.rearrange("p (r g) -> p r g", g=GRID)[:, rows[0]:rows[1], c0:c0 + cn]

        def neighborhood(bias, layer, tokens):
            vt_ps, vt_free, vg_done = S("vt_ps"), S("vt_free"), S("vg_done")
            VG = [SQ[i][:].rearrange("p (c r g) -> p c r g", c=3, r=8) for i in range(2)]
            with block() as b:
                @b.scalar
                def _(act):
                    def gather(k):
                        if later(2 * k - 2):
                            act.wait_ge(vt_ps.sem, vt_ps.at(2 * k - 2))
                        for c in range(3):
                            ins = act.activation(VG[k % 2][:, c], grid(Z[:, NV + c, 0:SEQ], (0, 8), COL0[k], SPAN),
                                                 ACT.Copy)
                        ins.then_inc(vg_done.sem, 1)
                    gather(0)
                    gather(1)
                    for g in range(10):
                        act.wait_ge(vt_ps.sem, vt_ps.at(g + 1))
                        act.activation(VTN[:, g, :], PS[g % 2][:, 0:3 * P], ACT.Copy).then_inc(vt_free.sem, 1)
                        if g % 2 and g // 2 + 2 < 4:
                            gather(g // 2 + 2)
                    for c in range(3):
                        for k in range(4):
                            act.activation(QP[:, c, k * P:k * P + P].rearrange("p (r g) -> p r g", r=8),
                                           grid(Z[:, NQ + c, 0:SEQ], (0, 8), 16 * k, 16), ACT.Copy, scale=0.125)
                    if tokens == TOK:
                        act.activation(QP[:, :, SEQ:TOK], Z[:, NQ:NQ + 3, SEQ:TOK], ACT.Copy, scale=0.125)

                @b.tensor
                def _(pe):
                    for g in range(10):
                        if later(g - 1):
                            pe.wait_ge(vt_free.sem, vt_free.at(g - 1))
                        pe.wait_ge(vg_done.sem, vg_done.at(min(g // 2 + 1, 4)))
                        for c in range(3):
                            if g < 8:
                                src = SQ[g // 2 % 2][:, c * PAIR + (g % 2) * P:c * PAIR + (g % 2) * P + P]
                            else:
                                src = Z[:, NV + c, SEQ + (g - 8) * P:SEQ + (g - 7) * P]
                            ins = pe.transpose(PS[g % 2][:, c * P:c * P + P], src, IDENT)
                        ins.then_inc(vt_ps.sem, 1)
            done(vt_ps=10, vt_free=10, vg_done=4)

            kinds = 4 if tokens == SEQ else 6
            units = [(h, k) for h in range(NA_H) for k in range(kinds)]
            U = len(units)
            names = ("s_ps", "masked", "max_step", "exp_done", "norm_step", "pt_ps", "pt_done",
                     "pv_done", "o_done", "bias_done")
            s_ps, masked, max_step, exp_done, norm_step, pt_ps, pt_done, pv_done, o_done, bias_done = (
                S(n) for n in names)
            bias_in = [S("bias_in0"), S("bias_in1")]
            NMX = [SM[:, 32 + 16 * i:33 + 16 * i] for i in range(2)]
            SUMS = [SM[:, 40 + 16 * i:41 + 16 * i] for i in range(2)]
            local = lambda k: k < 4
            with block() as b:
                @b.sync
                def _(sp):
                    for h in range(NA_H):
                        if later(4 * (h - 1)):
                            sp.wait_ge(masked.sem, masked.at(4 * (h - 1)))
                        sp.dma_start(BM[h % 2][:], bias[layer * NA_H + h]).then_inc(bias_in[h % 2].sem, 16)

                @b.gpsimd
                def _(pool):
                    for h in range(NA_H):
                        pool.wait_ge(bias_in[h % 2].sem, bias_in[h % 2].at(16 * (h // 2 + 1)))
                        pool.tensor_tensor(BM[h % 2][:], BM[h % 2][:], CNM[:], ALU.add).then_inc(bias_done.sem, 1)

                @b.tensor
                def _(pe):
                    def scores(u):
                        h, k = units[u]
                        r = 64 * (h % 2)
                        if later(u - 1):
                            pe.wait_ge(exp_done.sem, exp_done.at(u - 1))
                        if local(k):
                            q = QP[r:r + 64, h // 2, k * P:k * P + P]
                            pe.matmul(PS[u % 2][:, 0:PAIR].rearrange("p (a b) -> p a b", b=SPAN), q,
                                      grid(Z[r:r + 64, NK + h // 2, 0:SEQ], (0, 8), COL0[k], SPAN),
                                      start=True, stop=True)
                        else:
                            q = QP[r:r + 64, h // 2, SEQ + (k - 4) * P:SEQ + (k - 3) * P]
                        pe.matmul(PS[u % 2][:, PAIR:SEQ], q, Z[r:r + 64, NK + h // 2, SEQ:TOK],
                                  start=True, stop=True).then_inc(s_ps.sem, 1)
                    scores(0)
                    for u, (h, k) in enumerate(units):
                        if u + 1 < U:
                            scores(u + 1)
                        r = 64 * (h % 2)
                        pe.wait_ge(norm_step.sem, norm_step.at(2 * u + 2))
                        if later(u):
                            pe.wait_ge(pt_done.sem, pt_done.at(u))
                        blocks = range(4) if local(k) else (2, 3)
                        for m in blocks:
                            ins = pe.transpose(PS[2][:, m * P:m * P + P], PN[u % 2][:, m * P:m * P + P], IDENT)
                        ins.then_inc(pt_ps.sem, 1)
                        pe.wait_ge(pt_done.sem, pt_done.at(u + 1))
                        if later(u):
                            pe.wait_ge(o_done.sem, o_done.at(u))
                        for m in blocks:
                            g = 2 * k + m if m < 2 else 6 + m
                            ins = pe.matmul(PS[3][r:r + 64, 0:P], VTN[:, g, h * 64:h * 64 + 64],
                                            PTN[u % 2][:, m * P:m * P + P],
                                            start=(m == blocks[0]), stop=(m == 3))
                        ins.then_inc(pv_done.sem, 1)

                @b.scalar
                def _(act):
                    for u, (h, k) in enumerate(units):
                        lo = 0 if local(k) else PAIR
                        act.wait_ge(max_step.sem, max_step.at(u + 1))
                        if later(u - 1):
                            act.wait_ge(pt_ps.sem, pt_ps.at(u - 1))
                        act.activation(PN[u % 2][:, lo:], PS[u % 2][:, lo:SEQ], ACT.Exp, bias=NMX[u % 2],
                                       accum_out=SUMS[u % 2]).then_inc(exp_done.sem, 1)
                        act.wait_ge(pt_ps.sem, pt_ps.at(u + 1))
                        if later(u - 1):
                            act.wait_ge(pv_done.sem, pv_done.at(u - 1))
                        act.activation(PTN[u % 2][:, lo:], PS[2][:, lo:SEQ], ACT.Copy).then_inc(pt_done.sem, 1)

                @b.vector
                def _(dve):
                    norm_step = S("norm_step")
                    n_masked = [0]

                    def masked_max(u):
                        h, k = units[u]
                        lo = 0 if local(k) else PAIR
                        dve.wait_ge(s_ps.sem, s_ps.at(u + 1))
                        if local(k):
                            dve.wait_ge(bias_done.sem, bias_done.at(h + 1))
                            dve.tensor_tensor(PS[u % 2][:, 0:PAIR], PS[u % 2][:, 0:PAIR],
                                              BM[h % 2][:, k * PAIR:k * PAIR + PAIR],
                                              ALU.add).then_inc(masked.sem, 1)
                            n_masked[0] += 1
                            if later(n_masked[0]):
                                dve.wait_ge(masked.sem, masked.at(n_masked[0]))
                        if later(u - 1):
                            dve.wait_ge(exp_done.sem, exp_done.at(u - 1))
                        dve.tensor_reduce(NMX[u % 2], PS[u % 2][:, lo:SEQ], AX.X, ALU.max,
                                          negate=True).then_inc(max_step.sem, 1)

                    masked_max(0)
                    for u, (h, k) in enumerate(units):
                        if u + 1 < U:
                            masked_max(u + 1)
                        lo = 0 if local(k) else PAIR
                        dve.wait_ge(exp_done.sem, exp_done.at(u + 1))
                        dve.reciprocal(SUMS[u % 2], SUMS[u % 2]).then_inc(norm_step.sem, 1)
                        dve.wait_ge(norm_step.sem, norm_step.next())
                        dve.tensor_scalar(PN[u % 2][:, lo:], PN[u % 2][:, lo:], SUMS[u % 2], None, ALU.mult).then_inc(norm_step.sem, 1)
                        dve.wait_ge(norm_step.sem, norm_step.next())
                        dve.wait_ge(pv_done.sem, pv_done.at(u + 1))
                        r = 64 * (h % 2)
                        if local(k):
                            dst = grid(Z[r:r + 64, NQ + h // 2, 0:SEQ], (0, 8), 16 * k, 16)
                            src = PS[3][r:r + 64, 0:P].rearrange("p (r c) -> p r c", c=16)
                        else:
                            dst = Z[r:r + 64, NQ + h // 2, SEQ + (k - 4) * P:SEQ + (k - 3) * P]
                            src = PS[3][r:r + 64, 0:P]
                        dve.tensor_copy(dst, src).then_inc(o_done.sem, 1)
            done(s_ps=U, masked=24, max_step=U, exp_done=U, norm_step=2 * U, pt_ps=U, pt_done=U,
                 pv_done=U, o_done=U, bias_done=NA_H, bias_in0=48, bias_in1=48)

        h4 = region(o_h, 2 * DC * TOK * 4)
        VR = h4("VR", [P, 6, 3 * P])
        KR = h4("KR", [P, 2, 3 * P])
        CR = h4("CR", [P, CR_N])
        STRIP = h4("STRIP", [P, 7 * P])
        BACK = h4("BACK", [P, P])
        QD = h4("QD", [P, 2, SEQ])
        KD = h4("KD", [P, 4, 64])
        ST = h4("ST", [P, 2, 64])
        PR = [h4(f"PR{i}", [P, SEQ]) for i in range(2)]
        ROT = h4("ROT", [P, SEQ])
        KDEC = SM[:, 80:84]

        def retention(tokens):
            rot_ps, rot_free, vt_ps, vt_free = S("rot_ps"), S("rot_free"), S("vt_ps"), S("vt_free")
            rope = [RQ, RQ + 1, RQ + 2, RK, RK + 1, RK + 2]
            jobs = [(VR[:, g, :], RV, g * P) for g in range(6)] + [(KR[:, g, :], RK, SEQ + g * P) for g in range(2)]
            with block() as b:
                @b.tensor
                def _(pe):
                    for n, c in enumerate(rope):
                        if later(n - 1):
                            pe.wait_ge(rot_free.sem, rot_free.at(n - 1))
                        pe.matmul(PS[n % 2 + 2][:, 0:SEQ], RROT, Z[:, c, 0:SEQ],
                                  start=True, stop=True).then_inc(rot_ps.sem, 1)
                    for g, (_, chunk, t0) in enumerate(jobs):
                        if later(g - 1):
                            pe.wait_ge(vt_free.sem, vt_free.at(g - 1))
                        for c in range(3):
                            ins = pe.transpose(PS[g % 2][:, c * P:c * P + P], Z[:, chunk + c, t0:t0 + P], IDENT)
                        ins.then_inc(vt_ps.sem, 1)

                @b.scalar
                def _(act):
                    for g, (dst, _, _) in enumerate(jobs):
                        act.wait_ge(vt_ps.sem, vt_ps.at(g + 1))
                        act.activation(dst, PS[g % 2][:, 0:3 * P], ACT.Copy).then_inc(vt_free.sem, 1)

                @b.vector
                def _(dve):
                    rot_step = S("rot_step")
                    for n, c in enumerate(rope):
                        dve.wait_ge(rot_ps.sem, rot_ps.at(n + 1))
                        dve.tensor_tensor(ROT[:], PS[n % 2 + 2][:, 0:SEQ], CR[:, CR_SIN:CR_SIN + SEQ],
                                          ALU.mult).then_inc(rot_free.sem, 1)
                        dve.tensor_tensor(Z[:, c, 0:SEQ], Z[:, c, 0:SEQ], CR[:, CR_COS:CR_COS + SEQ],
                                          ALU.mult).then_inc(rot_step.sem, 1)
                        dve.wait_ge(rot_step.sem, rot_step.next())
                        dve.wait_ge(rot_free.sem, rot_free.at(n + 1))
                        dve.tensor_tensor(Z[:, c, 0:SEQ], Z[:, c, 0:SEQ], ROT[:], ALU.add).then_inc(rot_step.sem, 1)
                        dve.wait_ge(rot_step.sem, rot_step.next())
            done(rot_ps=6, rot_free=6, vt_ps=8, vt_free=8, rot_step=12)

            NB = SEQ // P
            per = NB + (2 if tokens == TOK else 0)
            names = ("decay_exp", "decay_step", "st_ps", "s_ps", "p_done", "pv_done", "y_done", "yc_done")
            decay_exp, decay_step, st_ps, s_ps, p_done, pv_done, y_done, yc_done = (S(n) for n in names)
            DSTEPS = 3 + 4 + 2 + 1 + 1
            with block() as b:
                @b.scalar
                def _(act):
                    for h in range(RET_H):
                        lf, lb = VEC[:, V2_LF + h:V2_LF + h + 1], VEC[:, V2_LB + h:V2_LB + h + 1]
                        if later(per * h):
                            act.wait_ge(p_done.sem, p_done.at(per * h))
                        if later(h):
                            act.wait_ge(y_done.sem, y_done.at(h))
                        act.activation(STRIP[:, 3 * P:], CR[:, CR_DP:CR_DP + SEQ], ACT.Exp, scale=lf)
                        act.activation(STRIP[:, 0:3 * P], CR[:, CR_DN:CR_DN + 3 * P], ACT.Exp, scale=lb)
                        act.activation(BACK[:], CR[:, CR_DN + 3 * P:CR_DN + SEQ], ACT.Exp, scale=lb)
                        act.activation(QD[:, 0, :], CR[:, CR_QF:CR_QF + SEQ], ACT.Exp, scale=lf)
                        act.activation(QD[:, 1, :], CR[:, CR_QB:CR_QB + SEQ], ACT.Exp, scale=lb)
                        act.activation(KDEC[:, 0:2], CR[:, CR_KE:CR_KE + 2], ACT.Exp, scale=lf)
                        act.activation(KDEC[:, 2:4], CR[:, CR_KE + 2:CR_KE + 4], ACT.Exp,
                                       scale=lb).then_inc(decay_exp.sem, 1)

                @b.tensor
                def _(pe):
                    for h in range(RET_H):
                        r, c = 64 * (h % 2), h // 2
                        pe.wait_ge(decay_step.sem, decay_step.at(DSTEPS * h + 9))
                        for d in range(2):
                            for g in range(2):
                                ins = pe.matmul(PS[3][r:r + 64, SEQ + 64 * d:SEQ + 64 * d + 64],
                                                KD[:, 2 * d + g, :], VR[:, NB + g, h * 64:h * 64 + 64],
                                                start=(g == 0), stop=(g == 1))
                        ins.then_inc(st_ps.sem, 1)

                        def scores(i):
                            n = per * h + i
                            if later(n - 1):
                                pe.wait_ge(p_done.sem, p_done.at(n - 1))
                            t0, tn, kb = (0, SEQ, i) if i < NB else (SEQ, CTX, i - NB)
                            pe.matmul(PS[n % 2][:, 0:tn], Z[r:r + 64, RK + c, t0 + kb * P:t0 + kb * P + P],
                                      Z[r:r + 64, RQ + c, t0:t0 + tn], start=True, stop=True
                                      ).then_inc(s_ps.sem, 1)
                        scores(0)
                        pe.wait_ge(decay_step.sem, decay_step.at(DSTEPS * (h + 1)))
                        if later(h):
                            pe.wait_ge(y_done.sem, y_done.at(h))
                        for d in range(2):
                            pe.matmul(PS[2][r:r + 64, 0:SEQ], ST[r:r + 64, d, :], QD[r:r + 64, d, :],
                                      start=(d == 0), stop=False)
                        for i in range(per):
                            if i + 1 < per:
                                scores(i + 1)
                            n = per * h + i
                            pe.wait_ge(p_done.sem, p_done.at(n + 1))
                            if i < NB:
                                dst, tn, kb = PS[2][r:r + 64, 0:SEQ], SEQ, i
                            else:
                                dst, tn, kb = PS[2][r:r + 64, SEQ:SEQ + CTX], CTX, i
                            pe.matmul(dst, VR[:, kb, h * 64:h * 64 + 64], PR[n % 2][:, 0:tn],
                                      start=(i == NB), stop=(i == NB - 1 or i == per - 1)
                                      ).then_inc(pv_done.sem, 1)

                @b.vector
                def _(dve):
                    decay_step = S("decay_step")
                    for h in range(RET_H):
                        r, c = 64 * (h % 2), h // 2
                        dve.wait_ge(decay_exp.sem, decay_exp.at(h + 1))
                        mid = STRIP[:, 3 * P:4 * P]
                        dve.tensor_tensor(mid, mid, CR[:, CR_MF:CR_MF + P], ALU.mult).then_inc(decay_step.sem, 1)
                        dve.wait_ge(decay_step.sem, decay_step.next())
                        dve.tensor_tensor(BACK[:], BACK[:], CR[:, CR_MB:CR_MB + P], ALU.mult).then_inc(decay_step.sem, 1)
                        dve.wait_ge(decay_step.sem, decay_step.next())
                        dve.tensor_tensor(mid, mid, BACK[:], ALU.add).then_inc(decay_step.sem, 1)
                        dve.wait_ge(decay_step.sem, decay_step.next())
                        for d in range(2):
                            for g in range(2):
                                dve.tensor_scalar(KD[:, 2 * d + g, :], KR[:, g, h * 64:h * 64 + 64],
                                                  KDEC[:, 2 * d + g:2 * d + g + 1], 0.125,
                                                  ALU.mult, ALU.mult).then_inc(decay_step.sem, 1)
                                dve.wait_ge(decay_step.sem, decay_step.next())
                        for d in range(2):
                            dve.tensor_tensor(QD[r:r + 64, d, :], QD[r:r + 64, d, :],
                                              Z[r:r + 64, RQ + c, 0:SEQ], ALU.mult).then_inc(decay_step.sem, 1)
                            dve.wait_ge(decay_step.sem, decay_step.next())
                        dve.wait_ge(st_ps.sem, st_ps.at(h + 1))
                        for d in range(2):
                            dve.tensor_copy(ST[r:r + 64, d, :], PS[3][r:r + 64, SEQ + 64 * d:SEQ + 64 * d + 64]).then_inc(decay_step.sem, 1)
                            dve.wait_ge(decay_step.sem, decay_step.next())
                        for i in range(per):
                            n = per * h + i
                            dve.wait_ge(s_ps.sem, s_ps.at(n + 1))
                            if later(n - 1):
                                dve.wait_ge(pv_done.sem, pv_done.at(n - 1))
                            tn, kb = (SEQ, i) if i < NB else (CTX, i - NB)
                            dve.scalar_tensor_tensor(out=PR[n % 2][:, 0:tn], in0=PS[n % 2][:, 0:tn], scalar=0.125,
                                                     in1=STRIP[:, (3 - kb) * P:(3 - kb) * P + tn],
                                                     op0=ALU.mult, op1=ALU.mult).then_inc(p_done.sem, 1)
                        dve.wait_ge(pv_done.sem, pv_done.at(per * (h + 1)))
                        if tokens == TOK:
                            dve.tensor_copy(Z[r:r + 64, RQ + c, SEQ:TOK], PS[2][r:r + 64, SEQ:SEQ + CTX])
                        dve.tensor_copy(Z[r:r + 64, RQ + c, 0:SEQ], PS[2][r:r + 64, 0:SEQ]).then_inc(y_done.sem, 1)
            U = per * RET_H
            done(decay_exp=RET_H, decay_step=DSTEPS * RET_H, st_ps=RET_H, s_ps=U, p_done=U, pv_done=U, y_done=RET_H)

            mean_ps, centred, sq_done, var_ps, ln_done, rstd, out_step = (
                S("mean_ps"), S("centred"), S("sq_done"), S("ms_done"), S("log_done"), S("rstd_done"), S("out_step"))
            rs = ranges(tokens)
            with block() as b:
                @b.tensor
                def _(pe):
                    for c in range(3):
                        for t0, tn in rs:
                            ins = pe.matmul(PS[0][:, t0:t0 + tn], BLK, Z[:, RQ + c, t0:t0 + tn], start=True, stop=True)
                        ins.then_inc(mean_ps.sem, 1)
                        pe.wait_ge(sq_done.sem, sq_done.at(c + 1))
                        for t0, tn in rs:
                            ins = pe.matmul(PS[1][:, t0:t0 + tn], BLK, SQ[0][:, t0:t0 + tn], start=True, stop=True)
                        ins.then_inc(var_ps.sem, 1)

                @b.scalar
                def _(act):
                    act.activation(Z[:, RG:RG + 3, 0:tokens], Z[:, RG:RG + 3, 0:tokens], ACT.Silu)
                    for c in range(3):
                        act.wait_ge(centred.sem, centred.at(c + 1))
                        act.activation(SQ[0][:, 0:tokens], Z[:, RQ + c, 0:tokens], ACT.Square).then_inc(sq_done.sem, 1)
                        act.wait_ge(var_ps.sem, var_ps.at(c + 1))
                        act.activation(RSTD[:, 0:tokens], PS[1][:, 0:tokens], ACT.Ln,
                                       bias=EPSC[:, 0:1]).then_inc(ln_done.sem, 1)
                        act.wait_ge(ln_done.sem, ln_done.at(c + 1))
                        act.activation(RSTD[:, 0:tokens], RSTD[:, 0:tokens], ACT.Exp, scale=-0.5).then_inc(rstd.sem, 1)

                @b.vector
                def _(dve):
                    out_step = S("out_step")
                    for c in range(3):
                        dve.wait_ge(mean_ps.sem, mean_ps.at(c + 1))
                        dve.tensor_tensor(Z[:, RQ + c, 0:tokens], Z[:, RQ + c, 0:tokens], PS[0][:, 0:tokens],
                                          ALU.subtract).then_inc(centred.sem, 1)
                        dve.wait_ge(rstd.sem, rstd.at(c + 1))
                        dve.scalar_tensor_tensor(out=Z[:, RQ + c, 0:tokens], in0=Z[:, RQ + c, 0:tokens],
                                                 scalar=VEC[:, V2_GN + c:V2_GN + c + 1],
                                                 in1=RSTD[:, 0:tokens], op0=ALU.mult, op1=ALU.mult).then_inc(out_step.sem, 1)
                        dve.wait_ge(out_step.sem, out_step.next())
                        dve.tensor_tensor(Z[:, RG + c, 0:tokens], Z[:, RG + c, 0:tokens],
                                          Z[:, RQ + c, 0:tokens], ALU.mult).then_inc(out_step.sem, 1)
                        dve.wait_ge(out_step.sem, out_step.next())
            done(mean_ps=3, centred=3, sq_done=3, ms_done=3, log_done=3, rstd_done=3, out_step=6)

        with block() as b:
            @b.gpsimd
            def _(pool):
                filled = S("filled")
                pool.memset(ONES[:], 1.0).then_inc(filled.sem, 1)
                pool.wait_ge(filled.sem, filled.next())
                pool.memset(MEAN[:], 1.0 / D).then_inc(filled.sem, 1)
                pool.wait_ge(filled.sem, filled.next())
                pool.memset(EPSC[:], EPS).then_inc(filled.sem, 1)
                pool.wait_ge(filled.sem, filled.next())
                pool.memset(ZERO[:], 0.0).then_inc(filled.sem, 1)
                pool.wait_ge(filled.sem, filled.next())
        load([(CS[:], a["consts"]), (X[:, :, 0:SEQ], a["x"]), (X[:, :, SEQ:TOK], a["ctx"]), (CC[:], a["cond"])])

        def zero(c, st):
            return ZERO[:, 0:1]

        def store(z, tokens=SEQ, first=0):
            def put(act, t, acc):
                return act.activation(z[:, at(t + first), 0:tokens].rearrange("p a t -> p (a t)"),
                                      acc[:, 0:tokens], ACT.Copy)
            return put

        def to_y(dve, t, acc):
            return dve.tensor_copy(Y[:, at(t), :].rearrange("p a t -> p (a t)"), acc[:, 0:SEQ])

        def add_y(dve, t, acc):
            y = Y[:, at(t), :].rearrange("p a t -> p (a t)")
            return dve.tensor_tensor(y, y, acc[:, 0:SEQ], ALU.add)

        def column(first):
            return lambda c, st=0: VEC[:, first + c:first + c + 1]

        for l in range(DEPTH):
            load([(VEC[:, 0:V1_N], a["vec1"][l]), (CST1[:], a["const1"])])
            pre_norm(column(V1_PRE), zero, SEQ)
            gemm(a["w_in"], l * N1, N1, DC, HH, HL, SEQ, out_act=store(Z1))
            mix1_prepare()
            mix1_gates()
            mlstm()
            window_attention()
            split_rows(Z1, [V1, V1 + 1, V1 + 2, V1 + 3, AQ1, AQ1 + 1, AQ1 + 2, AQ1 + 3], SEQ)
            gemm(a["w_out"], l * DC, DC, DC, HH, HL, SEQ, out_dve=to_y)
            add_normed(Y, column(V1_POST))
            pre_norm(column(V1_PREF), zero, SEQ)
            for half in range(2):
                ffn_up(a["w_up"], (2 * l + half) * 2 * HALF, GH1, GL1, SEQ,
                       (2, ((1, 1), (0, 2))), V1_FCW, None, half)
                gemm(a["w_down"], (2 * l + half) * DC, DC, HALF, GH1, GL1, SEQ,
                     out_dve=add_y if half else to_y)
            add_normed(Y, column(V1_POSTF))

        silu_conditions()
        for l in range(DEPTH):
            tokens = TOK if l < DEPTH - 1 else SEQ
            load([(VEC[:, 0:V2_N], a["vec2"][l])])
            modulation(a["w_mod"], l * 48)

            def mod(which):
                return lambda c, st: MOD[:, at(c + which * DC), st]

            def gated(which):
                def put(dve, t, acc):
                    for st, (t0, tn) in enumerate(ranges(tokens)):
                        x = X[:, at(t), t0:t0 + tn].rearrange("p a t -> p (a t)")
                        ins = dve.scalar_tensor_tensor(out=x, in0=acc[:, t0:t0 + tn], scalar=mod(which)(t, st),
                                                       in1=x, op0=ALU.mult, op1=ALU.add)
                    return ins
                return put

            pre_norm(lambda c, st: A1[:, c, st:st + 1], mod(0), TOK)
            gemm(a["w_in2"], l * N2, N2_KV, DC, HH, HL, TOK, out_act=store(Z, TOK))
            gemm(a["w_in2"], l * N2 + N2_KV, N2 - N2_KV, DC, HH, HL, tokens, out_act=store(Z, tokens, N2_KV))
            load([(INV[:], a["const_pool"]), (PWM[:], a["pool_w"][l])])
            pooling(tokens)
            load([(CNM[:], a["const_na"])])
            neighborhood(a["na_bias"], l, tokens)
            load([(CR[:], a["const_ret"])])
            retention(tokens)
            split_rows(Z, [PO, PO + 1, NQ, NQ + 1, NQ + 2, RG, RG + 1, RG + 2], tokens)
            gemm(a["w_out2"], l * DC, DC, DC, HH, HL, tokens, out_dve=gated(2))
            pre_norm(lambda c, st: A2[:, c, st:st + 1], mod(3), tokens)
            for half in range(2):
                ffn_up(a["w_up2"], (2 * l + half) * 2 * HALF, GH, GL, tokens,
                       (1, ((0, 1), (2, -1))), V2_CW, V2_CB, half)
                gemm(a["w_down2"], (2 * l + half) * DC, DC, HALF, GH, GL, tokens, out_dve=gated(5))

        load([(VEC[:, 0:DC], a["final"])])
        fin, out_stored = S("t_done"), S("out_stored")
        rstd = S("rstd_done")
        with block() as b:
            @b.tensor
            def _(pe):
                statistics(None, None, pe, X, SEQ, "pe")

            @b.scalar
            def _(act):
                statistics(act, None, None, X, SEQ, "act")

            @b.vector
            def _(dve):
                statistics(None, dve, None, X, SEQ, "dve")
                dve.wait_ge(rstd.sem, rstd.at(1))
                for c in range(DC):
                    dve.scalar_tensor_tensor(out=X[:, c, 0:SEQ], in0=X[:, c, 0:SEQ], scalar=VEC[:, c:c + 1],
                                             in1=RSTD[:, 0:SEQ], op0=ALU.mult, op1=ALU.mult).then_inc(fin.sem, 1)

            @b.sync
            def _(sp):
                sp.wait_ge(fin.sem, fin.at(DC))
                sp.dma_start(out, X[:, :, 0:SEQ]).then_inc(out_stored.sem, 16)
                sp.wait_ge(out_stored.sem, 16)


def constants():
    f = np.float32
    i = np.arange(P)
    small = np.zeros((P, C_SMALL), f)
    small[:, C_ID:C_ID + P] = np.eye(P)
    small[:, C_BLK:C_BLK + P] = (i[:, None] // 64 == i[None, :] // 64) / 64.0

    def partner(size):
        m = np.zeros((P, P), f)
        for p in range(P):
            if p % size < size // 2:
                m[p + size // 2, p] = -1
            else:
                m[p - size // 2, p] = 1
        return m
    small[:, C_RR:C_RR + P] = partner(32)

    c1 = np.zeros((P, C1_N), f)
    s = np.arange(PAIR)
    diff = i[:, None] + P - s[None, :]
    c1[:, C1_MASK:C1_MASK + PAIR] = np.where((diff >= 0) & (diff < P), 0, -1e30)
    t = np.arange(SEQ, dtype=f)
    inv = (1.0 / (10000.0 ** (np.arange(0, 64, 2, dtype=f) / f(64)))).astype(f)
    ang = (t[None, :] * inv[i % 32][:, None]).astype(f)
    c1[:, C1_COS:C1_COS + SEQ] = np.cos(ang)
    c1[:, C1_SIN:C1_SIN + SEQ] = np.sin(ang)
    c1[:, C1_RP:C1_RP + P] = partner(64)
    for h in range(4):
        c1[32 + h, C1_SELF + h] = 1
        c1[h, C1_SELH + h * P:C1_SELH + (h + 1) * P] = 1

    pool = np.zeros((P, 2, TOK), f)
    for g, w in enumerate((2, 4, 8, 16)):
        rows = slice(64 * (g % 2), 64 * (g % 2) + 64)
        for t0, n in ((0, SEQ), (SEQ, CTX)):
            tt = np.arange(n)
            count = np.clip(tt - w // 2 + w, 0, n) - np.clip(tt - w // 2, 0, n)
            pool[rows, g // 2, t0:t0 + n] = 1.0 / count

    na = np.zeros((P, 4, 8, SPAN), f)
    for k in range(4):
        col = 16 * k + i % 16
        first = np.clip(col - 8, 0, GRID - 16)
        key = COL0[k] + np.arange(SPAN)
        ok = (key[None, :] >= first[:, None]) & (key[None, :] < first[:, None] + 16)
        na[:, k] = np.where(ok, 0, -1e30)[:, None, :]

    cr = np.zeros((P, CR_N), f)
    inv = (10000.0 ** (-np.arange(16, dtype=f) / f(16))).astype(f)
    tt = np.arange(SEQ)
    pos = np.where((i % 64 < 32)[:, None], (tt // GRID)[None, :], (tt % GRID)[None, :]).astype(f)
    ang = (pos * inv[i % 16][:, None]).astype(f)
    cr[:, CR_COS:CR_COS + SEQ] = np.cos(ang)
    cr[:, CR_SIN:CR_SIN + SEQ] = np.sin(ang)
    cr[:, CR_DP:CR_DP + SEQ] = np.maximum(tt[None, :] - i[:, None], 0)
    cr[:, CR_DN:CR_DN + SEQ] = np.maximum(i[:, None] - (tt[None, :] - 3 * P), 0)
    cr[:, CR_QF:CR_QF + SEQ] = tt + 1
    cr[:, CR_QB:CR_QB + SEQ] = SEQ - tt
    cr[:, CR_MF:CR_MF + P] = i[None, :] >= i[:, None]
    cr[:, CR_MB:CR_MB + P] = i[None, :] <= i[:, None]
    for g in range(2):
        cr[:, CR_KE + g] = CTX - 1 - (g * P + i)
        cr[:, CR_KE + 2 + g] = g * P + i
    return small, c1, pool, na.reshape(P, 4 * PAIR), cr


def lay_out(v):
    out = {}

    def tiles(w):
        k, m = w.shape
        return w.reshape(k // P, P, m // P, P).transpose(2, 1, 0, 3).reshape(m // P, P, k)

    def cols(x):
        return x.reshape(-1, P).T

    small, c1, pool, na, cr = constants()
    out.update(consts=small, const1=c1, const_pool=pool, const_na=na, const_ret=cr)
    feature = lambda x: x.T.reshape(DC, P, -1).transpose(1, 0, 2)
    out["x"] = feature(v["x"][0])
    out["ctx"] = feature(v["ctx_2"][0])
    out["cond"] = np.stack([cols(v["c_2"][0]), cols(v["c_ctx_2"])], axis=2)

    o = np.cumsum([0, 256, 256, 512, 512, 8, 512, 128, 128])
    head_rows = np.concatenate([np.arange(64) + 64 * h for j in range(4) for h in (j, 4 + j)])
    order = np.concatenate([np.arange(o[0], o[4]), o[5] + head_rows, np.arange(o[6], o[8])])
    w_in, w_out, w_up, w_down, vec = [], [], [], [], []
    for l in range(DEPTH):
        w = v["w_in"][l]
        gates = np.zeros((D, P), np.float32)
        gates[:, 0:4], gates[:, 32:36] = w[:, o[4]:o[4] + 4], w[:, o[4] + 4:o[5]]
        w_in.append(tiles(np.concatenate([w[:, order], gates], axis=1)))
        rows = np.concatenate([np.arange(512), 512 + head_rows])
        w_out.append(tiles(v["w_out"][l][rows]))
        w_up.append(up_tiles(v["w_up"][l], tiles))
        w_down.append(down_tiles(v["w_down"][l]))
        q = np.zeros((P, V1_N), np.float32)
        q[:, V1_PRE:V1_PRE + 8] = cols(v["g_pre_mix"][l])
        q[:, V1_CW:V1_CW + 16] = v["qk_conv_w"][l].reshape(4, 4, P).transpose(2, 1, 0).reshape(P, 16)
        q[:, V1_CB:V1_CB + 4] = cols(v["qk_conv_b"][l])
        q[0:4, V1_GI], q[0:4, V1_GF] = v["gate_bias"][l][0:4], v["gate_bias"][l][4:8]
        q[:, V1_MH:V1_MH + 4] = cols(v["mh_norm_g"][l])
        q[:, V1_SINK:V1_SINK + 8] = v["attn_sinks"][l][None, :]
        q[:, V1_POST:V1_POST + 8] = cols(v["g_post_mix"][l])
        q[:, V1_PREF:V1_PREF + 8] = cols(v["g_pre_ffn"][l])
        q[:, V1_FCW:V1_FCW + 132] = taps(v["ffn_conv_w"][l])
        q[:, V1_POSTF:V1_POSTF + 8] = cols(v["g_post_ffn"][l])
        vec.append(q)
    out.update(w_in=np.concatenate(w_in), w_out=np.concatenate(w_out), w_up=np.concatenate(w_up),
               w_down=np.concatenate(w_down), vec1=np.stack(vec))

    o = np.cumsum([0, 256, 384, 384, 384, 384, 384, 384, 384])
    part = lambda n: np.arange(o[n], o[n + 1])
    order = np.concatenate([part(n) for n in (2, 3, 5, 6, 0, 1, 4, 7)])
    w_in, w_out, w_up, w_down, w_mod, vec, pw, bias = [], [], [], [], [], [], [], []
    r, c = np.arange(P) // 16, np.arange(P) % 16
    for l in range(DEPTH):
        w_in.append(tiles(v["w_in_2"][l][:, order]))
        w_out.append(tiles(v["w_out_2"][l]))
        w_mod.append(tiles(v["w_mod_2"][l]))
        w_up.append(up_tiles(v["w_up_2"][l], tiles))
        w_down.append(down_tiles(v["w_down_2"][l]))
        q = np.zeros((P, V2_N), np.float32)
        q[:, V2_BM:V2_BM + 48] = cols(v["b_mod_2"][l])
        q[:, V2_N1:V2_N1 + 8] = cols(v["norm1_g_2"][l])
        q[:, V2_PS:V2_PS + 2] = cols(v["pool_scale_2"][l])
        q[:, V2_LF:V2_LF + 6] = v["ret_decay_fwd_2"][l][None, :]
        q[:, V2_LB:V2_LB + 6] = v["ret_decay_bwd_2"][l][None, :]
        q[:, V2_GN:V2_GN + 3] = cols(v["ret_gn_g_2"][l])
        q[:, V2_N2:V2_N2 + 8] = cols(v["norm2_g_2"][l])
        q[:, V2_CW:V2_CW + 132] = taps(v["conv_w_2"][l])
        q[:, V2_CB:V2_CB + 44] = cols(v["conv_b_2"][l])[:, paired()]
        vec.append(q)
        m = np.zeros((P, 2, P), np.float32)
        for g in range(4):
            rows = slice(64 * (g % 2), 64 * (g % 2) + 64)
            m[rows, g // 2, rows] = v["pool_w_2"][l][g]
        pw.append(m)
        for h in range(NA_H):
            table = v["na_rpb_2"][l][h]
            per_k = []
            for k in range(4):
                dr = np.arange(8)[None, :] - r[:, None] + 7
                dc = np.clip(COL0[k] + np.arange(SPAN)[None, :] - 16 * k - c[:, None] + 15, 0, 30)
                per_k.append(table[dr[:, :, None], dc[:, None, :]].reshape(P, PAIR))
            bias.append(np.concatenate(per_k, axis=1))
    out.update(w_in2=np.concatenate(w_in), w_out2=np.concatenate(w_out), w_up2=np.concatenate(w_up),
               w_down2=np.concatenate(w_down), w_mod=np.concatenate(w_mod), vec2=np.stack(vec),
               pool_w=np.stack(pw), na_bias=np.stack(bias), final=cols(v["final_g_2"]))
    return {k: np.ascontiguousarray(x, dtype=np.float32) for k, x in out.items()}


def paired():
    return np.stack([np.arange(FF // P), np.arange(FF // P) + FF // P], axis=1).reshape(-1)


def up_tiles(w, tiles):
    return tiles(w)[paired()]


def down_tiles(w):
    return w.reshape(2, HALF, P, DC, P).transpose(0, 3, 2, 1, 4).reshape(2 * DC, P, HALF * P)


def taps(w):
    return w.reshape(3, 2 * FF // P, P)[:, paired(), :].transpose(2, 1, 0).reshape(P, -1)


def kernel(**inputs):
    import concourse.bacc as bacc
    from concourse.bass_utils import run_bass_kernel_spmd as run

    v = {k: np.asarray(x) for k, x in inputs.items()}
    arrays = lay_out(v)
    nc = bacc.Bacc("TRN2", target_bir_lowering=False, num_devices=1)
    handles = {k: nc.dram_tensor("in_" + k, x.shape, F32, kind="ExternalInput").ap() for k, x in arrays.items()}
    out = nc.dram_tensor("out_rows", (P, DC, SEQ), F32, kind="ExternalOutput").ap()
    build(nc, handles, out)
    r = run(nc, [{"in_" + k: x for k, x in arrays.items()}], core_ids=[0])
    got = np.asarray(r.results[0]["out_rows"])
    return np.ascontiguousarray(got.transpose(2, 1, 0).reshape(1, SEQ, D))
```

```python
from contextlib import ExitStack

import numpy as np

import concourse.bass as bass
from concourse import mybir

F32 = mybir.dt.float32
F32R = mybir.dt.float32r
ALU = mybir.AluOpType
ACT = mybir.ActivationFunctionType
AX = mybir.AxisListType

P = 128
D = 1024
DC = D // P
SEQ = 512
CTX = 256
TOK = SEQ + CTX
DEPTH = 2
EPS = 1e-6
FF = 2816
HALF = FF // P // 2
PAIR = 2 * P

Q1, K1, V1, O1, AQ1, AK1, AV1, GT1 = 0, 2, 4, 8, 12, 16, 17, 18
N1 = 19
NK, NV, RK, RV, PO, NQ, RQ, RG = 0, 3, 6, 9, 12, 14, 17, 20
N2 = 23
N2_KV = 12
NA_H = 6
RET_H = 6
GRID = 64
SPAN = 32
COL0 = (0, 8, 24, 32)

V1_PRE, V1_CW, V1_CB, V1_GI, V1_GF, V1_MH, V1_SINK, V1_POST, V1_PREF, V1_FCW, V1_POSTF = (
    0, 8, 24, 28, 29, 30, 34, 42, 50, 58, 58 + 132)
V1_N = V1_POSTF + 8
V2_BM, V2_N1, V2_PS, V2_LF, V2_LB, V2_GN, V2_N2, V2_CW, V2_CB = (
    0, 48, 56, 58, 64, 70, 73, 81, 81 + 132)
V2_N = V2_CB + 44

C_ID, C_BLK, C_RR = 0, 128, 256
C_SMALL = 384
C1_MASK, C1_COS, C1_SIN, C1_RP, C1_SELF, C1_SELH = 0, 256, 768, 1280, 1408, 1412
C1_N = C1_SELH + 512
CN_MASK = 1024
CR_COS, CR_SIN, CR_DP, CR_DN, CR_QF, CR_QB, CR_MF, CR_MB, CR_KE = (
    0, 512, 1024, 1536, 2048, 2560, 3072, 3200, 3328)
CR_N = CR_KE + 4


def ranges(tokens):
    return [(0, SEQ)] + ([(SEQ, CTX)] if tokens == TOK else [])


class Signal:

    def __init__(self, nc, ctx, name):
        self.sem = ctx.enter_context(nc.semaphore(name))
        self.base = 0
        self.n = 0

    def at(self, n):
        return n + self.base

    def next(self):
        self.n += 1
        return self.base + self.n


def later(n):
    return not isinstance(n, int) or n > 0


def tile_loop(eng, n, body, tail=1):
    pairs = (n - tail) // 2
    body(0, 0)
    body(1, 1)
    if pairs > 1:
        with eng.Fori(1, pairs) as i:
            body(i * 2, 0)
            body(i * 2 + 1, 1)
    for t in range(max(2, 2 * pairs), n):
        body(t, t % 2)


def at(i, n=1):
    return slice(i, i + n) if isinstance(i, int) else bass.ds(i, n)


def build(nc, a, out):
    ctx = ExitStack()
    with ctx:
        base = (nc.sbuf_base + 31) // 32 * 32
        used = [base]

        def sb(name, shape, dt=F32, offset=None):
            size = 4 * int(np.prod(shape[1:]))
            if offset is None:
                offset = used[0]
                used[0] += (size + 31) // 32 * 32
            return nc.alloc_sbuf_tensor_at(name, shape, dt, offset=offset)

        def room(size):
            offset = used[0]
            used[0] += (size + 31) // 32 * 32
            return offset

        X = sb("X", [P, DC, TOK])
        o_h = used[0]
        HH = sb("HH", [P, DC, TOK], F32R)
        HL = sb("HL", [P, DC, TOK], F32R)
        o_big = room(N2 * TOK * 4)
        o_stage = used[0]
        STAGE = [sb(f"STAGE{s}", [P, HALF * P]) for s in range(2)]
        WH = [sb(f"WH{s}", [P, HALF * P], F32R) for s in range(2)]
        WL = [sb(f"WL{s}", [P, HALF * P], F32R) for s in range(2)]
        o_tmp = room(5 * TOK * 4)
        SQ = [sb(f"SQ{s}", [P, TOK], offset=o_tmp + s * TOK * 4) for s in range(2)]
        RSTD = sb("RSTD", [P, TOK], offset=o_tmp + 3 * TOK * 4)
        CG = sb("CG", [P, TOK], offset=o_tmp)
        CV = sb("CV", [P, TOK], offset=o_tmp + TOK * 4)
        T1 = [sb(f"T1{s}", [P, TOK], offset=o_tmp + s * TOK * 4) for s in range(2)]
        VEC1 = [sb(f"VEC1_{l}", [P, V1_N]) for l in range(DEPTH)]
        VEC2 = [sb(f"VEC2_{l}", [P, V2_N]) for l in range(DEPTH)]
        FIN = sb("FIN", [P, DC])
        CST1 = sb("CST1", [P, C1_N])
        CS = sb("CS", [P, C_SMALL])
        IDENT, BLK, RROT = CS[:, 0:128], CS[:, 128:256], CS[:, 256:384]
        MODBUF = [sb(f"MODBUF{i}", [P, DC, P], offset=o_stage + i * HALF * P * 4) for i in range(6)]
        ONES = sb("ONES", [P, P])
        EPSC = sb("EPSC", [P, 1])
        ZERO = sb("ZERO", [P, 1])
        MEAN = sb("MEAN", [P, P])
        MODS = [sb(f"MOD{l}", [P, 48, 2]) for l in range(DEPTH)]
        A1S = [sb(f"A1_{l}", [P, DC, 2]) for l in range(DEPTH)]
        A2S = [sb(f"A2_{l}", [P, DC, 2]) for l in range(DEPTH)]
        CC = sb("CC", [P, DC, 2])
        SC = sb("SC", [P, DC, 2])
        SM = sb("SM", [P, 256])
        MROW = sb("MROW", [P, 3 * P])
        assert used[0] <= nc.sbuf_usable_end, used[0]

        Z = sb("Z", [P, N2, TOK], offset=o_big)
        Z1 = sb("Z1", [P, N1, SEQ], offset=o_big)
        GH = sb("GH", [P, HALF, TOK], F32R, offset=o_big)
        GL = sb("GL", [P, HALF, TOK], F32R, offset=o_big + HALF * TOK * 4)
        GH1 = sb("GH1", [P, HALF, SEQ], F32R, offset=o_big)
        GL1 = sb("GL1", [P, HALF, SEQ], F32R, offset=o_big + HALF * SEQ * 4)
        Y = sb("Y", [P, DC, SEQ], offset=o_big + 2 * HALF * SEQ * 4)

        PS = [ctx.enter_context(nc.psum_tensor(f"PS{i}", [P, 1024], F32)) for i in range(4)]

        sig = {}

        def S(name):
            if name not in sig:
                sig[name] = Signal(nc, ctx, name)
            return sig[name]

        def block():
            return nc.Block(no_gpsimd_drain=True)

        def done(**counts):
            for name, n in counts.items():
                S(name).base += n
                S(name).n = 0

        def load(pairs):
            loaded = S("small_loaded")
            with block() as b:
                @b.sync
                def _(sp):
                    for dst, src in pairs:
                        sp.dma_start(dst, src).then_inc(loaded.sem, 16)
                    sp.wait_ge(loaded.sem, loaded.at(16 * len(pairs)))
            done(small_loaded=16 * len(pairs))

        class Segment:

            def __init__(self, weights, first, n, kc, hi, lo, tokens, kind="rows", out_act=None,
                         out_dve=None, squares=None, half=0, ready=None,
                         gh=None, gl=None, own=0, others=(), vec=None, tap_col=0, bias_col=None):
                self.weights, self.first, self.n, self.kc = weights, first, n, kc
                self.hi, self.lo, self.tokens, self.kind = hi, lo, tokens, kind
                self.out_act, self.out_dve, self.squares = out_act, out_dve, squares
                self.half, self.ready, self.size = half, ready, kc * P
                self.gh, self.gl, self.own, self.others = gh, gl, own, others
                self.vec, self.tap_col, self.bias_col = vec, tap_col, bias_col

        def place(segments):
            g = 0
            for i, seg in enumerate(segments):
                yield seg, g, (segments[i + 1] if i + 1 < len(segments) else None)
                g += seg.n

        loaded = [S("w_loaded0"), S("w_loaded1")]
        w_hi, w_lo, acc_done, acc_free = S("w_hi"), S("w_lo"), S("acc_done"), S("acc_free")
        own_done, tap_done, silu_done = S("own_done"), S("tap_done"), S("silu_done")
        gated, g_hi, g_lo = S("gated"), S("g_hi"), S("g_lo")
        sq_done, sq_summed, log_done, rstd_done = S("sq_done"), S("sq_summed"), S("log_done"), S("rstd_done")
        t_done, h_hi, h_lo, added = S("t_done"), S("h_hi"), S("h_lo"), S("added")

        def stream_sync(sp, segments):
            for seg, g, _ in place(segments):
                def body(t, s):
                    if later(t + g - 1):
                        sp.wait_ge(w_lo.sem, w_lo.at(t + g - 1))
                    src = seg.weights[at(t + seg.first)].rearrange("a p n -> p (a n)")
                    sp.dma_start(STAGE[s][:, 0:seg.size], src).then_inc(loaded[s].sem, 16)
                tile_loop(sp, seg.n, body, tail=0)

        def split_high(act, g, s, size):
            act.wait_ge(loaded[s].sem, loaded[s].at((g - s) * 8 + 16))
            act.activation(WH[s][:, 0:size], STAGE[s][:, 0:size], ACT.Copy).then_inc(w_hi.sem, 1)

        def split_low(dve, g, s, size):
            dve.wait_ge(w_hi.sem, w_hi.at(g + 1))
            dve.tensor_tensor(WL[s][:, 0:size], STAGE[s][:, 0:size], WH[s][:, 0:size].bitcast(F32),
                              ALU.subtract).then_inc(w_lo.sem, 1)

        def split_next(split, eng, seg, g, after, t, s):
            if not isinstance(t, int) or t + 2 < seg.n:
                split(eng, t + g + 2, s, seg.size)
            elif after is not None:
                split(eng, t + g + 2, s, after.size)

        def tap(seg, t, k):
            return seg.vec[:, at(t * 3 + (seg.tap_col + seg.half * seg.n * 3 + k))]

        def stream_act(act, segments):
            for seg, g, after in place(segments):
                tokens, j0 = seg.tokens, seg.half * HALF

                def rows(t, s):
                    act.wait_ge(acc_done.sem, acc_done.at(t + g + 1))
                    if seg.out_act:
                        seg.out_act(act, t, PS[s]).then_inc(acc_free.sem, 1)
                    split_next(split_high, act, seg, g, after, t, s)
                    if seg.squares:
                        act.wait_ge(acc_free.sem, acc_free.at(t + g + 1))
                        if later(t - 1):
                            act.wait_ge(sq_summed.sem, sq_summed.at(t - 1))
                        act.activation(SQ[s][:, 0:tokens], seg.squares(t), ACT.Square).then_inc(sq_done.sem, 1)

                def hidden(t, s, j):
                    buf = (CG, CV)[s]
                    act.wait_ge(acc_done.sem, acc_done.at(t + g + 1))
                    if later(j + j0):
                        act.wait_ge(g_lo.sem, g_lo.at(j + j0))
                    bias = (seg.vec[:, at(t + (seg.bias_col + seg.half * seg.n))]
                            if seg.bias_col is not None else ZERO[:, 0:1])
                    act.activation(buf[:, 0:tokens], PS[s][:, 0:tokens], ACT.Identity,
                                   scale=tap(seg, t, seg.own), bias=bias).then_inc(own_done.sem, 1)
                    split_next(split_high, act, seg, g, after, t, s)
                    if s == 1:
                        act.wait_ge(acc_free.sem, acc_free.at(t + g))
                        act.activation(CG[:, 0:tokens], CG[:, 0:tokens], ACT.Silu).then_inc(silu_done.sem, 1)
                        act.wait_ge(gated.sem, gated.at(j + (j0 + 1)))
                        act.activation(seg.gh[:, at(j), 0:tokens].rearrange("p a t -> p (a t)"),
                                       CV[:, 0:tokens], ACT.Copy).then_inc(g_hi.sem, 1)

                if seg.kind == "rows":
                    tile_loop(act, seg.n, rows, tail=2)
                else:
                    hidden_loop(act, hidden)

        def hidden_loop(eng, body):
            body(0, 0, 0)
            body(1, 1, 0)
            with eng.Fori(1, HALF - 1) as j:
                body(j * 2, 0, j)
                body(j * 2 + 1, 1, j)
            body(2 * HALF - 2, 0, HALF - 1)
            body(2 * HALF - 1, 1, HALF - 1)

        def stream_dve(dve, segments):
            for seg, g, after in place(segments):
                tokens, j0 = seg.tokens, seg.half * HALF

                def rows(t, s):
                    if seg.out_dve:
                        dve.wait_ge(acc_done.sem, acc_done.at(t + g + 1))
                        seg.out_dve(dve, t, PS[s]).then_inc(acc_free.sem, 1)
                    split_next(split_low, dve, seg, g, after, t, s)

                def hidden(t, s, j):
                    buf = (CG, CV)[s]
                    u = t + seg.half * seg.n
                    dve.wait_ge(own_done.sem, own_done.at(u + 1))
                    for m, (k, shift) in enumerate(seg.others):
                        if m:
                            dve.wait_ge(tap_done.sem, tap_done.at(u + 1))
                        for r, (t0, tn) in enumerate(ranges(tokens)):
                            lo, hi = max(0, shift), min(0, shift)
                            ins = dve.scalar_tensor_tensor(
                                out=buf[:, t0 + lo:t0 + tn + hi],
                                in0=PS[s][:, t0 + lo - shift:t0 + tn + hi - shift], scalar=tap(seg, t, k),
                                in1=buf[:, t0 + lo:t0 + tn + hi], op0=ALU.mult, op1=ALU.add)
                        ins.then_inc((tap_done if m == 0 else acc_free).sem, 1)
                    split_next(split_low, dve, seg, g, after, t, s)
                    if s == 1:
                        dve.wait_ge(silu_done.sem, silu_done.at(j + (j0 + 1)))
                        dve.wait_ge(acc_free.sem, acc_free.at(t + g + 1))
                        dve.tensor_tensor(CV[:, 0:tokens], CV[:, 0:tokens], CG[:, 0:tokens],
                                          ALU.mult).then_inc(gated.sem, 1)
                        dve.wait_ge(g_hi.sem, g_hi.at(j + (j0 + 1)))
                        dve.tensor_tensor(seg.gl[:, at(j), 0:tokens].rearrange("p a t -> p (a t)"),
                                          CV[:, 0:tokens],
                                          seg.gh[:, at(j), 0:tokens].rearrange("p a t -> p (a t)").bitcast(F32),
                                          ALU.subtract).then_inc(g_lo.sem, 1)

                if seg.kind == "rows":
                    tile_loop(dve, seg.n, rows, tail=2)
                else:
                    hidden_loop(dve, hidden)

        def stream_pe(pe, segments):
            for seg, g, _ in place(segments):
                def sum_squares(t, s):
                    pe.wait_ge(sq_done.sem, sq_done.at(t + 1))
                    for t0, tn in ranges(seg.tokens):
                        ins = pe.matmul(PS[2][:, t0:t0 + tn], MEAN[:], SQ[s][:, t0:t0 + tn],
                                        start=(isinstance(t, int) and t == 0),
                                        stop=(isinstance(t, int) and t == seg.n - 1), skip_group_check=True)
                    ins.then_inc(sq_summed.sem, 1)

                def body(t, s):
                    pe.wait_ge(w_lo.sem, w_lo.at(t + g + 1))
                    if later(t + g - 1):
                        pe.wait_ge(acc_free.sem, acc_free.at(t + g - 1))
                    for k in range(seg.kc):
                        if seg.ready and isinstance(t, int) and t == 0:
                            signal, n0 = seg.ready
                            pe.wait_ge(signal.sem, signal.at(n0 + k + 1))
                        parts = ((WH[s], seg.hi), (WH[s], seg.lo), (WL[s], seg.hi))
                        for m, (w, r) in enumerate(parts):
                            for t0, tn in ranges(seg.tokens):
                                ins = pe.matmul(PS[s][:, t0:t0 + tn], w[:, k * P:k * P + P], r[:, k, t0:t0 + tn],
                                                start=(k == 0 and m == 0), stop=(k == seg.kc - 1 and m == 2))
                    ins.then_inc(acc_done.sem, 1)
                    if seg.squares and later(t):
                        sum_squares(t - 1, 1 - s)
                tile_loop(pe, seg.n, body, tail=2)
                if seg.squares:
                    sum_squares(seg.n - 1, (seg.n - 1) % 2)

        def stream_counts(segments):
            n = sum(seg.n for seg in segments)
            hid = sum(seg.n for seg in segments if seg.kind == "hidden")
            sq = sum(seg.n for seg in segments if seg.squares)
            return dict(w_loaded0=16 * ((n + 1) // 2), w_loaded1=16 * (n // 2), w_hi=n, w_lo=n, acc_done=n,
                        acc_free=n, own_done=hid, tap_done=hid, silu_done=hid // 2, gated=hid // 2,
                        g_hi=hid // 2, g_lo=hid // 2, sq_done=sq, sq_summed=sq)

        def rstd_act(act, n, tokens, squares):
            if squares:
                act.wait_ge(sq_summed.sem, sq_summed.at(squares))
            act.activation(RSTD[:, 0:tokens], PS[2][:, 0:tokens], ACT.Ln, bias=EPSC[:, 0:1]).then_inc(log_done.sem, 1)
            act.wait_ge(log_done.sem, log_done.at(n))
            act.activation(RSTD[:, 0:tokens], RSTD[:, 0:tokens], ACT.Exp, scale=-0.5).then_inc(rstd_done.sem, 1)

        def normed_stream(segments, tokens, scale, shift, fresh=False, gain=None):
            rs = ranges(tokens)
            fresh = fresh or gain is not None
            first = segments[0]
            first.ready = (h_lo, 0)
            norms = 2 if gain else 1
            sq0 = DC if fresh else 0

            with block() as b:
                @b.sync
                def _(sp):
                    stream_sync(sp, segments)

                @b.scalar
                def _(act):
                    if gain:
                        rstd_act(act, 1, tokens, 0)
                    if fresh:
                        for c in range(DC):
                            if gain:
                                act.wait_ge(added.sem, added.at(c + 1))
                            if c > 1:
                                act.wait_ge(sq_summed.sem, sq_summed.at(c - 1))
                            act.activation(SQ[c % 2][:, 0:tokens], X[:, c, 0:tokens],
                                           ACT.Square).then_inc(sq_done.sem, 1)
                            if c in (4, 6):
                                split_high(act, c // 2 - 2, c // 2 - 2, first.size)
                    if gain:
                        act.wait_ge(added.sem, added.at(DC))
                    rstd_act(act, norms, tokens, sq0)
                    if not fresh:
                        split_high(act, 0, 0, first.size)
                    for c in range(DC):
                        if c == 3 and not fresh:
                            split_high(act, 1, 1, first.size)
                        act.wait_ge(t_done.sem, t_done.at(c + 1))
                        for st, (t0, tn) in enumerate(rs):
                            ins = act.activation(HH[:, c, t0:t0 + tn], T1[c % 2][:, t0:t0 + tn],
                                                 ACT.Identity, bias=shift(c, st))
                        ins.then_inc(h_hi.sem, 1)
                    sq_done.base, sq_summed.base = sq_done.base + sq0, sq_summed.base + sq0
                    stream_act(act, segments)
                    sq_done.base, sq_summed.base = sq_done.base - sq0, sq_summed.base - sq0

                @b.vector
                def _(dve):
                    if gain:
                        dve.wait_ge(rstd_done.sem, rstd_done.at(1))
                        y_scaled = S("y_scaled")
                        for c in range(DC + 1):
                            if c < DC:
                                dve.scalar_tensor_tensor(out=Y[:, c, :], in0=Y[:, c, :], scalar=gain(c),
                                                         in1=RSTD[:, 0:SEQ], op0=ALU.mult,
                                                         op1=ALU.mult).then_inc(y_scaled.sem, 1)
                            if c:
                                dve.wait_ge(y_scaled.sem, y_scaled.at(c))
                                dve.tensor_tensor(X[:, c - 1, 0:SEQ], X[:, c - 1, 0:SEQ], Y[:, c - 1, :],
                                                  ALU.add).then_inc(added.sem, 1)
                    if fresh:
                        split_low(dve, 0, 0, first.size)
                        split_low(dve, 1, 1, first.size)
                    dve.wait_ge(rstd_done.sem, rstd_done.at(norms))

                    def normed(c):
                        if c > 1:
                            dve.wait_ge(h_lo.sem, h_lo.at(c - 1))
                        for st, (t0, tn) in enumerate(rs):
                            ins = dve.scalar_tensor_tensor(
                                out=T1[c % 2][:, t0:t0 + tn], in0=X[:, c, t0:t0 + tn], scalar=scale(c, st),
                                in1=RSTD[:, t0:t0 + tn], op0=ALU.mult, op1=ALU.mult)
                        ins.then_inc(t_done.sem, 1)

                    normed(0)
                    if not fresh:
                        split_low(dve, 0, 0, first.size)
                    for c in range(DC):
                        if c == 4 and not fresh:
                            split_low(dve, 1, 1, first.size)
                        if c + 1 < DC:
                            normed(c + 1)
                        dve.wait_ge(h_hi.sem, h_hi.at(c + 1))
                        for st, (t0, tn) in enumerate(rs):
                            ins = dve.scalar_tensor_tensor(
                                out=HL[:, c, t0:t0 + tn], in0=T1[c % 2][:, t0:t0 + tn], scalar=shift(c, st),
                                in1=HH[:, c, t0:t0 + tn].bitcast(F32), op0=ALU.add, op1=ALU.subtract)
                        ins.then_inc(h_lo.sem, 1)
                    stream_dve(dve, segments)

                @b.tensor
                def _(pe):
                    if fresh:
                        if gain:
                            pe.wait_ge(log_done.sem, log_done.at(1))
                        for c in range(DC):
                            pe.wait_ge(sq_done.sem, sq_done.at(c + 1))
                            for t0, tn in rs:
                                ins = pe.matmul(PS[2][:, t0:t0 + tn], MEAN[:], SQ[c % 2][:, t0:t0 + tn],
                                                start=(c == 0), stop=(c == DC - 1))
                            ins.then_inc(sq_summed.sem, 1)
                    sq_done.base += sq0
                    stream_pe(pe, segments)
                    sq_done.base -= sq0
            counts = stream_counts(segments)
            counts["sq_done"] += sq0
            counts["sq_summed"] += sq0
            done(**counts, log_done=norms, rstd_done=norms, t_done=DC, h_hi=DC, h_lo=DC,
                 added=DC if gain else 0, y_scaled=DC if gain else 0)

        def update_x(gain):
            y_scaled = S("y_scaled")
            with block() as b:
                @b.scalar
                def _(act):
                    rstd_act(act, 1, SEQ, 0)

                @b.vector
                def _(dve):
                    dve.wait_ge(rstd_done.sem, rstd_done.at(1))
                    for c in range(DC + 1):
                        if c < DC:
                            dve.scalar_tensor_tensor(out=Y[:, c, :], in0=Y[:, c, :], scalar=gain(c),
                                                     in1=RSTD[:, 0:SEQ], op0=ALU.mult,
                                                     op1=ALU.mult).then_inc(y_scaled.sem, 1)
                        if c:
                            dve.wait_ge(y_scaled.sem, y_scaled.at(c))
                            dve.tensor_tensor(X[:, c - 1, 0:SEQ], X[:, c - 1, 0:SEQ], Y[:, c - 1, :],
                                              ALU.add).then_inc(added.sem, 1)
            done(log_done=1, rstd_done=1, y_scaled=DC, added=DC)

        def split_stream(src, chunks, tokens, segments):
            first = segments[0]
            first.ready = (h_lo, 0)
            with block() as b:
                @b.sync
                def _(sp):
                    stream_sync(sp, segments)

                @b.scalar
                def _(act):
                    for c, z in enumerate(chunks):
                        act.activation(HH[:, c, 0:tokens], src[:, z, 0:tokens], ACT.Copy).then_inc(h_hi.sem, 1)
                        if c == 3:
                            split_high(act, 0, 0, first.size)
                    split_high(act, 1, 1, first.size)
                    stream_act(act, segments)

                @b.vector
                def _(dve):
                    for c, z in enumerate(chunks):
                        dve.wait_ge(h_hi.sem, h_hi.at(c + 1))
                        dve.tensor_tensor(HL[:, c, 0:tokens], src[:, z, 0:tokens],
                                          HH[:, c, 0:tokens].bitcast(F32), ALU.subtract).then_inc(h_lo.sem, 1)
                        if c == 3:
                            split_low(dve, 0, 0, first.size)
                    split_low(dve, 1, 1, first.size)
                    stream_dve(dve, segments)

                @b.tensor
                def _(pe):
                    stream_pe(pe, segments)
            done(**stream_counts(segments), h_hi=DC, h_lo=DC)

        def region(offset, size):
            at_, end = [offset], offset + size

            def take(name, shape):
                o = at_[0]
                at_[0] += (4 * int(np.prod(shape[1:])) + 31) // 32 * 32
                assert at_[0] <= end, (name, at_[0], end)
                return sb(name, shape, offset=o)
            return take

        h1 = region(o_h, 2 * DC * TOK * 4)
        QK = h1("QK", [P, 4, SEQ])
        VT = h1("VT", [P, 4, SEQ])
        AVT = h1("AVT", [P, 4, P])
        EM = [h1(f"EM{i}", [P, SEQ]) for i in range(2)]
        LI, XF, AB, CUM, GG, MX, NM = (h1(n, [P, SEQ]) for n in ("LI", "XF", "AB", "CUM", "GG", "MX", "NM"))
        WT = [h1(f"WT{i}", [P, SEQ]) for i in range(2)]
        PT = [h1(f"PT{i}", [P, SEQ]) for i in range(2)]
        HT = h1("HT", [P, SEQ])
        ONE4 = h1("ONE4", [P, SEQ])
        b1 = region(o_big + N1 * SEQ * 4, (N2 * TOK - N1 * SEQ) * 4)
        PW = [b1(f"PW{i}", [P, 4, PAIR]) for i in range(2)]
        PTT = [b1(f"PTT{i}", [P, 2 * SEQ]) for i in range(2)]
        GT = SM[:, 0:16]

        RING = 6
        mod_in = [S(f"mod_in{i}") for i in range(RING)]
        mod_done, mod_copied, mod_turned = S("mod_done"), S("mod_copied"), S("mod_turned")
        MOD_N = 6 * D // P
        PREPARE_TILES, GATE_TILES = range(0, 6), range(6, 15)
        MLSTM_TILES, WINDOW_TILES = range(15, 30), range(30, MOD_N)
        MOD_EARLY, MOD_LATE = PS[1][:, SEQ:], PS[3][:, SEQ:]

        def mod_sync(sp, l, tiles):
            first = tiles.start + RING if tiles.start else 0
            for t in range(first, min(tiles.stop + RING, MOD_N)):
                if later(t - RING + 1):
                    sp.wait_ge(mod_done.sem, mod_done.at(t - RING + 1))
                sp.dma_start(MODBUF[t % RING][:].rearrange("p k m -> p (k m)"),
                             a["w_mod"][l * MOD_N + t]).then_inc(mod_in[t % RING].sem, 16)

        def mod_rows(pe, g, ps):
            if later(g):
                pe.wait_ge(mod_copied.sem, mod_copied.at(g))
            for i in range(3):
                t = 3 * g + i
                pe.wait_ge(mod_in[t % RING].sem, mod_in[t % RING].at(16 * (t // RING + 1)))
                for k in range(DC):
                    ins = pe.matmul(ps[0:2, i * P:i * P + P], SC[:, k, :], MODBUF[t % RING][:, k, :],
                                    start=(k == 0), stop=(k == DC - 1))
                ins.then_inc(mod_done.sem, 1)

        def mod_copy(act, g, ps):
            act.wait_ge(mod_done.sem, mod_done.at(3 * g + 3))
            if later(g):
                act.wait_ge(mod_turned.sem, mod_turned.at(g))
            act.activation(MROW[0:2, :], ps[0:2, 0:3 * P], ACT.Copy).then_inc(mod_copied.sem, 1)

        def mod_turn(pe, g, ps):
            pe.wait_ge(mod_copied.sem, mod_copied.at(g + 1))
            for i in range(3):
                c = 3 * P + 2 * (3 * g + i)
                ins = pe.transpose(ps[:, c:c + 2], MROW[0:2, i * P:i * P + P], IDENT[0:2, 0:2])
            ins.then_inc(mod_turned.sem, 1)

        def mod_add(dve, l, t0, t1, ps):
            return dve.tensor_tensor(MODS[l][:, t0:t1, :], ps[:, 3 * P + 2 * t0:3 * P + 2 * t1].rearrange("p (t c) -> p t c", c=2),
                                     VEC2[l][:, V2_BM + t0:V2_BM + t1].unsqueeze(2).broadcast_to([P, t1 - t0, 2]),
                                     ALU.add)

        def mod_out(l):
            VEC, MOD = VEC2[l], MODS[l]
            mod_sum = S("mod_sum")
            with block() as b:
                @b.vector
                def _(dve):
                    mod_add(dve, l, MLSTM_TILES.start, MOD_N, MOD_LATE).then_inc(mod_sum.sem, 1)
                    dve.wait_ge(mod_sum.sem, mod_sum.at(1))
                    for dst, scale, gain in ((A1S[l], 1, V2_N1), (A2S[l], 4, V2_N2)):
                        dve.scalar_tensor_tensor(
                            out=dst[:], in0=MOD[:, scale * DC:(scale + 1) * DC, :], scalar=1.0,
                            in1=VEC[:, gain:gain + DC].unsqueeze(2).broadcast_to([P, DC, 2]),
                            op0=ALU.add, op1=ALU.mult)
            done(mod_sum=1)

        def mix1_prepare(VEC, l):
            vt_ps, vt_free, rot_ps, rot_free = S("vt_ps"), S("vt_free"), S("rot_ps"), S("rot_free")
            own_done, conv_done = S("own_done"), S("conv_done")
            rope = [AQ1, AQ1 + 1, AQ1 + 2, AQ1 + 3, AK1]
            with block() as b:
                @b.sync
                def _(sp):
                    mod_sync(sp, l, PREPARE_TILES)

                @b.tensor
                def _(pe):
                    pe.matmul(PS[3][0:4, 0:SEQ], CST1[:, C1_SELF:C1_SELF + 4], Z1[:, GT1, :],
                              start=True, stop=True)
                    for i in range(4):
                        if later(i - 1):
                            pe.wait_ge(vt_free.sem, vt_free.at(i - 1))
                        for c in range(4):
                            ins = pe.transpose(PS[i % 2][:, c * P:c * P + P],
                                               Z1[:, V1 + c, i * P:i * P + P], IDENT)
                        ins.then_inc(vt_ps.sem, 1)
                    for i in range(4):
                        ins = pe.transpose(PS[2][:, i * P:i * P + P], Z1[:, AV1, i * P:i * P + P], IDENT)
                    ins.then_inc(vt_ps.sem, 1)
                    mod_rows(pe, 0, MOD_EARLY)
                    for n, c in enumerate(rope):
                        if n == 3:
                            mod_turn(pe, 0, MOD_EARLY)
                            mod_rows(pe, 1, MOD_EARLY)
                        if later(n - 1):
                            pe.wait_ge(rot_free.sem, rot_free.at(n - 1))
                        pe.matmul(PS[n % 2 + 2][:, SEQ:2 * SEQ], CST1[:, C1_RP:C1_RP + P], Z1[:, c, :],
                                  start=True, stop=True).then_inc(rot_ps.sem, 1)

                @b.scalar
                def _(act):
                    for i in range(4):
                        act.wait_ge(vt_ps.sem, vt_ps.at(i + 1))
                        act.activation(VT[:, i, :], PS[i % 2][:, 0:SEQ], ACT.Copy).then_inc(vt_free.sem, 1)
                    for c in range(4):
                        act.activation(QK[:, c, :], Z1[:, c, :], ACT.Identity,
                                       scale=VEC[:, V1_CW + c * 4 + 3:V1_CW + c * 4 + 4],
                                       bias=VEC[:, V1_CB + c:V1_CB + c + 1]).then_inc(own_done.sem, 1)
                    act.wait_ge(vt_ps.sem, vt_ps.at(5))
                    act.activation(AVT[:].rearrange("p a b -> p (a b)"), PS[2][:, 0:SEQ],
                                   ACT.Copy).then_inc(vt_free.sem, 1)
                    act.activation(Z1[:, O1:O1 + 4, :], Z1[:, O1:O1 + 4, :], ACT.Sigmoid)
                    for c in range(4):
                        act.wait_ge(conv_done.sem, conv_done.at(3 * c + 3))
                        act.activation(QK[:, c, :], QK[:, c, :], ACT.Silu)
                        if c == 1:
                            mod_copy(act, 0, MOD_EARLY)
                    mod_copy(act, 1, MOD_EARLY)

                @b.vector
                def _(dve):
                    conv_done, rot_step = S("conv_done"), S("rot_step")
                    for c in range(4):
                        dve.wait_ge(own_done.sem, own_done.at(c + 1))
                        for k in range(3):
                            d = 3 - k
                            dve.scalar_tensor_tensor(
                                out=QK[:, c, d:SEQ], in0=Z1[:, c, 0:SEQ - d],
                                scalar=VEC[:, V1_CW + c * 4 + k:V1_CW + c * 4 + k + 1],
                                in1=QK[:, c, d:SEQ], op0=ALU.mult, op1=ALU.add).then_inc(conv_done.sem, 1)
                            dve.wait_ge(conv_done.sem, conv_done.next())
                    for n, c in enumerate(rope):
                        dve.wait_ge(rot_ps.sem, rot_ps.at(n + 1))
                        dve.tensor_tensor(HT[:], PS[n % 2 + 2][:, SEQ:2 * SEQ],
                                          CST1[:, C1_SIN:C1_SIN + SEQ], ALU.mult).then_inc(rot_free.sem, 1)
                        dve.tensor_tensor(Z1[:, c, :], Z1[:, c, :], CST1[:, C1_COS:C1_COS + SEQ],
                                          ALU.mult).then_inc(rot_step.sem, 1)
                        dve.wait_ge(rot_step.sem, rot_step.next())
                        dve.wait_ge(rot_free.sem, rot_free.at(n + 1))
                        dve.tensor_tensor(Z1[:, c, :], Z1[:, c, :], HT[:], ALU.add).then_inc(rot_step.sem, 1)
                        dve.wait_ge(rot_step.sem, rot_step.next())
            done(vt_ps=5, vt_free=5, rot_ps=5, rot_free=5, own_done=4, conv_done=12, rot_step=10)

        def mix1_gates(VEC, l):
            abs_done, exp_done, ln_done, scans, gt_ps = (S("abs_done"), S("exp_done"), S("ln_done"),
                                                         S("scan_step"), S("gt_ps"))
            with block() as b:
                @b.vector
                def _(dve):
                    scan_step = S("scan_step")
                    dve.tensor_scalar(LI[0:4, :], Z1[0:4, GT1, :], VEC[0:4, V1_GI:V1_GI + 1], None, ALU.add)
                    dve.tensor_scalar(XF[0:4, :], PS[3][0:4, 0:SEQ], VEC[0:4, V1_GF:V1_GF + 1],
                                      None, ALU.add).then_inc(scan_step.sem, 1)
                    dve.wait_ge(scan_step.sem, scan_step.next())
                    dve.memset(ONE4[0:4, :], 1.0).then_inc(scan_step.sem, 1)
                    dve.wait_ge(scan_step.sem, scan_step.next())
                    dve.wait_ge(ln_done.sem, ln_done.at(1))
                    dve.scalar_tensor_tensor(out=XF[0:4, :], in0=XF[0:4, :], scalar=0.0,
                                             in1=AB[0:4, :], op0=ALU.min, op1=ALU.subtract).then_inc(scan_step.sem, 1)
                    dve.wait_ge(scan_step.sem, scan_step.next())
                    dve.tensor_tensor_scan(CUM[0:4, :], ONE4[0:4, :], XF[0:4, :], 0.0,
                                           ALU.mult, ALU.add).then_inc(scan_step.sem, 1)
                    dve.wait_ge(scan_step.sem, scan_step.next())
                    dve.tensor_tensor(GG[0:4, :], LI[0:4, :], CUM[0:4, :], ALU.subtract).then_inc(scan_step.sem, 1)
                    dve.wait_ge(scan_step.sem, scan_step.next())
                    dve.tensor_tensor_scan(MX[0:4, :], GG[0:4, :], GG[0:4, :], 0.0, ALU.max, ALU.max).then_inc(scan_step.sem, 1)
                    dve.wait_ge(scan_step.sem, scan_step.next())
                    dve.scalar_tensor_tensor(out=NM[0:4, :], in0=CUM[0:4, :], scalar=-1.0,
                                             in1=MX[0:4, :], op0=ALU.mult, op1=ALU.subtract).then_inc(scan_step.sem, 1)
                    dve.wait_ge(scan_step.sem, scan_step.next())
                    dve.wait_ge(gt_ps.sem, gt_ps.at(1))
                    dve.tensor_copy(GT, PS[3][:, SEQ:SEQ + 16])
                    dve.wait_ge(mod_turned.sem, mod_turned.at(GATE_TILES.stop // 3))
                    mod_add(dve, l, 0, GATE_TILES.stop, MOD_EARLY)

                @b.sync
                def _(sp):
                    mod_sync(sp, l, GATE_TILES)

                @b.scalar
                def _(act):
                    act.wait_ge(scans.sem, scans.at(1))
                    act.activation(AB[0:4, :], XF[0:4, :], ACT.Abs).then_inc(abs_done.sem, 1)
                    act.wait_ge(abs_done.sem, abs_done.at(1))
                    act.activation(AB[0:4, :], AB[0:4, :], ACT.Exp, scale=-1.0).then_inc(exp_done.sem, 1)
                    act.wait_ge(exp_done.sem, exp_done.at(1))
                    act.activation(AB[0:4, :], AB[0:4, :], ACT.Ln, bias=ONES[0:4, 0:1]).then_inc(ln_done.sem, 1)
                    for g in (2, 3, 4):
                        mod_copy(act, g, MOD_EARLY)

                @b.tensor
                def _(pe):
                    for g in (2, 3):
                        mod_turn(pe, g - 1, MOD_EARLY)
                        mod_rows(pe, g, MOD_EARLY)
                    pe.wait_ge(scans.sem, scans.at(5))
                    for i in range(4):
                        ins = pe.transpose(PS[3][:, SEQ + 4 * i:SEQ + 4 * i + 4],
                                           GG[0:4, i * P:i * P + P], IDENT[0:4, 0:4])
                    ins.then_inc(gt_ps.sem, 1)
                    mod_turn(pe, 3, MOD_EARLY)
                    mod_rows(pe, 4, MOD_EARLY)
                    mod_turn(pe, 4, MOD_EARLY)
            done(scan_step=7, abs_done=1, exp_done=1, ln_done=1, gt_ps=1)

        def mlstm(VEC, l):
            names = ("bc_ps", "em_done", "w_exp", "w_done", "s_ps", "p_done", "pv_done", "den_step",
                     "hsq_done", "hms_ps", "hln_done", "hrstd", "head_out")
            bc_ps, em_done, w_exp, w_done, s_ps, p_done, pv_done, den_step, hsq, hms, hln, hrstd, head_out = (
                S(n) for n in names)
            NB = SEQ // P
            N = 4 * NB
            with block() as b:
                @b.sync
                def _(sp):
                    mod_sync(sp, l, MLSTM_TILES)

                @b.tensor
                def _(pe):
                    def rows(h):
                        sel = CST1[0:4, C1_SELH + h * P:C1_SELH + (h + 1) * P]
                        if later(h):
                            pe.wait_ge(w_exp.sem, w_exp.at(NB * h))
                            pe.wait_ge(em_done.sem, em_done.at(h))
                        pe.matmul(PS[0][:, 0:SEQ], sel, MX[0:4, :], start=True, stop=True)
                        pe.matmul(PS[0][:, SEQ:], sel, NM[0:4, :], start=True,
                                  stop=True).then_inc(bc_ps.sem, 1)

                    def scores(n):
                        h, i = divmod(n, NB)
                        r, q = 64 * (h % 2), (i % 2) * SEQ
                        if later(n - 1):
                            pe.wait_ge(p_done.sem, p_done.at(n - 1))
                        pe.matmul(PS[1][:, q:q + SEQ - i * P], QK[r:r + 64, 2 + h // 2, i * P:i * P + P],
                                  QK[r:r + 64, h // 2, i * P:SEQ], start=True, stop=True).then_inc(s_ps.sem, 1)

                    def mean_square(h):
                        pe.wait_ge(hsq.sem, hsq.at(h + 1))
                        pe.matmul(PS[3][:, 0:SEQ], MEAN[:], HSQ, start=True, stop=True).then_inc(hms.sem, 1)

                    rows(0)
                    scores(0)
                    scores(1)
                    for n in range(N):
                        h, i = divmod(n, NB)
                        if i == 0:
                            if h:
                                mod_turn(pe, 4 + h, MOD_LATE)
                            mod_rows(pe, 5 + h, MOD_LATE)
                        pe.wait_ge(p_done.sem, p_done.at(n + 1))
                        if n + 2 < N:
                            scores(n + 2)
                        if i == 0 and later(h):
                            pe.wait_ge(den_step.sem, den_step.at(4 * h))
                        w = PT[i % 2][:, 0:SEQ - i * P]
                        pe.matmul(PS[2][:, i * P:SEQ], VT[:, i, h * P:h * P + P], w,
                                  start=(i == 0), stop=(i == NB - 1))
                        pe.matmul(PS[2][:, SEQ + i * P:], ONES[:], w,
                                  start=(i == 0), stop=(i == NB - 1)).then_inc(pv_done.sem, 1)
                        if i == 1 and h > 0:
                            mean_square(h - 1)
                        if i == 2 and h < 3:
                            rows(h + 1)
                    mod_turn(pe, 8, MOD_LATE)
                    mod_rows(pe, 9, MOD_LATE)
                    mean_square(3)

                @b.scalar
                def _(act):
                    def weights(h, i):
                        n = NB * h + i
                        if later(n - 1):
                            act.wait_ge(p_done.sem, p_done.at(n - 1))
                        act.activation(WT[i % 2][:, 0:SEQ - i * P], PS[0][:, i * P:SEQ], ACT.Exp,
                                       scale=-1.0, bias=GT[:, 4 * i + h:4 * i + h + 1]).then_inc(w_exp.sem, 1)

                    def head_rstd(h):
                        act.wait_ge(den_step.sem, den_step.at(4 * h + 4))
                        act.activation(HSQ, HT[:], ACT.Square).then_inc(hsq.sem, 1)
                        mod_copy(act, 6 + h, MOD_LATE)
                        act.wait_ge(hms.sem, hms.at(h + 1))
                        if later(h):
                            act.wait_ge(head_out.sem, head_out.at(2 * h - 1))
                        act.activation(RSTD[:, 0:SEQ], PS[3][:, 0:SEQ], ACT.Ln, scale=float(D // P),
                                       bias=EPSC[:, 0:1]).then_inc(hln.sem, 1)
                        act.wait_ge(hln.sem, hln.at(h + 1))
                        act.activation(RSTD[:, 0:SEQ], RSTD[:, 0:SEQ], ACT.Exp, scale=-0.5).then_inc(hrstd.sem, 1)

                    for h in range(4):
                        act.wait_ge(bc_ps.sem, bc_ps.at(h + 1))
                        if h > 1:
                            act.wait_ge(den_step.sem, den_step.at(4 * (h - 1)))
                        act.activation(EM[h % 2][:], PS[0][:, SEQ:], ACT.Exp).then_inc(em_done.sem, 1)
                        weights(h, 0)
                        weights(h, 1)
                        if h:
                            head_rstd(h - 1)
                        else:
                            mod_copy(act, 5, MOD_LATE)
                        weights(h, 2)
                        weights(h, 3)
                    head_rstd(3)

                @b.gpsimd
                def _(pool):
                    for n in range(N):
                        pool.wait_ge(w_exp.sem, w_exp.at(n + 1))
                        pool.affine_select(out=WT[n % 2][:, 0:P], in_=WT[n % 2][:, 0:P],
                                           compare_op=ALU.is_ge, fill=0.0, base=0, pattern=[[1, P]],
                                           channel_multiplier=-1).then_inc(w_done.sem, 1)

                @b.vector
                def _(dve):
                    def weigh(h, i):
                        n, q = NB * h + i, (i % 2) * SEQ
                        dve.wait_ge(s_ps.sem, s_ps.at(n + 1))
                        dve.wait_ge(w_done.sem, w_done.at(n + 1))
                        if later(n - 1):
                            dve.wait_ge(pv_done.sem, pv_done.at(n - 1))
                        dve.scalar_tensor_tensor(
                            out=PT[i % 2][:, 0:SEQ - i * P], in0=PS[1][:, q:q + SEQ - i * P], scalar=0.125,
                            in1=WT[i % 2][:, 0:SEQ - i * P], op0=ALU.mult, op1=ALU.mult).then_inc(p_done.sem, 1)

                    def divide(h):
                        dve.wait_ge(pv_done.sem, pv_done.at(NB * (h + 1)))
                        dve.wait_ge(em_done.sem, em_done.at(h + 1))
                        if later(h):
                            dve.wait_ge(hsq.sem, hsq.at(h))
                            dve.wait_ge(head_out.sem, head_out.at(2 * h))
                        dve.scalar_tensor_tensor(out=DEN, in0=PS[2][:, SEQ:], scalar=-1.0, in1=EM[h % 2][:],
                                                 op0=ALU.mult, op1=ALU.max).then_inc(den_step.sem, 1)
                        dve.wait_ge(den_step.sem, den_step.next())
                        dve.tensor_tensor(DEN, DEN, PS[2][:, SEQ:], ALU.max).then_inc(den_step.sem, 1)
                        dve.wait_ge(den_step.sem, den_step.next())
                        dve.reciprocal(DEN, DEN).then_inc(den_step.sem, 1)
                        dve.wait_ge(den_step.sem, den_step.next())
                        dve.tensor_tensor(HT[:], PS[2][:, 0:SEQ], DEN, ALU.mult).then_inc(den_step.sem, 1)
                        dve.wait_ge(den_step.sem, den_step.next())

                    def gate(h):
                        dve.wait_ge(hrstd.sem, hrstd.at(h + 1))
                        dve.scalar_tensor_tensor(out=DEN, in0=Z1[:, O1 + h, :],
                                                 scalar=VEC[:, V1_MH + h:V1_MH + h + 1], in1=RSTD[:, 0:SEQ],
                                                 op0=ALU.mult, op1=ALU.mult).then_inc(head_out.sem, 1)
                        dve.wait_ge(head_out.sem, head_out.at(2 * h + 1))
                        dve.tensor_tensor(Z1[:, V1 + h, :], HT[:], DEN, ALU.mult).then_inc(head_out.sem, 1)

                    for h in range(4):
                        weigh(h, 0)
                        if h:
                            divide(h - 1)
                        weigh(h, 1)
                        weigh(h, 2)
                        if h:
                            gate(h - 1)
                        weigh(h, 3)
                    divide(3)
                    gate(3)
            done(bc_ps=4, em_done=4, w_exp=16, w_done=16, s_ps=16, p_done=16, pv_done=16, den_step=16,
                 hsq_done=4, hms_ps=4, hln_done=4, hrstd=4, head_out=8)

        HSQ, DEN = SQ[0][:, 0:SEQ], SQ[1][:, 0:SEQ]

        def window_attention(VEC, l):
            names = ("s_ps", "masked", "max_step", "exp_done", "sink_exp", "norm_step", "pt_ps",
                     "pt_done", "pv_done", "o_done")
            s_ps, masked, max_step, exp_done, sink_exp, norm_step, pt_ps, pt_done, pv_done, o_done = (
                S(n) for n in names)
            units = [(n, kv) for n in range(4) for kv in range(2)]
            U = len(units)
            MXV = [SM[:, 32 + 16 * i:36 + 16 * i] for i in range(2)]
            SE = [SM[:, 36 + 16 * i:40 + 16 * i] for i in range(2)]
            SUMS = [SM[:, 40 + 16 * i:44 + 16 * i] for i in range(2)]
            with block() as b:
                @b.sync
                def _(sp):
                    mod_sync(sp, l, WINDOW_TILES)

                @b.tensor
                def _(pe):
                    def scores(u):
                        n, kv = units[u]
                        r = 64 * kv
                        if later(u - 1):
                            pe.wait_ge(masked.sem, masked.at(u - 1))
                        for j in range(4):
                            k0 = max(0, n - 1) * P
                            lo = 0 if n else P
                            ins = pe.matmul(PS[u % 2][:, j * PAIR + lo:(j + 1) * PAIR],
                                            Z1[r:r + 64, AQ1 + j, n * P:n * P + P],
                                            Z1[r:r + 64, AK1, k0:(n + 1) * P], start=True, stop=True)
                        ins.then_inc(s_ps.sem, 1)

                    def mixed(u):
                        n, kv = units[u]
                        r = 64 * kv
                        blocks = (0, 1) if n else (1,)
                        pe.wait_ge(pt_done.sem, pt_done.at(u + 1))
                        if later(u - 1):
                            pe.wait_ge(o_done.sem, o_done.at(u - 1))
                        for m in blocks:
                            ins = pe.matmul(PS[3][r:r + 64, 0:SEQ], AVT[:, n - 1 + m, r:r + 64],
                                            PTT[u % 2][:, m * SEQ:m * SEQ + SEQ],
                                            start=(m == blocks[0]), stop=(m == 1))
                        ins.then_inc(pv_done.sem, 1)

                    scores(0)
                    scores(1)
                    for u, (n, kv) in enumerate(units):
                        if u + 2 < U:
                            scores(u + 2)
                        if u < 6:
                            mod_turn(pe, 9 + u, MOD_LATE)
                            mod_rows(pe, 10 + u, MOD_LATE)
                        pe.wait_ge(norm_step.sem, norm_step.at(3 * u + 3))
                        if later(u):
                            pe.wait_ge(pt_done.sem, pt_done.at(u))
                        blocks = (0, 1) if n else (1,)
                        for m in blocks:
                            for j in range(4):
                                ins = pe.transpose(PS[2][:, m * SEQ + j * P:m * SEQ + j * P + P],
                                                   PW[u % 2][:, j, m * P:m * P + P], IDENT)
                        ins.then_inc(pt_ps.sem, 1)
                        if u:
                            mixed(u - 1)
                        if u == 6:
                            mod_turn(pe, 15, MOD_LATE)
                    mixed(U - 1)

                @b.scalar
                def _(act):
                    def turned(u):
                        act.wait_ge(pt_ps.sem, pt_ps.at(u + 1))
                        if later(u - 1):
                            act.wait_ge(pv_done.sem, pv_done.at(u - 1))
                        b0 = 0 if units[u][0] else SEQ
                        act.activation(PTT[u % 2][:, b0:], PS[2][:, b0:], ACT.Copy).then_inc(pt_done.sem, 1)

                    for u, (n, kv) in enumerate(units):
                        lo = 0 if n else P
                        act.wait_ge(max_step.sem, max_step.at(4 * u + 4))
                        for j in range(4):
                            ins = act.activation(PW[u % 2][:, j, lo:], PW[u % 2][:, j, lo:], ACT.Exp,
                                                 bias=MXV[u % 2][:, j:j + 1],
                                                 accum_out=SUMS[u % 2][:, j:j + 1])
                        ins.then_inc(exp_done.sem, 1)
                        act.activation(SE[u % 2], SE[u % 2], ACT.Exp).then_inc(sink_exp.sem, 1)
                        if u:
                            turned(u - 1)
                        if u < 6:
                            mod_copy(act, 10 + u, MOD_LATE)
                    turned(U - 1)

                @b.vector
                def _(dve):
                    max_step, norm_step = S("max_step"), S("norm_step")

                    def masked_max(u):
                        n, kv = units[u]
                        lo = 0 if n else P
                        sink = VEC[:, V1_SINK + 4 * kv:V1_SINK + 4 * kv + 4]
                        dve.wait_ge(s_ps.sem, s_ps.at(u + 1))
                        if later(u - 1):
                            dve.wait_ge(pt_ps.sem, pt_ps.at(u - 1))
                        mask = CST1[:, None, C1_MASK + lo:C1_MASK + PAIR].broadcast_to([P, 4, PAIR - lo])
                        dve.scalar_tensor_tensor(
                            out=PW[u % 2][:, :, lo:],
                            in0=PS[u % 2][:].rearrange("p (j s) -> p j s", j=4)[:, :, lo:],
                            scalar=0.125, in1=mask, op0=ALU.mult, op1=ALU.add).then_inc(masked.sem, 1)
                        dve.wait_ge(masked.sem, masked.at(u + 1))
                        dve.tensor_reduce(MXV[u % 2], PW[u % 2][:, :, lo:], AX.X, ALU.max).then_inc(max_step.sem, 1)
                        dve.wait_ge(max_step.sem, max_step.next())
                        dve.tensor_tensor(MXV[u % 2], MXV[u % 2], sink, ALU.max).then_inc(max_step.sem, 1)
                        dve.wait_ge(max_step.sem, max_step.next())
                        dve.tensor_scalar(MXV[u % 2], MXV[u % 2], -1.0, None, ALU.mult).then_inc(max_step.sem, 1)
                        dve.wait_ge(max_step.sem, max_step.next())
                        dve.tensor_tensor(SE[u % 2], MXV[u % 2], sink, ALU.add).then_inc(max_step.sem, 1)
                        dve.wait_ge(max_step.sem, max_step.next())

                    def store_rows(u):
                        n, kv = units[u]
                        r = 64 * kv
                        dve.wait_ge(pv_done.sem, pv_done.at(u + 1))
                        dve.tensor_copy(Z1[r:r + 64, AQ1:AQ1 + 4, n * P:n * P + P],
                                        PS[3][r:r + 64, 0:SEQ].rearrange("p (j q) -> p j q", j=4)
                                        ).then_inc(o_done.sem, 1)

                    masked_max(0)
                    for u, (n, kv) in enumerate(units):
                        lo = 0 if n else P
                        if u + 1 < U:
                            masked_max(u + 1)
                        dve.wait_ge(exp_done.sem, exp_done.at(u + 1))
                        dve.wait_ge(sink_exp.sem, sink_exp.at(u + 1))
                        dve.tensor_tensor(SUMS[u % 2], SUMS[u % 2], SE[u % 2], ALU.add).then_inc(norm_step.sem, 1)
                        dve.wait_ge(norm_step.sem, norm_step.next())
                        dve.reciprocal(SUMS[u % 2], SUMS[u % 2]).then_inc(norm_step.sem, 1)
                        dve.wait_ge(norm_step.sem, norm_step.next())
                        dve.tensor_tensor(PW[u % 2][:, :, lo:], PW[u % 2][:, :, lo:],
                                          SUMS[u % 2].unsqueeze(2).broadcast_to([P, 4, PAIR - lo]),
                                          ALU.mult).then_inc(norm_step.sem, 1)
                        dve.wait_ge(norm_step.sem, norm_step.next())
                        if u > 1:
                            store_rows(u - 2)
                    store_rows(U - 2)
                    store_rows(U - 1)
            done(s_ps=U, masked=U, max_step=4 * U, exp_done=U, sink_exp=U, norm_step=3 * U, pt_ps=U,
                 pt_done=U, pv_done=U, o_done=U, mod_done=MOD_N, mod_copied=MOD_N // 3, mod_turned=MOD_N // 3,
                 **{f"mod_in{i}": 16 * (MOD_N // RING) for i in range(RING)})

        PADX, PADC, PADN = 8, SEQ + 24, TOK + 32
        h2 = region(o_h, 2 * DC * TOK * 4)
        PP = [h2(f"PP{i}", [P, 2, PADN]) for i in range(5)]
        INV = h2("INV", [P, 2, TOK])
        PU = h2("PU", [P, 2, TOK])
        PWM = h2("PWM", [P, 2, P])

        st = region(o_stage, 6 * HALF * P * 4)
        VTN = st("VTN", [P, 10, 3 * P])
        CNM = st("CNM", [P, 4 * PAIR])
        QP = st("QP", [P, 3, TOK])

        def grid(z, rows, c0, cn):
            return z.rearrange("p (r g) -> p r g", g=GRID)[:, rows[0]:rows[1], c0:c0 + cn]

        def pooling_and_gather(tokens, VEC, layer):
            vt_ps, vt_free, vg_done, small_loaded = S("vt_ps"), S("vt_free"), S("vg_done"), S("small_loaded")
            VG = [SQ[i][:].rearrange("p (c r g) -> p c r g", c=3, r=8) for i in range(2)]
            pads, copied, psum, y_ps, o_done = (S("pads"), S("copied"), S("pool_step"), S("y_ps"), S("o_done"))
            rs = ranges(tokens)
            with block() as b:
                @b.gpsimd
                def _(pool):
                    pool.memset(PP[0][:], 0.0).then_inc(pads.sem, 1)

                @b.sync
                def _(sp):
                    for dst, src in ((INV[:], a["const_pool"]), (PWM[:], a["pool_w"][layer]), (CNM[:], a["const_na"])):
                        sp.dma_start(dst, src).then_inc(small_loaded.sem, 16)
                    sp.wait_ge(small_loaded.sem, small_loaded.at(48))

                @b.scalar
                def _(act):
                    def gather(k):
                        if later(2 * k - 2):
                            act.wait_ge(vt_ps.sem, vt_ps.at(2 * k - 2))
                        for c in range(3):
                            ins = act.activation(VG[k % 2][:, c], grid(Z[:, NV + c, 0:SEQ], (0, 8), COL0[k], SPAN),
                                                 ACT.Copy)
                        ins.then_inc(vg_done.sem, 1)
                    gather(0)
                    act.wait_ge(pads.sem, pads.at(1))
                    act.activation(PP[0][:, :, PADX:PADX + SEQ], Z[:, PO:PO + 2, 0:SEQ], ACT.Copy)
                    if tokens == TOK:
                        act.activation(PP[0][:, :, PADC:PADC + CTX], Z[:, PO:PO + 2, SEQ:TOK], ACT.Copy)
                    act.activation(ZERO[:], ZERO[:], ACT.Copy).then_inc(copied.sem, 1)
                    gather(1)
                    for g in range(10):
                        act.wait_ge(vt_ps.sem, vt_ps.at(g + 1))
                        act.activation(VTN[:, g, :], PS[g % 2][:, 0:3 * P], ACT.Copy).then_inc(vt_free.sem, 1)
                        if g % 2 and g // 2 + 2 < 4:
                            gather(g // 2 + 2)
                    for c in range(3):
                        for k in range(4):
                            act.activation(QP[:, c, k * P:k * P + P].rearrange("p (r g) -> p r g", r=8),
                                           grid(Z[:, NQ + c, 0:SEQ], (0, 8), 16 * k, 16), ACT.Copy, scale=0.125)
                    if tokens == TOK:
                        act.activation(QP[:, :, SEQ:TOK], Z[:, NQ:NQ + 3, SEQ:TOK], ACT.Copy, scale=0.125)
                    act.wait_ge(y_ps.sem, y_ps.at(2))
                    for c in range(2):
                        for t0, tn in rs:
                            act.activation(Z[:, PO + c, t0:t0 + tn], PS[2 + c][:, t0:t0 + tn], ACT.Copy,
                                           scale=VEC[:, V2_PS + c:V2_PS + c + 1])

                @b.vector
                def _(dve):
                    pool_step = S("pool_step")
                    dve.wait_ge(copied.sem, copied.at(1))
                    N = PADN
                    dve.tensor_tensor(PP[1][:, :, 1:N], PP[0][:, :, 0:N - 1], PP[0][:, :, 1:N], ALU.add).then_inc(pool_step.sem, 1)
                    dve.wait_ge(pool_step.sem, pool_step.next())
                    for i, d in ((2, 1), (3, 2), (4, 4)):
                        dve.tensor_tensor(PP[i][:, :, 2 * d:N - 2 * d + 1], PP[i - 1][:, :, d:N - 3 * d + 1],
                                          PP[i - 1][:, :, 3 * d:N - d + 1], ALU.add).then_inc(pool_step.sem, 1)
                        dve.wait_ge(pool_step.sem, pool_step.next())
                    dve.wait_ge(small_loaded.sem, small_loaded.at(48))
                    for c in range(2):
                        for half in range(2):
                            r = 64 * half
                            for t0, tn in rs:
                                p0 = PADX if t0 == 0 else PADC
                                dve.tensor_tensor(PU[r:r + 64, c, t0:t0 + tn],
                                                  PP[1 + 2 * c + half][r:r + 64, c, p0:p0 + tn],
                                                  INV[r:r + 64, c, t0:t0 + tn], ALU.mult).then_inc(pool_step.sem, 1)
                                dve.wait_ge(pool_step.sem, pool_step.next())
                    for c in range(2):
                        dve.tensor_tensor(PU[:, c, 0:tokens], PU[:, c, 0:tokens],
                                          Z[:, PO + c, 0:tokens], ALU.subtract).then_inc(pool_step.sem, 1)
                        dve.wait_ge(pool_step.sem, pool_step.next())

                @b.tensor
                def _(pe):
                    for g in range(10):
                        if later(g - 1):
                            pe.wait_ge(vt_free.sem, vt_free.at(g - 1))
                        pe.wait_ge(vg_done.sem, vg_done.at(min(g // 2 + 1, 4)))
                        for c in range(3):
                            if g < 8:
                                src = SQ[g // 2 % 2][:, c * PAIR + (g % 2) * P:c * PAIR + (g % 2) * P + P]
                            else:
                                src = Z[:, NV + c, SEQ + (g - 8) * P:SEQ + (g - 7) * P]
                            ins = pe.transpose(PS[g % 2][:, c * P:c * P + P], src, IDENT)
                        ins.then_inc(vt_ps.sem, 1)
                    pe.wait_ge(small_loaded.sem, small_loaded.at(48))
                    pe.wait_ge(psum.sem, psum.at(4 + 4 * len(rs) + 2))
                    for c in range(2):
                        for t0, tn in rs:
                            ins = pe.matmul(PS[2 + c][:, t0:t0 + tn], PWM[:, c, :], PU[:, c, t0:t0 + tn],
                                            start=True, stop=True)
                        ins.then_inc(y_ps.sem, 1)
            done(pads=1, copied=1, pool_step=4 + 4 * len(rs) + 2, y_ps=2, vt_ps=10, vt_free=10, vg_done=4,
                 small_loaded=48)

        h3 = region(o_h, 2 * DC * TOK * 4)
        BM = [h3(f"BM{i}", [P, 4 * PAIR]) for i in range(2)]
        PN = [h3(f"PN{i}", [P, SEQ]) for i in range(2)]
        PTN = [h3(f"PTN{i}", [P, SEQ]) for i in range(2)]
        CR = h3("CR", [P, CR_N])

        def neighborhood(bias, layer, tokens):
            kinds = 4 if tokens == SEQ else 6
            units = [(h, k) for h in range(NA_H) for k in range(kinds)]
            U = len(units)
            names = ("s_ps", "masked", "max_step", "exp_done", "norm_step", "pt_ps", "pt_done",
                     "pv_done", "o_done", "bias_done")
            s_ps, masked, max_step, exp_done, norm_step, pt_ps, pt_done, pv_done, o_done, bias_done = (
                S(n) for n in names)
            bias_in = [S("bias_in0"), S("bias_in1")]
            NMX = [SM[:, 32 + 16 * i:33 + 16 * i] for i in range(2)]
            SUMS = [SM[:, 40 + 16 * i:41 + 16 * i] for i in range(2)]
            local = lambda k: k < 4

            def score_bank(u):
                return PS[u % 2][:, u // 2 % 2 * SEQ:u // 2 % 2 * SEQ + SEQ]

            with block() as b:
                @b.sync
                def _(sp):
                    small_loaded = S("small_loaded")
                    for h in range(NA_H):
                        if h == 2:
                            sp.dma_start(CR[:], a["const_ret"]).then_inc(small_loaded.sem, 16)
                        if later(4 * (h - 1)):
                            sp.wait_ge(masked.sem, masked.at(4 * (h - 1)))
                        sp.dma_start(BM[h % 2][:], bias[layer * NA_H + h]).then_inc(bias_in[h % 2].sem, 16)
                    sp.wait_ge(small_loaded.sem, small_loaded.at(16))

                @b.gpsimd
                def _(pool):
                    for h in range(NA_H):
                        pool.wait_ge(bias_in[h % 2].sem, bias_in[h % 2].at(16 * (h // 2 + 1)))
                        pool.tensor_tensor(BM[h % 2][:], BM[h % 2][:], CNM[:], ALU.add).then_inc(bias_done.sem, 1)

                @b.tensor
                def _(pe):
                    def scores(u):
                        h, k = units[u]
                        r = 64 * (h % 2)
                        if later(u - 3):
                            pe.wait_ge(exp_done.sem, exp_done.at(u - 3))
                        if local(k):
                            q = QP[r:r + 64, h // 2, k * P:k * P + P]
                            pe.matmul(score_bank(u)[:, 0:PAIR].rearrange("p (a b) -> p a b", b=SPAN), q,
                                      grid(Z[r:r + 64, NK + h // 2, 0:SEQ], (0, 8), COL0[k], SPAN),
                                      start=True, stop=True)
                        else:
                            q = QP[r:r + 64, h // 2, SEQ + (k - 4) * P:SEQ + (k - 3) * P]
                        pe.matmul(score_bank(u)[:, PAIR:SEQ], q, Z[r:r + 64, NK + h // 2, SEQ:TOK],
                                  start=True, stop=True).then_inc(s_ps.sem, 1)

                    def mixed(u):
                        h, k = units[u]
                        r, o = 64 * (h % 2), u % 2 * SEQ
                        blocks = range(4) if local(k) else (2, 3)
                        pe.wait_ge(pt_done.sem, pt_done.at(u + 1))
                        if later(u - 1):
                            pe.wait_ge(o_done.sem, o_done.at(u - 1))
                        for m in blocks:
                            g = 2 * k + m if m < 2 else 6 + m
                            ins = pe.matmul(PS[3][r:r + 64, o:o + P], VTN[:, g, h * 64:h * 64 + 64],
                                            PTN[u % 2][:, m * P:m * P + P],
                                            start=(m == blocks[0]), stop=(m == 3))
                        ins.then_inc(pv_done.sem, 1)

                    scores(0)
                    scores(1)
                    for u, (h, k) in enumerate(units):
                        if u + 2 < U:
                            scores(u + 2)
                        pe.wait_ge(norm_step.sem, norm_step.at(2 * u + 2))
                        if later(u - 1):
                            pe.wait_ge(pt_done.sem, pt_done.at(u - 1))
                        blocks = range(4) if local(k) else (2, 3)
                        for m in blocks:
                            ins = pe.transpose(PS[2][:, u % 2 * SEQ + m * P:u % 2 * SEQ + m * P + P], PN[u % 2][:, m * P:m * P + P], IDENT)
                        ins.then_inc(pt_ps.sem, 1)
                        if u:
                            mixed(u - 1)
                    mixed(U - 1)

                @b.scalar
                def _(act):
                    def turned(u):
                        lo, o = (0 if local(units[u][1]) else PAIR), u % 2 * SEQ
                        act.wait_ge(pt_ps.sem, pt_ps.at(u + 1))
                        if later(u - 1):
                            act.wait_ge(pv_done.sem, pv_done.at(u - 1))
                        act.activation(PTN[u % 2][:, lo:], PS[2][:, o + lo:o + SEQ], ACT.Copy).then_inc(pt_done.sem, 1)

                    for u, (h, k) in enumerate(units):
                        lo = 0 if local(k) else PAIR
                        act.wait_ge(max_step.sem, max_step.at(u + 1))
                        if later(u - 1):
                            act.wait_ge(pt_ps.sem, pt_ps.at(u - 1))
                        act.activation(PN[u % 2][:, lo:], score_bank(u)[:, lo:SEQ], ACT.Exp, bias=NMX[u % 2],
                                       accum_out=SUMS[u % 2]).then_inc(exp_done.sem, 1)
                        if u:
                            turned(u - 1)
                    turned(U - 1)

                @b.vector
                def _(dve):
                    norm_step = S("norm_step")
                    def masked_max(u):
                        h, k = units[u]
                        lo = 0 if local(k) else PAIR
                        dve.wait_ge(s_ps.sem, s_ps.at(u + 1))
                        if local(k):
                            dve.wait_ge(bias_done.sem, bias_done.at(h + 1))
                            dve.tensor_tensor(score_bank(u)[:, 0:PAIR], score_bank(u)[:, 0:PAIR],
                                              BM[h % 2][:, k * PAIR:k * PAIR + PAIR],
                                              ALU.add).then_inc(masked.sem, 1)
                            dve.wait_ge(masked.sem, masked.at(4 * h + k + 1))
                        if later(u - 1):
                            dve.wait_ge(exp_done.sem, exp_done.at(u - 1))
                        dve.tensor_reduce(NMX[u % 2], score_bank(u)[:, lo:SEQ], AX.X, ALU.max,
                                          negate=True).then_inc(max_step.sem, 1)

                    def store_rows(u):
                        h, k = units[u]
                        o = u % 2 * SEQ
                        dve.wait_ge(pv_done.sem, pv_done.at(u + 1))
                        r = 64 * (h % 2)
                        if local(k):
                            dst = grid(Z[r:r + 64, NQ + h // 2, 0:SEQ], (0, 8), 16 * k, 16)
                            src = PS[3][r:r + 64, o:o + P].rearrange("p (r c) -> p r c", c=16)
                        else:
                            dst = Z[r:r + 64, NQ + h // 2, SEQ + (k - 4) * P:SEQ + (k - 3) * P]
                            src = PS[3][r:r + 64, o:o + P]
                        dve.tensor_copy(dst, src).then_inc(o_done.sem, 1)

                    masked_max(0)
                    for u, (h, k) in enumerate(units):
                        if u + 1 < U:
                            masked_max(u + 1)
                        lo = 0 if local(k) else PAIR
                        dve.wait_ge(exp_done.sem, exp_done.at(u + 1))
                        dve.reciprocal(SUMS[u % 2], SUMS[u % 2]).then_inc(norm_step.sem, 1)
                        dve.wait_ge(norm_step.sem, norm_step.next())
                        dve.tensor_scalar(PN[u % 2][:, lo:], PN[u % 2][:, lo:], SUMS[u % 2], None, ALU.mult).then_inc(norm_step.sem, 1)
                        dve.wait_ge(norm_step.sem, norm_step.next())
                        if u > 1:
                            store_rows(u - 2)
                    store_rows(U - 2)
                    store_rows(U - 1)
            done(s_ps=U, masked=24, max_step=U, exp_done=U, norm_step=2 * U, pt_ps=U, pt_done=U,
                 pv_done=U, o_done=U, bias_done=NA_H, bias_in0=48, bias_in1=48, small_loaded=16)

        h4 = region(o_h, 16 * P * 8)
        VR = h4("VR", [P, 6, 3 * P])
        KR = h4("KR", [P, 2, 3 * P])
        KD = [h4(f"KD{i}", [P, 4, 64]) for i in range(2)]
        ST = [h4(f"ST{i}", [P, 2, 64]) for i in range(2)]
        after_cr = 16 * P * 8 + (4 * CR_N + 31) // 32 * 32
        h5 = region(o_h + after_cr, 2 * DC * TOK * 4 - after_cr)
        STRIP = [h5(f"STRIP{i}", [P, 7 * P]) for i in range(2)]
        BACK = h5("BACK", [P, P])
        QD = [h5(f"QD{i}", [P, 2, SEQ]) for i in range(2)]
        PR = [sb(f"PR{i}", [P, SEQ], offset=o_stage + i * SEQ * 4) for i in range(2)]
        ROT = sb("ROT", [P, SEQ], offset=o_tmp)
        KDEC = [SM[:, 80:84], SM[:, 84:88]]

        def retention(tokens, VEC):
            rot_ps, rot_free, vt_ps, vt_free = S("rot_ps"), S("rot_free"), S("vt_ps"), S("vt_free")
            rope = [RQ, RQ + 1, RQ + 2, RK, RK + 1, RK + 2]
            jobs = [(VR[:, g, :], RV, g * P) for g in range(6)] + [(KR[:, g, :], RK, SEQ + g * P) for g in range(2)]
            with block() as b:
                @b.tensor
                def _(pe):
                    for n, c in enumerate(rope):
                        if later(n - 1):
                            pe.wait_ge(rot_free.sem, rot_free.at(n - 1))
                        pe.matmul(PS[n % 2 + 2][:, 0:SEQ], RROT, Z[:, c, 0:SEQ],
                                  start=True, stop=True).then_inc(rot_ps.sem, 1)
                    for g, (_, chunk, t0) in enumerate(jobs):
                        if later(g - 1):
                            pe.wait_ge(vt_free.sem, vt_free.at(g - 1))
                        for c in range(3):
                            ins = pe.transpose(PS[g % 2][:, c * P:c * P + P], Z[:, chunk + c, t0:t0 + P], IDENT)
                        ins.then_inc(vt_ps.sem, 1)

                @b.scalar
                def _(act):
                    for g, (dst, _, _) in enumerate(jobs):
                        act.wait_ge(vt_ps.sem, vt_ps.at(g + 1))
                        act.activation(dst, PS[g % 2][:, 0:3 * P], ACT.Copy).then_inc(vt_free.sem, 1)

                @b.vector
                def _(dve):
                    rot_step = S("rot_step")
                    for n, c in enumerate(rope):
                        dve.wait_ge(rot_ps.sem, rot_ps.at(n + 1))
                        dve.tensor_tensor(ROT[:], PS[n % 2 + 2][:, 0:SEQ], CR[:, CR_SIN:CR_SIN + SEQ],
                                          ALU.mult).then_inc(rot_free.sem, 1)
                        dve.tensor_tensor(Z[:, c, 0:SEQ], Z[:, c, 0:SEQ], CR[:, CR_COS:CR_COS + SEQ],
                                          ALU.mult).then_inc(rot_step.sem, 1)
                        dve.wait_ge(rot_step.sem, rot_step.next())
                        dve.wait_ge(rot_free.sem, rot_free.at(n + 1))
                        dve.tensor_tensor(Z[:, c, 0:SEQ], Z[:, c, 0:SEQ], ROT[:], ALU.add).then_inc(rot_step.sem, 1)
                        dve.wait_ge(rot_step.sem, rot_step.next())
            done(rot_ps=6, rot_free=6, vt_ps=8, vt_free=8, rot_step=12)

            NB = SEQ // P
            per = NB + (2 if tokens == TOK else 0)
            names = ("decay_exp", "decay_step", "st_ps", "s_ps", "p_done", "pv_done", "y_done")
            decay_exp, decay_step, st_ps, s_ps, p_done, pv_done, y_done = (S(n) for n in names)
            DSTEPS = 3 + 4 + 2 + 2
            N = RET_H * per
            with block() as b:
                @b.scalar
                def _(act):
                    for h in range(RET_H):
                        lf, lb = VEC[:, V2_LF + h:V2_LF + h + 1], VEC[:, V2_LB + h:V2_LB + h + 1]
                        strip, qd, kdec = STRIP[h % 2], QD[h % 2], KDEC[h % 2]
                        if h:
                            act.wait_ge(decay_step.sem, decay_step.at(DSTEPS * (h - 1) + 3))
                        if h > 1:
                            act.wait_ge(p_done.sem, p_done.at(per * (h - 1)))
                            act.wait_ge(y_done.sem, y_done.at(h - 1))
                        act.activation(strip[:, 3 * P:], CR[:, CR_DP:CR_DP + SEQ], ACT.Exp, scale=lf)
                        act.activation(strip[:, 0:3 * P], CR[:, CR_DN:CR_DN + 3 * P], ACT.Exp, scale=lb)
                        act.activation(BACK[:], CR[:, CR_DN + 3 * P:CR_DN + SEQ], ACT.Exp, scale=lb)
                        act.activation(qd[:, 0, :], CR[:, CR_QF:CR_QF + SEQ], ACT.Exp, scale=lf)
                        act.activation(qd[:, 1, :], CR[:, CR_QB:CR_QB + SEQ], ACT.Exp, scale=lb)
                        act.activation(kdec[:, 0:2], CR[:, CR_KE:CR_KE + 2], ACT.Exp, scale=lf)
                        act.activation(kdec[:, 2:4], CR[:, CR_KE + 2:CR_KE + 4], ACT.Exp,
                                       scale=lb).then_inc(decay_exp.sem, 1)

                @b.tensor
                def _(pe):
                    def states(h):
                        r = 64 * (h % 2)
                        pe.wait_ge(decay_step.sem, decay_step.at(DSTEPS * h + 9))
                        for d in range(2):
                            for g in range(2):
                                ins = pe.matmul(PS[3][r:r + 64, SEQ + 64 * d:SEQ + 64 * d + 64],
                                                KD[h % 2][:, 2 * d + g, :], VR[:, NB + g, h * 64:h * 64 + 64],
                                                start=(g == 0), stop=(g == 1))
                        ins.then_inc(st_ps.sem, 1)

                    def scores(n):
                        h, i = divmod(n, per)
                        r, c = 64 * (h % 2), h // 2
                        if later(n - 1):
                            pe.wait_ge(p_done.sem, p_done.at(n - 1))
                        t0, tn, kb = (0, SEQ, i) if i < NB else (SEQ, CTX, i - NB)
                        pe.matmul(PS[n % 2][:, 0:tn], Z[r:r + 64, RK + c, t0 + kb * P:t0 + kb * P + P],
                                  Z[r:r + 64, RQ + c, t0:t0 + tn], start=True, stop=True).then_inc(s_ps.sem, 1)

                    states(0)
                    scores(0)
                    for n in range(N):
                        h, i = divmod(n, per)
                        r = 64 * (h % 2)
                        if n + 1 < N:
                            scores(n + 1)
                        if i == 0:
                            pe.wait_ge(decay_step.sem, decay_step.at(DSTEPS * (h + 1)))
                            if later(h - 1):
                                pe.wait_ge(y_done.sem, y_done.at(h - 1))
                            for d in range(2):
                                pe.matmul(PS[2][r:r + 64, 0:SEQ], ST[h % 2][r:r + 64, d, :],
                                          QD[h % 2][r:r + 64, d, :], start=(d == 0), stop=False)
                        pe.wait_ge(p_done.sem, p_done.at(n + 1))
                        dst, tn = (PS[2][r:r + 64, 0:SEQ], SEQ) if i < NB else (PS[2][r:r + 64, SEQ:SEQ + CTX], CTX)
                        pe.matmul(dst, VR[:, i, h * 64:h * 64 + 64], PR[n % 2][:, 0:tn],
                                  start=(i == NB), stop=(i == NB - 1 or i == per - 1)).then_inc(pv_done.sem, 1)
                        if i == 2 and h + 1 < RET_H:
                            states(h + 1)

                @b.vector
                def _(dve):
                    def decays(h):
                        r, c = 64 * (h % 2), h // 2
                        strip, qd, kd = STRIP[h % 2], QD[h % 2], KD[h % 2]
                        mid = strip[:, 3 * P:4 * P]
                        dve.wait_ge(decay_exp.sem, decay_exp.at(h + 1))
                        dve.tensor_tensor(mid, mid, CR[:, CR_MF:CR_MF + P], ALU.mult).then_inc(decay_step.sem, 1)
                        dve.tensor_tensor(BACK[:], BACK[:], CR[:, CR_MB:CR_MB + P],
                                          ALU.mult).then_inc(decay_step.sem, 1)
                        dve.wait_ge(decay_step.sem, decay_step.at(DSTEPS * h + 2))
                        dve.tensor_tensor(mid, mid, BACK[:], ALU.add).then_inc(decay_step.sem, 1)
                        for d in range(2):
                            for g in range(2):
                                dve.tensor_scalar(kd[:, 2 * d + g, :], KR[:, g, h * 64:h * 64 + 64],
                                                  KDEC[h % 2][:, 2 * d + g:2 * d + g + 1], 0.125,
                                                  ALU.mult, ALU.mult).then_inc(decay_step.sem, 1)
                        for d in range(2):
                            dve.tensor_tensor(qd[r:r + 64, d, :], qd[r:r + 64, d, :], Z[r:r + 64, RQ + c, 0:SEQ],
                                              ALU.mult).then_inc(decay_step.sem, 1)

                    def keep_states(h):
                        r = 64 * (h % 2)
                        dve.wait_ge(st_ps.sem, st_ps.at(h + 1))
                        for d in range(2):
                            dve.tensor_copy(ST[h % 2][r:r + 64, d, :],
                                            PS[3][r:r + 64, SEQ + 64 * d:SEQ + 64 * d + 64]
                                            ).then_inc(decay_step.sem, 1)

                    decays(0)
                    keep_states(0)
                    for n in range(N):
                        h, i = divmod(n, per)
                        r, c = 64 * (h % 2), h // 2
                        dve.wait_ge(decay_step.sem, decay_step.at(DSTEPS * h + 3))
                        dve.wait_ge(s_ps.sem, s_ps.at(n + 1))
                        if later(n - 1):
                            dve.wait_ge(pv_done.sem, pv_done.at(n - 1))
                        tn, kb = (SEQ, i) if i < NB else (CTX, i - NB)
                        dve.scalar_tensor_tensor(out=PR[n % 2][:, 0:tn], in0=PS[n % 2][:, 0:tn], scalar=0.125,
                                                 in1=STRIP[h % 2][:, (3 - kb) * P:(3 - kb) * P + tn],
                                                 op0=ALU.mult, op1=ALU.mult).then_inc(p_done.sem, 1)
                        if i == 1 and h + 1 < RET_H:
                            decays(h + 1)
                        if i == 3 and h + 1 < RET_H:
                            keep_states(h + 1)
                        if i == per - 1:
                            dve.wait_ge(pv_done.sem, pv_done.at(per * (h + 1)))
                            if tokens == TOK:
                                dve.tensor_copy(Z[r:r + 64, RQ + c, SEQ:TOK], PS[2][r:r + 64, SEQ:SEQ + CTX])
                            dve.tensor_copy(Z[r:r + 64, RQ + c, 0:SEQ],
                                            PS[2][r:r + 64, 0:SEQ]).then_inc(y_done.sem, 1)
            U = per * RET_H
            done(decay_exp=RET_H, decay_step=DSTEPS * RET_H, st_ps=RET_H, s_ps=U, p_done=U, pv_done=U, y_done=RET_H)

            mean_ps, centred, sq_done, var_ps, ln_done, rstd, out_step = (
                S("mean_ps"), S("centred"), S("sq_done"), S("var_ps"), S("log_done"), S("rstd_done"), S("out_step"))
            rs = ranges(tokens)
            R = [SQ[0], SQ[1], RSTD]
            with block() as b:
                @b.tensor
                def _(pe):
                    for c in range(3):
                        for t0, tn in rs:
                            ins = pe.matmul(PS[c][:, t0:t0 + tn], BLK, Z[:, RQ + c, t0:t0 + tn], start=True, stop=True)
                        ins.then_inc(mean_ps.sem, 1)
                    for c in range(3):
                        pe.wait_ge(sq_done.sem, sq_done.at(c + 1))
                        for t0, tn in rs:
                            ins = pe.matmul(PS[c][:, t0:t0 + tn], BLK, R[c][:, t0:t0 + tn], start=True, stop=True)
                        ins.then_inc(var_ps.sem, 1)

                @b.scalar
                def _(act):
                    act.activation(Z[:, RG:RG + 3, 0:tokens], Z[:, RG:RG + 3, 0:tokens], ACT.Silu)
                    for c in range(3):
                        act.wait_ge(centred.sem, centred.at(c + 1))
                        act.activation(R[c][:, 0:tokens], Z[:, RQ + c, 0:tokens], ACT.Square).then_inc(sq_done.sem, 1)
                    for c in range(3):
                        act.wait_ge(var_ps.sem, var_ps.at(c + 1))
                        act.activation(R[c][:, 0:tokens], PS[c][:, 0:tokens], ACT.Ln,
                                       bias=EPSC[:, 0:1]).then_inc(ln_done.sem, 1)
                    for c in range(3):
                        act.wait_ge(ln_done.sem, ln_done.at(c + 1))
                        act.activation(R[c][:, 0:tokens], R[c][:, 0:tokens], ACT.Exp, scale=-0.5).then_inc(rstd.sem, 1)

                @b.vector
                def _(dve):
                    out_step = S("out_step")
                    for c in range(3):
                        dve.wait_ge(mean_ps.sem, mean_ps.at(c + 1))
                        dve.tensor_tensor(Z[:, RQ + c, 0:tokens], Z[:, RQ + c, 0:tokens], PS[c][:, 0:tokens],
                                          ALU.subtract).then_inc(centred.sem, 1)
                    for c in range(3):
                        dve.wait_ge(rstd.sem, rstd.at(c + 1))
                        dve.scalar_tensor_tensor(out=Z[:, RQ + c, 0:tokens], in0=Z[:, RQ + c, 0:tokens],
                                                 scalar=VEC[:, V2_GN + c:V2_GN + c + 1],
                                                 in1=R[c][:, 0:tokens], op0=ALU.mult, op1=ALU.mult).then_inc(out_step.sem, 1)
                        dve.wait_ge(out_step.sem, out_step.next())
                        dve.tensor_tensor(Z[:, RG + c, 0:tokens], Z[:, RG + c, 0:tokens],
                                          Z[:, RQ + c, 0:tokens], ALU.mult).then_inc(out_step.sem, 1)
                        dve.wait_ge(out_step.sem, out_step.next())
            done(mean_ps=3, centred=3, sq_done=3, var_ps=3, log_done=3, rstd_done=3, out_step=6)

        with block() as b:
            @b.gpsimd
            def _(pool):
                filled = S("filled")
                pool.memset(ONES[:], 1.0).then_inc(filled.sem, 1)
                pool.wait_ge(filled.sem, filled.next())
                pool.memset(MEAN[:], 1.0 / D).then_inc(filled.sem, 1)
                pool.wait_ge(filled.sem, filled.next())
                pool.memset(EPSC[:], EPS).then_inc(filled.sem, 1)
                pool.wait_ge(filled.sem, filled.next())
                pool.memset(ZERO[:], 0.0).then_inc(filled.sem, 1)
                pool.wait_ge(filled.sem, filled.next())
        load([(CS[:], a["consts"]), (CST1[:], a["const1"]), (X[:, :, 0:SEQ], a["x"]), (X[:, :, SEQ:TOK], a["ctx"]),
              (CC[:], a["cond"]), (FIN[:], a["final"])]
             + [(VEC1[l][:], a["vec1"][l]) for l in range(DEPTH)] + [(VEC2[l][:], a["vec2"][l]) for l in range(DEPTH)])

        with block() as b:
            @b.scalar
            def _(act):
                act.activation(SC[:], CC[:], ACT.Silu)

        def zero(c, st):
            return ZERO[:, 0:1]

        def store(z, tokens, first=0):
            def put(act, t, acc):
                return act.activation(z[:, at(t + first), 0:tokens].rearrange("p a t -> p (a t)"),
                                      acc[:, 0:tokens], ACT.Copy)
            return put

        def chunk(rows, t, tokens):
            return rows[:, at(t), 0:tokens].rearrange("p a t -> p (a t)")

        def to_y(dve, t, acc):
            return dve.tensor_copy(chunk(Y, t, SEQ), acc[:, 0:SEQ])

        def add_y(dve, t, acc):
            return dve.tensor_tensor(chunk(Y, t, SEQ), chunk(Y, t, SEQ), acc[:, 0:SEQ], ALU.add)

        def column(vec, first):
            return lambda c, st=0: vec[:, first + c:first + c + 1]

        for l in range(DEPTH):
            VEC = VEC1[l]
            gain = column(VEC1[l - 1], V1_POSTF) if l else None
            normed_stream([Segment(a["w_in"], l * N1, N1, DC, HH, HL, SEQ, out_act=store(Z1, SEQ))],
                          SEQ, column(VEC, V1_PRE), zero, fresh=True, gain=gain)
            mix1_prepare(VEC, l)
            mix1_gates(VEC, l)
            mlstm(VEC, l)
            window_attention(VEC, l)
            mod_out(l)
            split_stream(Z1, [V1, V1 + 1, V1 + 2, V1 + 3, AQ1, AQ1 + 1, AQ1 + 2, AQ1 + 3], SEQ,
                         [Segment(a["w_out"], l * DC, DC, DC, HH, HL, SEQ, out_dve=to_y,
                                  squares=lambda t: chunk(Y, t, SEQ))])
            segments = []
            for half in range(2):
                segments += [
                    Segment(a["w_up"], (2 * l + half) * 2 * HALF, 2 * HALF, DC, HH, HL, SEQ, kind="hidden",
                            half=half, gh=GH1, gl=GL1, own=2, others=((1, 1), (0, 2)), vec=VEC,
                            tap_col=V1_FCW, bias_col=None),
                    Segment(a["w_down"], (2 * l + half) * DC, DC, HALF, GH1, GL1, SEQ,
                            ready=(g_lo, half * HALF), out_dve=add_y if half else to_y,
                            squares=(lambda t: chunk(Y, t, SEQ)) if half else None)]
            normed_stream(segments, SEQ, column(VEC, V1_PREF), zero, gain=column(VEC, V1_POST))

        for l in range(DEPTH):
            VEC, MOD, A1, A2 = VEC2[l], MODS[l], A1S[l], A2S[l]
            tokens = TOK if l < DEPTH - 1 else SEQ

            def mod(which):
                return lambda c, st: MOD[:, at(c + which * DC), st]

            def gated_by(which):
                def put(dve, t, acc):
                    for st, (t0, tn) in enumerate(ranges(tokens)):
                        x = X[:, at(t), t0:t0 + tn].rearrange("p a t -> p (a t)")
                        ins = dve.scalar_tensor_tensor(out=x, in0=acc[:, t0:t0 + tn], scalar=mod(which)(t, st),
                                                       in1=x, op0=ALU.mult, op1=ALU.add)
                    return ins
                return put

            if l == 0:
                update_x(column(VEC1[DEPTH - 1], V1_POSTF))
            normed_stream([Segment(a["w_in2"], l * N2, N2_KV, DC, HH, HL, TOK, out_act=store(Z, TOK)),
                           Segment(a["w_in2"], l * N2 + N2_KV, N2 - N2_KV, DC, HH, HL, tokens,
                                   out_act=store(Z, tokens, N2_KV))],
                          TOK, lambda c, st: A1[:, c, st:st + 1], mod(0), fresh=(l == 0))
            pooling_and_gather(tokens, VEC, l)
            neighborhood(a["na_bias"], l, tokens)
            retention(tokens, VEC)
            x_rows = lambda t: chunk(X, t, tokens)
            split_stream(Z, [PO, PO + 1, NQ, NQ + 1, NQ + 2, RG, RG + 1, RG + 2], tokens,
                         [Segment(a["w_out2"], l * DC, DC, DC, HH, HL, tokens, out_dve=gated_by(2), squares=x_rows)])
            segments = []
            for half in range(2):
                segments += [
                    Segment(a["w_up2"], (2 * l + half) * 2 * HALF, 2 * HALF, DC, HH, HL, tokens, kind="hidden",
                            half=half, gh=GH, gl=GL, own=1, others=((0, 1), (2, -1)), vec=VEC,
                            tap_col=V2_CW, bias_col=V2_CB),
                    Segment(a["w_down2"], (2 * l + half) * DC, DC, HALF, GH, GL, tokens,
                            ready=(g_lo, half * HALF), out_dve=gated_by(5), squares=x_rows if half else None)]
            normed_stream(segments, tokens, lambda c, st: A2[:, c, st:st + 1], mod(3))

        fin, out_stored = S("fin"), S("out_stored")
        with block() as b:
            @b.scalar
            def _(act):
                rstd_act(act, 1, SEQ, 0)

            @b.vector
            def _(dve):
                dve.wait_ge(rstd_done.sem, rstd_done.at(1))
                for c in range(DC):
                    dve.scalar_tensor_tensor(out=X[:, c, 0:SEQ], in0=X[:, c, 0:SEQ], scalar=FIN[:, c:c + 1],
                                             in1=RSTD[:, 0:SEQ], op0=ALU.mult, op1=ALU.mult).then_inc(fin.sem, 1)

            @b.sync
            def _(sp):
                for c in range(DC):
                    sp.wait_ge(fin.sem, fin.at(c + 1))
                    sp.dma_start(out[:, c, :], X[:, c, 0:SEQ]).then_inc(out_stored.sem, 16)
                sp.wait_ge(out_stored.sem, 16 * DC)


def constants():
    f = np.float32
    i = np.arange(P)
    small = np.zeros((P, C_SMALL), f)
    small[:, C_ID:C_ID + P] = np.eye(P)
    small[:, C_BLK:C_BLK + P] = (i[:, None] // 64 == i[None, :] // 64) / 64.0

    def partner(size):
        m = np.zeros((P, P), f)
        for p in range(P):
            if p % size < size // 2:
                m[p + size // 2, p] = -1
            else:
                m[p - size // 2, p] = 1
        return m
    small[:, C_RR:C_RR + P] = partner(32)

    c1 = np.zeros((P, C1_N), f)
    s = np.arange(PAIR)
    diff = i[:, None] + P - s[None, :]
    c1[:, C1_MASK:C1_MASK + PAIR] = np.where((diff >= 0) & (diff < P), 0, -1e30)
    t = np.arange(SEQ, dtype=f)
    inv = (1.0 / (10000.0 ** (np.arange(0, 64, 2, dtype=f) / f(64)))).astype(f)
    ang = (t[None, :] * inv[i % 32][:, None]).astype(f)
    c1[:, C1_COS:C1_COS + SEQ] = np.cos(ang)
    c1[:, C1_SIN:C1_SIN + SEQ] = np.sin(ang)
    c1[:, C1_RP:C1_RP + P] = partner(64)
    for h in range(4):
        c1[32 + h, C1_SELF + h] = 1
        c1[h, C1_SELH + h * P:C1_SELH + (h + 1) * P] = 1

    pool = np.zeros((P, 2, TOK), f)
    for g, w in enumerate((2, 4, 8, 16)):
        rows = slice(64 * (g % 2), 64 * (g % 2) + 64)
        for t0, n in ((0, SEQ), (SEQ, CTX)):
            tt = np.arange(n)
            count = np.clip(tt - w // 2 + w, 0, n) - np.clip(tt - w // 2, 0, n)
            pool[rows, g // 2, t0:t0 + n] = 1.0 / count

    na = np.zeros((P, 4, 8, SPAN), f)
    for k in range(4):
        col = 16 * k + i % 16
        first = np.clip(col - 8, 0, GRID - 16)
        key = COL0[k] + np.arange(SPAN)
        ok = (key[None, :] >= first[:, None]) & (key[None, :] < first[:, None] + 16)
        na[:, k] = np.where(ok, 0, -1e30)[:, None, :]

    cr = np.zeros((P, CR_N), f)
    inv = (10000.0 ** (-np.arange(16, dtype=f) / f(16))).astype(f)
    tt = np.arange(SEQ)
    pos = np.where((i % 64 < 32)[:, None], (tt // GRID)[None, :], (tt % GRID)[None, :]).astype(f)
    ang = (pos * inv[i % 16][:, None]).astype(f)
    cr[:, CR_COS:CR_COS + SEQ] = np.cos(ang)
    cr[:, CR_SIN:CR_SIN + SEQ] = np.sin(ang)
    cr[:, CR_DP:CR_DP + SEQ] = np.maximum(tt[None, :] - i[:, None], 0)
    cr[:, CR_DN:CR_DN + SEQ] = np.maximum(i[:, None] - (tt[None, :] - 3 * P), 0)
    cr[:, CR_QF:CR_QF + SEQ] = tt + 1
    cr[:, CR_QB:CR_QB + SEQ] = SEQ - tt
    cr[:, CR_MF:CR_MF + P] = i[None, :] >= i[:, None]
    cr[:, CR_MB:CR_MB + P] = i[None, :] <= i[:, None]
    for g in range(2):
        cr[:, CR_KE + g] = CTX - 1 - (g * P + i)
        cr[:, CR_KE + 2 + g] = g * P + i
    return small, c1, pool, na.reshape(P, 4 * PAIR), cr


def lay_out(v):
    out = {}

    def tiles(w):
        k, m = w.shape
        return w.reshape(k // P, P, m // P, P).transpose(2, 1, 0, 3).reshape(m // P, P, k)

    def cols(x):
        return x.reshape(-1, P).T

    small, c1, pool, na, cr = constants()
    out.update(consts=small, const1=c1, const_pool=pool, const_na=na, const_ret=cr)
    feature = lambda x: x.T.reshape(DC, P, -1).transpose(1, 0, 2)
    out["x"] = feature(v["x"][0])
    out["ctx"] = feature(v["ctx_2"][0])
    out["cond"] = np.stack([cols(v["c_2"][0]), cols(v["c_ctx_2"])], axis=2)

    o = np.cumsum([0, 256, 256, 512, 512, 8, 512, 128, 128])
    head_rows = np.concatenate([np.arange(64) + 64 * h for j in range(4) for h in (j, 4 + j)])
    order = np.concatenate([np.arange(o[0], o[4]), o[5] + head_rows, np.arange(o[6], o[8])])
    w_in, w_out, w_up, w_down, vec = [], [], [], [], []
    for l in range(DEPTH):
        w = v["w_in"][l]
        gates = np.zeros((D, P), np.float32)
        gates[:, 0:4], gates[:, 32:36] = w[:, o[4]:o[4] + 4], w[:, o[4] + 4:o[5]]
        w_in.append(tiles(np.concatenate([w[:, order], gates], axis=1)))
        rows = np.concatenate([np.arange(512), 512 + head_rows])
        w_out.append(tiles(v["w_out"][l][rows]))
        w_up.append(up_tiles(v["w_up"][l], tiles))
        w_down.append(down_tiles(v["w_down"][l]))
        q = np.zeros((P, V1_N), np.float32)
        q[:, V1_PRE:V1_PRE + 8] = cols(v["g_pre_mix"][l])
        q[:, V1_CW:V1_CW + 16] = v["qk_conv_w"][l].reshape(4, 4, P).transpose(2, 1, 0).reshape(P, 16)
        q[:, V1_CB:V1_CB + 4] = cols(v["qk_conv_b"][l])
        q[0:4, V1_GI], q[0:4, V1_GF] = v["gate_bias"][l][0:4], v["gate_bias"][l][4:8]
        q[:, V1_MH:V1_MH + 4] = cols(v["mh_norm_g"][l])
        q[:, V1_SINK:V1_SINK + 8] = v["attn_sinks"][l][None, :]
        q[:, V1_POST:V1_POST + 8] = cols(v["g_post_mix"][l])
        q[:, V1_PREF:V1_PREF + 8] = cols(v["g_pre_ffn"][l])
        q[:, V1_FCW:V1_FCW + 132] = taps(v["ffn_conv_w"][l])
        q[:, V1_POSTF:V1_POSTF + 8] = cols(v["g_post_ffn"][l])
        vec.append(q)
    out.update(w_in=np.concatenate(w_in), w_out=np.concatenate(w_out), w_up=np.concatenate(w_up),
               w_down=np.concatenate(w_down), vec1=np.stack(vec))

    o = np.cumsum([0, 256, 384, 384, 384, 384, 384, 384, 384])
    part = lambda n: np.arange(o[n], o[n + 1])
    order = np.concatenate([part(n) for n in (2, 3, 5, 6, 0, 1, 4, 7)])
    w_in, w_out, w_up, w_down, w_mod, vec, pw, bias = [], [], [], [], [], [], [], []
    r, c = np.arange(P) // 16, np.arange(P) % 16
    for l in range(DEPTH):
        w_in.append(tiles(v["w_in_2"][l][:, order]))
        w_out.append(tiles(v["w_out_2"][l]))
        w_mod.append(tiles(v["w_mod_2"][l]))
        w_up.append(up_tiles(v["w_up_2"][l], tiles))
        w_down.append(down_tiles(v["w_down_2"][l]))
        q = np.zeros((P, V2_N), np.float32)
        q[:, V2_BM:V2_BM + 48] = cols(v["b_mod_2"][l])
        q[:, V2_N1:V2_N1 + 8] = cols(v["norm1_g_2"][l])
        q[:, V2_PS:V2_PS + 2] = cols(v["pool_scale_2"][l])
        q[:, V2_LF:V2_LF + 6] = v["ret_decay_fwd_2"][l][None, :]
        q[:, V2_LB:V2_LB + 6] = v["ret_decay_bwd_2"][l][None, :]
        q[:, V2_GN:V2_GN + 3] = cols(v["ret_gn_g_2"][l])
        q[:, V2_N2:V2_N2 + 8] = cols(v["norm2_g_2"][l])
        q[:, V2_CW:V2_CW + 132] = taps(v["conv_w_2"][l])
        q[:, V2_CB:V2_CB + 44] = cols(v["conv_b_2"][l])[:, paired()]
        vec.append(q)
        m = np.zeros((P, 2, P), np.float32)
        for g in range(4):
            rows = slice(64 * (g % 2), 64 * (g % 2) + 64)
            m[rows, g // 2, rows] = v["pool_w_2"][l][g]
        pw.append(m)
        for h in range(NA_H):
            table = v["na_rpb_2"][l][h]
            per_k = []
            for k in range(4):
                dr = np.arange(8)[None, :] - r[:, None] + 7
                dc = np.clip(COL0[k] + np.arange(SPAN)[None, :] - 16 * k - c[:, None] + 15, 0, 30)
                per_k.append(table[dr[:, :, None], dc[:, None, :]].reshape(P, PAIR))
            bias.append(np.concatenate(per_k, axis=1))
    out.update(w_in2=np.concatenate(w_in), w_out2=np.concatenate(w_out), w_up2=np.concatenate(w_up),
               w_down2=np.concatenate(w_down), w_mod=np.concatenate(w_mod), vec2=np.stack(vec),
               pool_w=np.stack(pw), na_bias=np.stack(bias), final=cols(v["final_g_2"]))
    return {k: np.ascontiguousarray(x, dtype=np.float32) for k, x in out.items()}


def paired():
    return np.stack([np.arange(FF // P), np.arange(FF // P) + FF // P], axis=1).reshape(-1)


def up_tiles(w, tiles):
    return tiles(w)[paired()]


def down_tiles(w):
    return w.reshape(2, HALF, P, DC, P).transpose(0, 3, 2, 1, 4).reshape(2 * DC, P, HALF * P)


def taps(w):
    return w.reshape(3, 2 * FF // P, P)[:, paired(), :].transpose(2, 1, 0).reshape(P, -1)


def kernel(**inputs):
    import concourse.bacc as bacc
    from concourse.bass_utils import run_bass_kernel_spmd as run

    v = {k: np.asarray(x) for k, x in inputs.items()}
    arrays = lay_out(v)
    nc = bacc.Bacc("TRN2", target_bir_lowering=False, num_devices=1)
    handles = {k: nc.dram_tensor("in_" + k, x.shape, F32, kind="ExternalInput").ap() for k, x in arrays.items()}
    out = nc.dram_tensor("out_rows", (P, DC, SEQ), F32, kind="ExternalOutput").ap()
    build(nc, handles, out)
    r = run(nc, [{"in_" + k: x for k, x in arrays.items()}], core_ids=[0])
    got = np.asarray(r.results[0]["out_rows"])
    return np.ascontiguousarray(got.transpose(2, 1, 0).reshape(1, SEQ, D))
```
